# Optimizing a Trainium2 kernel written in Bass

```python
import jax, jax.numpy as jnp
from jax import lax
import numpy as np

D_MODEL = 1024
BATCH = 1
SEQ = 256
DEPTH = 1

SSD_EXPAND = 2
SSD_D_INNER = SSD_EXPAND * D_MODEL
SSD_HEAD_DIM = 64
SSD_N_HEADS = SSD_D_INNER // SSD_HEAD_DIM
SSD_N_GROUPS = 4
SSD_HEADS_PER_GROUP = SSD_N_HEADS // SSD_N_GROUPS
SSD_D_STATE = 128
SSD_CONV_WIDTH = 4
SSD_CHUNK = 128
SSD_CONV_DIM = SSD_D_INNER + 2 * SSD_N_GROUPS * SSD_D_STATE
DT_MIN = 1e-3
DT_MAX = 1e-1

SC_WIDTH = D_MODEL
SC_CONV_WIDTH = 3

N_BRANCHES = 2

D_FF = 2816
FFN_CONV_WIDTH = 3

EPS = 1e-6

IN_SPLIT_SIZES = (SSD_D_INNER, SSD_CONV_DIM, SSD_N_HEADS,
                  SC_WIDTH, SC_WIDTH, SC_WIDTH, N_BRANCHES * D_MODEL)
D_IN_PROJ = sum(IN_SPLIT_SIZES)


def rmsnorm(x, g):
    xf = x.astype(jnp.float32)
    xf = xf * lax.rsqrt(jnp.mean(xf * xf, axis=-1, keepdims=True) + EPS)
    return xf.astype(x.dtype) * g

def grouped_rmsnorm(y, g, n_groups):
    shp = y.shape
    yf = y.astype(jnp.float32).reshape(*shp[:-1], n_groups, shp[-1] // n_groups)
    yf = yf * lax.rsqrt(jnp.mean(yf * yf, axis=-1, keepdims=True) + EPS)
    return yf.reshape(shp) * g

def causal_dwconv(u, w, b=None):
    k_width = w.shape[0]
    seqlen = u.shape[1]
    up = jnp.pad(u, ((0, 0), (k_width - 1, 0), (0, 0)))
    y = up[:, 0:seqlen] * w[0]
    for k in range(1, k_width):
        y = y + up[:, k:k + seqlen] * w[k]
    if b is not None:
        y = y + b
    return y

def ssd_chunked(xh, dt, a, bmat, cmat):
    bsz, seqlen = xh.shape[0], xh.shape[1]
    nc = seqlen // SSD_CHUNK
    L, G, R, P, N = SSD_CHUNK, SSD_N_GROUPS, SSD_HEADS_PER_GROUP, SSD_HEAD_DIM, SSD_D_STATE
    x = (xh * dt[..., None]).reshape(bsz, nc, L, G, R, P)
    adt = jnp.moveaxis((dt * a).reshape(bsz, nc, L, G, R), 2, -1)
    a_cs = jnp.cumsum(adt, axis=-1)
    bc = bmat.reshape(bsz, nc, L, G, N)
    cc = cmat.reshape(bsz, nc, L, G, N)

    causal = jnp.tril(jnp.ones((L, L), dtype=bool))
    decay = jnp.exp(jnp.where(causal, a_cs[..., :, None] - a_cs[..., None, :], -jnp.inf))
    scores = jnp.einsum("bclgn,bcsgn->bcgls", cc, bc)
    m = scores[:, :, :, None] * decay
    y_diag = jnp.einsum("bcgrls,bcsgrp->bclgrp", m, x)

    decay_states = jnp.exp(a_cs[..., -1:] - a_cs)
    states = jnp.einsum("bclgn,bcgrl,bclgrp->bcgrpn", bc, decay_states, x)
    chunk_decay = jnp.exp(a_cs[..., -1])

    def step(h, inp):
        s_c, d_c = inp
        h_new = h * d_c[..., None, None] + s_c
        return h_new, h

    h0 = jnp.zeros((bsz, G, R, P, N), dtype=states.dtype)
    _, prev = lax.scan(step, h0, (jnp.moveaxis(states, 1, 0), jnp.moveaxis(chunk_decay, 1, 0)))
    prev = jnp.moveaxis(prev, 0, 1)

    y_off = jnp.einsum("bclgn,bcgrpn,bcgrl->bclgrp", cc, prev, jnp.exp(a_cs))
    return (y_diag + y_off).reshape(bsz, seqlen, SSD_N_HEADS, P)

def ssd_branch(z, xbc, dt_raw, conv_w, conv_b, dt_bias, a_log, d_skip, norm_g):
    bsz, seqlen = z.shape[0], z.shape[1]
    xbc = jax.nn.silu(causal_dwconv(xbc, conv_w, conv_b))
    gn = SSD_N_GROUPS * SSD_D_STATE
    xs, bm, cm = jnp.split(xbc, [SSD_D_INNER, SSD_D_INNER + gn], axis=-1)
    xh = xs.reshape(bsz, seqlen, SSD_N_HEADS, SSD_HEAD_DIM)
    dt = jax.nn.softplus(dt_raw.astype(jnp.float32) + dt_bias.astype(jnp.float32))
    a = -jnp.exp(a_log.astype(jnp.float32))
    y = ssd_chunked(xh.astype(jnp.float32), dt, a,
                    bm.reshape(bsz, seqlen, SSD_N_GROUPS, SSD_D_STATE).astype(jnp.float32),
                    cm.reshape(bsz, seqlen, SSD_N_GROUPS, SSD_D_STATE).astype(jnp.float32))
    y = y + d_skip.astype(jnp.float32)[:, None] * xh.astype(jnp.float32)
    y = y.reshape(bsz, seqlen, SSD_D_INNER) * jax.nn.silu(z.astype(jnp.float32))
    return grouped_rmsnorm(y, norm_g, SSD_N_GROUPS).astype(z.dtype)

def short_conv_branch(b_gate, c_gate, h, conv_w):
    return b_gate * causal_dwconv(c_gate * h, conv_w)

def hybrid_layer(x, c_act, ada_w, ada_b, mix_pre_g, mix_post_g, w_in,
                 ssd_conv_w, ssd_conv_b, ssd_dt_bias, ssd_a_log, ssd_d, ssd_norm_g,
                 w_ssd_out, sc_conv_w, w_sc_out, w_o,
                 ffn_pre_g, ffn_post_g, w_up, ffn_conv_w, ffn_conv_b, w_down):
    mod = c_act @ ada_w + ada_b
    sh1, sc1, gt1, sh2, sc2, gt2 = [m[:, None, :] for m in jnp.split(mod, 6, axis=-1)]

    h = rmsnorm(x, mix_pre_g) * (1.0 + sc1) + sh1
    proj = h @ w_in
    points, acc = [], 0
    for s in IN_SPLIT_SIZES[:-1]:
        acc += s
        points.append(acc)
    z, xbc, dt_raw, sc_b, sc_c, sc_h, gates = jnp.split(proj, points, axis=-1)
    y_ssd = ssd_branch(z, xbc, dt_raw, ssd_conv_w, ssd_conv_b, ssd_dt_bias,
                       ssd_a_log, ssd_d, ssd_norm_g) @ w_ssd_out
    y_sc = short_conv_branch(sc_b, sc_c, sc_h, sc_conv_w) @ w_sc_out
    g_ssd, g_sc = jnp.split(jax.nn.sigmoid(gates), 2, axis=-1)
    mix = (g_ssd * y_ssd + g_sc * y_sc) @ w_o
    x = x + gt1 * rmsnorm(mix, mix_post_g)

    h = rmsnorm(x, ffn_pre_g) * (1.0 + sc2) + sh2
    u = causal_dwconv(h @ w_up, ffn_conv_w, ffn_conv_b)
    u_gate, u_val = jnp.split(u, 2, axis=-1)
    f = (jax.nn.silu(u_gate) * u_val) @ w_down
    x = x + gt2 * rmsnorm(f, ffn_post_g)
    return x

def first_inputs(seed: int = 0) -> dict:
    key = jax.random.key(seed)
    ks = jax.random.split(key, 32)
    f32 = jnp.float32

    def dense(k, fan_in, fan_out, scale=1.0):
        return jax.random.normal(k, (DEPTH, fan_in, fan_out), f32) * (scale * fan_in ** -0.5)

    def gain(k, n):
        return 1.0 + 0.05 * jax.random.normal(k, (DEPTH, n), f32)

    def small(k, shape, s=0.02):
        return s * jax.random.normal(k, shape, f32)

    u = jax.random.uniform(ks[8], (DEPTH, SSD_N_HEADS), f32)
    dt0 = jnp.exp(u * (np.log(DT_MAX) - np.log(DT_MIN)) + np.log(DT_MIN))
    dt_bias = dt0 + jnp.log(-jnp.expm1(-dt0))
    a_log = jnp.log(jax.random.uniform(ks[9], (DEPTH, SSD_N_HEADS), f32, 1.0, 16.0))

    return {
        "x": jax.random.normal(ks[0], (BATCH, SEQ, D_MODEL), f32),
        "c": jax.random.normal(ks[1], (BATCH, D_MODEL), f32),
        "ada_w": dense(ks[2], D_MODEL, 6 * D_MODEL, 0.5),
        "ada_b": small(ks[3], (DEPTH, 6 * D_MODEL)),
        "mix_pre_g": gain(ks[4], D_MODEL),
        "mix_post_g": gain(ks[5], D_MODEL),
        "w_in": dense(ks[6], D_MODEL, D_IN_PROJ),
        "ssd_conv_w": jax.random.normal(ks[7], (DEPTH, SSD_CONV_WIDTH, SSD_CONV_DIM), f32) * SSD_CONV_WIDTH ** -0.5,
        "ssd_conv_b": small(ks[10], (DEPTH, SSD_CONV_DIM)),
        "ssd_dt_bias": dt_bias,
        "ssd_a_log": a_log,
        "ssd_d": 1.0 + 0.1 * jax.random.normal(ks[11], (DEPTH, SSD_N_HEADS), f32),
        "ssd_norm_g": gain(ks[12], SSD_D_INNER),
        "w_ssd_out": dense(ks[13], SSD_D_INNER, D_MODEL),
        "sc_conv_w": jax.random.normal(ks[14], (DEPTH, SC_CONV_WIDTH, SC_WIDTH), f32) * SC_CONV_WIDTH ** -0.5,
        "w_sc_out": dense(ks[15], SC_WIDTH, D_MODEL),
        "w_o": dense(ks[16], D_MODEL, D_MODEL),
        "ffn_pre_g": gain(ks[17], D_MODEL),
        "ffn_post_g": gain(ks[18], D_MODEL),
        "w_up": dense(ks[19], D_MODEL, 2 * D_FF),
        "ffn_conv_w": jax.random.normal(ks[20], (DEPTH, FFN_CONV_WIDTH, 2 * D_FF), f32) * FFN_CONV_WIDTH ** -0.5,
        "ffn_conv_b": small(ks[21], (DEPTH, 2 * D_FF)),
        "w_down": dense(ks[22], D_FF, D_MODEL),
    }

def first_block(x, c, ada_w, ada_b, mix_pre_g, mix_post_g, w_in,
              ssd_conv_w, ssd_conv_b, ssd_dt_bias, ssd_a_log, ssd_d, ssd_norm_g,
              w_ssd_out, sc_conv_w, w_sc_out, w_o,
              ffn_pre_g, ffn_post_g, w_up, ffn_conv_w, ffn_conv_b, w_down):
    c_act = jax.nn.silu(c)
    for i in range(DEPTH):
        x = hybrid_layer(x, c_act, ada_w[i], ada_b[i], mix_pre_g[i], mix_post_g[i], w_in[i],
                         ssd_conv_w[i], ssd_conv_b[i], ssd_dt_bias[i], ssd_a_log[i], ssd_d[i],
                         ssd_norm_g[i], w_ssd_out[i], sc_conv_w[i], w_sc_out[i], w_o[i],
                         ffn_pre_g[i], ffn_post_g[i], w_up[i], ffn_conv_w[i], ffn_conv_b[i],
                         w_down[i])
    return x


NSA_HEADS = 8
NSA_KV_HEADS = 2
NSA_GROUP = NSA_HEADS // NSA_KV_HEADS
NSA_HEAD_DIM = 128
CMP_BLOCK = 32
CMP_STRIDE = 16
CMP_HIDDEN = 256
SEL_BLOCK = 64
SEL_TOPK = 16
WINDOW = 512
NSA_Q_BLOCK = 64
MLA_HEADS = 8
MLA_Q_RANK = 384
MLA_KV_RANK = 256
MLA_NOPE_DIM = 128
MLA_ROPE_DIM = 64
MLA_QK_DIM = MLA_NOPE_DIM + MLA_ROPE_DIM
MLA_V_DIM = 128
MLA_Q_BLOCK = 128
CONV_WIDTH = 3
ROPE_THETA = 10000.0
NORM_EPS = 1e-6
NEG_INF = -1e30
SEL_FORCE = 1e9

W_NSA_Q = NSA_HEADS * NSA_HEAD_DIM
W_NSA_KV = NSA_KV_HEADS * NSA_HEAD_DIM
IN_SPLITS = (W_NSA_Q,
             W_NSA_KV, W_NSA_KV,
             W_NSA_KV, W_NSA_KV,
             W_NSA_KV, W_NSA_KV,
             3 * NSA_HEADS,
             MLA_Q_RANK, MLA_KV_RANK,
             MLA_ROPE_DIM,
             2 * D_MODEL)
IN_WIDTH = sum(IN_SPLITS)
IN_OFFSETS = tuple(int(v) for v in np.cumsum(IN_SPLITS)[:-1])


def rms_norm(x, gain):
    xf = x.astype(jnp.float32)
    y = xf * lax.rsqrt(jnp.mean(xf * xf, axis=-1, keepdims=True) + NORM_EPS)
    return (y * gain.astype(jnp.float32)).astype(x.dtype)

def rope(x, pos):
    dim = x.shape[-1]
    half = dim // 2
    inv = ROPE_THETA ** (-jnp.arange(half, dtype=jnp.float32) * 2.0 / dim)
    ang = pos[:, None] * inv[None, :]
    cos = jnp.cos(ang)[None, :, None, :]
    sin = jnp.sin(ang)[None, :, None, :]
    xf = x.astype(jnp.float32)
    x1, x2 = xf[..., :half], xf[..., half:]
    return jnp.concatenate([x1 * cos - x2 * sin, x1 * sin + x2 * cos], axis=-1).astype(x.dtype)

def masked_softmax(s, mask):
    p = jax.nn.softmax(jnp.where(mask, s.astype(jnp.float32), NEG_INF), axis=-1)
    return jnp.where(mask, p, 0.0)

def compress(x, pe, w1, w2):
    B, S, G, hd = x.shape
    n_chunks = S // CMP_STRIDE
    r = CMP_BLOCK // CMP_STRIDE
    n_cmp = n_chunks - r + 1
    chunks = x.reshape(B, n_chunks, CMP_STRIDE, G, hd)
    blocks = jnp.concatenate([chunks[:, j:j + n_cmp] for j in range(r)], axis=2)
    blocks = blocks + pe[None, None, :, None, :].astype(x.dtype)
    flat = blocks.transpose(0, 1, 3, 2, 4).reshape(B, n_cmp, G, CMP_BLOCK * hd)
    return jax.nn.silu(flat @ w1) @ w2

def nsa_mixer(q, kc, vc, ks, vs, kw, vw, gates):
    B, S, H, hd = q.shape
    G, R, Cq = NSA_KV_HEADS, NSA_GROUP, NSA_Q_BLOCK
    scale = hd ** -0.5
    n_cmp = kc.shape[1]
    n_sel = S // SEL_BLOCK
    k_top = min(SEL_TOPK, n_sel)
    cmp_start = jnp.arange(n_cmp) * CMP_STRIDE
    cmp_end = cmp_start + CMP_BLOCK - 1
    sel_idx = jnp.arange(n_sel)
    sel_start = sel_idx * SEL_BLOCK
    overlap = ((cmp_start[:, None] <= (sel_start + SEL_BLOCK - 1)[None, :])
               & (cmp_end[:, None] >= sel_start[None, :])).astype(jnp.float32)
    ks_blk = ks.reshape(B, n_sel, SEL_BLOCK, G, hd).transpose(0, 3, 1, 2, 4)
    vs_blk = vs.reshape(B, n_sel, SEL_BLOCK, G, hd).transpose(0, 3, 1, 2, 4)
    kw_pad = jnp.pad(kw, ((0, 0), (WINDOW, 0), (0, 0), (0, 0)))
    vw_pad = jnp.pad(vw, ((0, 0), (WINDOW, 0), (0, 0), (0, 0)))
    b_ix = jnp.arange(B)[:, None, None, None]
    g_ix = jnp.arange(G)[None, :, None, None]

    def block(n):
        q0 = n * Cq
        t = q0 + jnp.arange(Cq)
        qb = lax.dynamic_slice_in_dim(q, q0, Cq, axis=1).reshape(B, Cq, G, R, hd)
        gb = lax.dynamic_slice_in_dim(gates, q0, Cq, axis=1).reshape(B, Cq, G, R, 3)
        s = jnp.einsum('bqgrd,bngd->bgrqn', qb, kc) * scale
        p_cmp = masked_softmax(s, cmp_end[None, :] <= t[:, None])
        o_cmp = jnp.einsum('bgrqn,bngd->bqgrd', p_cmp.astype(vc.dtype), vc)
        imp = jnp.einsum('bgqn,nj->bgqj', p_cmp.sum(axis=2), overlap)
        cur = t // SEL_BLOCK
        forced = ((sel_idx[None, :] == 0) | (sel_idx[None, :] == cur[:, None])
                  | (sel_idx[None, :] == cur[:, None] - 1))
        allowed = sel_start[None, :] <= t[:, None]
        score = jnp.where(forced, SEL_FORCE, jnp.where(allowed, imp, NEG_INF))
        _, idx = lax.top_k(score, k_top)
        k_sel = ks_blk[b_ix, g_ix, idx]
        v_sel = vs_blk[b_ix, g_ix, idx]
        kpos = idx[..., None] * SEL_BLOCK + jnp.arange(SEL_BLOCK)
        sel_mask = (kpos <= t[None, None, :, None, None]).reshape(B, G, 1, Cq, k_top * SEL_BLOCK)
        s = jnp.einsum('bqgrd,bgqkld->bgrqkl', qb, k_sel) * scale
        p = masked_softmax(s.reshape(B, G, R, Cq, k_top * SEL_BLOCK), sel_mask)
        p = p.reshape(B, G, R, Cq, k_top, SEL_BLOCK)
        o_slc = jnp.einsum('bgrqkl,bgqkld->bqgrd', p.astype(vs.dtype), v_sel)
        k_w = lax.dynamic_slice_in_dim(kw_pad, q0, Cq + WINDOW, axis=1)
        v_w = lax.dynamic_slice_in_dim(vw_pad, q0, Cq + WINDOW, axis=1)
        wpos = q0 - WINDOW + jnp.arange(Cq + WINDOW)
        win_mask = ((wpos[None, :] <= t[:, None]) & (wpos[None, :] > t[:, None] - WINDOW)
                    & (wpos[None, :] >= 0))
        s = jnp.einsum('bqgrd,bkgd->bgrqk', qb, k_w) * scale
        p = masked_softmax(s, win_mask)
        o_win = jnp.einsum('bgrqk,bkgd->bqgrd', p.astype(vw.dtype), v_w)
        o = gb[..., 0:1] * o_cmp + gb[..., 1:2] * o_slc + gb[..., 2:3] * o_win
        return o.reshape(B, Cq, H * hd)

    out = lax.map(block, jnp.arange(S // Cq))
    return out.transpose(1, 0, 2, 3).reshape(B, S, H * hd)

def mla_mixer(q, k, v):
    B, S, H, _ = q.shape
    scale = MLA_QK_DIM ** -0.5
    kpos = jnp.arange(S)

    def block(n):
        q0 = n * MLA_Q_BLOCK
        t = q0 + jnp.arange(MLA_Q_BLOCK)
        qb = lax.dynamic_slice_in_dim(q, q0, MLA_Q_BLOCK, axis=1)
        s = jnp.einsum('bqhd,bkhd->bhqk', qb, k) * scale
        p = masked_softmax(s, kpos[None, :] <= t[:, None])
        o = jnp.einsum('bhqk,bkhd->bqhd', p.astype(v.dtype), v)
        return o.reshape(B, MLA_Q_BLOCK, H * MLA_V_DIM)

    out = lax.map(block, jnp.arange(S // MLA_Q_BLOCK))
    return out.transpose(1, 0, 2, 3).reshape(B, S, H * MLA_V_DIM)

def hybrid_layer_2(x, c, pos, w_ada, b_ada, attn_norm, ffn_norm, w_in,
                 nsa_q_norm, nsa_kc_norm, nsa_ks_norm, nsa_kw_norm,
                 cmp_k_pe, cmp_k_w1, cmp_k_w2, cmp_v_pe, cmp_v_w1, cmp_v_w2,
                 mla_cq_norm, mla_ckv_norm, w_uq, w_ukv, mla_q_norm, mla_k_norm,
                 w_o, w_up, w_conv, b_conv, w_down):
    B, S, D = x.shape
    G = NSA_KV_HEADS
    mod = (jax.nn.silu(c) @ w_ada + b_ada)[:, None, :]
    shift_a, scale_a, gate_a, shift_f, scale_f, gate_f = jnp.split(mod, 6, axis=-1)

    h = rms_norm(x, attn_norm) * (1.0 + scale_a) + shift_a
    (nq, nkc, nvc, nks, nvs, nkw, nvw, ngate,
     cq, ckv, kr, bgate) = jnp.split(h @ w_in, IN_OFFSETS, axis=-1)

    def heads(t, n):
        return t.reshape(B, S, n, -1)

    q_a = rope(rms_norm(heads(nq, NSA_HEADS), nsa_q_norm), pos)
    kc = rms_norm(compress(rope(heads(nkc, G), pos), cmp_k_pe, cmp_k_w1, cmp_k_w2), nsa_kc_norm)
    vc = compress(heads(nvc, G), cmp_v_pe, cmp_v_w1, cmp_v_w2)
    ks = rope(rms_norm(heads(nks, G), nsa_ks_norm), pos)
    kw = rope(rms_norm(heads(nkw, G), nsa_kw_norm), pos)
    g_nsa = jax.nn.sigmoid(heads(ngate, NSA_HEADS))
    o_a = nsa_mixer(q_a, kc, vc, ks, heads(nvs, G), kw, heads(nvw, G), g_nsa)

    q_b = (rms_norm(cq, mla_cq_norm) @ w_uq).reshape(B, S, MLA_HEADS, MLA_QK_DIM)
    kv_b = (rms_norm(ckv, mla_ckv_norm) @ w_ukv).reshape(B, S, MLA_HEADS, MLA_NOPE_DIM + MLA_V_DIM)
    k_nope, v_b = jnp.split(kv_b, [MLA_NOPE_DIM], axis=-1)
    k_b = jnp.concatenate(
        [k_nope, jnp.broadcast_to(kr[:, :, None, :], (B, S, MLA_HEADS, MLA_ROPE_DIM))], axis=-1)
    q_b = rms_norm(q_b, mla_q_norm)
    k_b = rms_norm(k_b, mla_k_norm)
    q_b = jnp.concatenate([q_b[..., :MLA_NOPE_DIM], rope(q_b[..., MLA_NOPE_DIM:], pos)], axis=-1)
    k_b = jnp.concatenate([k_b[..., :MLA_NOPE_DIM], rope(k_b[..., MLA_NOPE_DIM:], pos)], axis=-1)
    o_b = mla_mixer(q_b, k_b, v_b)

    g_a, g_b = jnp.split(jax.nn.sigmoid(bgate), 2, axis=-1)
    x = x + gate_a * ((g_a * o_a + g_b * o_b) @ w_o)

    h = rms_norm(x, ffn_norm) * (1.0 + scale_f) + shift_f
    u = lax.conv_general_dilated(
        h @ w_up, w_conv[:, None, :], window_strides=(1,), padding=[(CONV_WIDTH - 1, 0)],
        dimension_numbers=('NWC', 'WIO', 'NWC'), feature_group_count=2 * D_FF) + b_conv
    val, gt = jnp.split(u, 2, axis=-1)
    x = x + gate_f * ((jax.nn.silu(gt) * val) @ w_down)
    return x

def second_inputs(seed: int = 0) -> dict:
    key = jax.random.key(seed)
    k = jax.random.split(key, 32)
    L, hd = DEPTH, NSA_HEAD_DIM

    def nrm(kk, shape, scale):
        return jax.random.normal(kk, shape, jnp.float32) * scale

    def gain(kk, n):
        return 1.0 + nrm(kk, (L, n), 0.02)

    return {
        'x': nrm(k[0], (BATCH, SEQ, D_MODEL), 1.0),
        'c': nrm(k[1], (BATCH, D_MODEL), 1.0),
        'w_ada': nrm(k[2], (L, D_MODEL, 6 * D_MODEL), D_MODEL ** -0.5),
        'b_ada': nrm(k[3], (L, 6 * D_MODEL), 0.01),
        'attn_norm': gain(k[4], D_MODEL),
        'ffn_norm': gain(k[5], D_MODEL),
        'w_in': nrm(k[6], (L, D_MODEL, IN_WIDTH), D_MODEL ** -0.5),
        'nsa_q_norm': gain(k[7], hd),
        'nsa_kc_norm': gain(k[8], hd),
        'nsa_ks_norm': gain(k[9], hd),
        'nsa_kw_norm': gain(k[10], hd),
        'cmp_k_pe': nrm(k[11], (L, CMP_BLOCK, hd), 0.5),
        'cmp_k_w1': nrm(k[12], (L, CMP_BLOCK * hd, CMP_HIDDEN), (CMP_BLOCK * hd) ** -0.5),
        'cmp_k_w2': nrm(k[13], (L, CMP_HIDDEN, hd), CMP_HIDDEN ** -0.5),
        'cmp_v_pe': nrm(k[14], (L, CMP_BLOCK, hd), 0.5),
        'cmp_v_w1': nrm(k[15], (L, CMP_BLOCK * hd, CMP_HIDDEN), (CMP_BLOCK * hd) ** -0.5),
        'cmp_v_w2': nrm(k[16], (L, CMP_HIDDEN, hd), CMP_HIDDEN ** -0.5),
        'mla_cq_norm': gain(k[17], MLA_Q_RANK),
        'mla_ckv_norm': gain(k[18], MLA_KV_RANK),
        'w_uq': nrm(k[19], (L, MLA_Q_RANK, MLA_HEADS * MLA_QK_DIM), MLA_Q_RANK ** -0.5),
        'w_ukv': nrm(k[20], (L, MLA_KV_RANK, MLA_HEADS * (MLA_NOPE_DIM + MLA_V_DIM)), MLA_KV_RANK ** -0.5),
        'mla_q_norm': gain(k[21], MLA_QK_DIM),
        'mla_k_norm': gain(k[22], MLA_QK_DIM),
        'w_o': nrm(k[23], (L, D_MODEL, D_MODEL), D_MODEL ** -0.5),
        'w_up': nrm(k[24], (L, D_MODEL, 2 * D_FF), D_MODEL ** -0.5),
        'w_conv': nrm(k[25], (L, CONV_WIDTH, 2 * D_FF), CONV_WIDTH ** -0.5),
        'b_conv': nrm(k[26], (L, 2 * D_FF), 0.01),
        'w_down': nrm(k[27], (L, D_FF, D_MODEL), D_FF ** -0.5),
    }

def second_block(x, c, w_ada, b_ada, attn_norm, ffn_norm, w_in,
              nsa_q_norm, nsa_kc_norm, nsa_ks_norm, nsa_kw_norm,
              cmp_k_pe, cmp_k_w1, cmp_k_w2, cmp_v_pe, cmp_v_w1, cmp_v_w2,
              mla_cq_norm, mla_ckv_norm, w_uq, w_ukv, mla_q_norm, mla_k_norm,
              w_o, w_up, w_conv, b_conv, w_down):
    pos = jnp.arange(x.shape[1], dtype=jnp.float32)
    for l in range(DEPTH):
        x = hybrid_layer_2(x, c, pos, w_ada[l], b_ada[l], attn_norm[l], ffn_norm[l], w_in[l],
                         nsa_q_norm[l], nsa_kc_norm[l], nsa_ks_norm[l], nsa_kw_norm[l],
                         cmp_k_pe[l], cmp_k_w1[l], cmp_k_w2[l], cmp_v_pe[l], cmp_v_w1[l], cmp_v_w2[l],
                         mla_cq_norm[l], mla_ckv_norm[l], w_uq[l], w_ukv[l], mla_q_norm[l], mla_k_norm[l],
                         w_o[l], w_up[l], w_conv[l], b_conv[l], w_down[l])
    return x


def setup_inputs(seed=0):
    out = dict(first_inputs(seed))
    for name, value in second_inputs(seed + 1).items():
        if name != "x":
            out[name + "_2"] = value
    return out


def reference(
    x, c, ada_w, ada_b, mix_pre_g, mix_post_g, w_in, ssd_conv_w, ssd_conv_b, ssd_dt_bias,
    ssd_a_log, ssd_d, ssd_norm_g, w_ssd_out, sc_conv_w, w_sc_out, w_o, ffn_pre_g, ffn_post_g,
    w_up, ffn_conv_w, ffn_conv_b, w_down, c_2, w_ada_2, b_ada_2, attn_norm_2, ffn_norm_2,
    w_in_2, nsa_q_norm_2, nsa_kc_norm_2, nsa_ks_norm_2, nsa_kw_norm_2, cmp_k_pe_2, cmp_k_w1_2,
    cmp_k_w2_2, cmp_v_pe_2, cmp_v_w1_2, cmp_v_w2_2, mla_cq_norm_2, mla_ckv_norm_2, w_uq_2,
    w_ukv_2, mla_q_norm_2, mla_k_norm_2, w_o_2, w_up_2, w_conv_2, b_conv_2, w_down_2,
):
    x = first_block(
        x, c, ada_w, ada_b, mix_pre_g, mix_post_g, w_in, ssd_conv_w, ssd_conv_b, ssd_dt_bias,
        ssd_a_log, ssd_d, ssd_norm_g, w_ssd_out, sc_conv_w, w_sc_out, w_o, ffn_pre_g,
        ffn_post_g, w_up, ffn_conv_w, ffn_conv_b, w_down,
    )
    return second_block(
        x, c_2, w_ada_2, b_ada_2, attn_norm_2, ffn_norm_2, w_in_2, nsa_q_norm_2, nsa_kc_norm_2,
        nsa_ks_norm_2, nsa_kw_norm_2, cmp_k_pe_2, cmp_k_w1_2, cmp_k_w2_2, cmp_v_pe_2,
        cmp_v_w1_2, cmp_v_w2_2, mla_cq_norm_2, mla_ckv_norm_2, w_uq_2, w_ukv_2, mla_q_norm_2,
        mla_k_norm_2, w_o_2, w_up_2, w_conv_2, b_conv_2, w_down_2,
    )


_drawn_inputs = setup_inputs


def setup_inputs(seed=0):
    import zlib

    import numpy as np

    out = dict(_drawn_inputs(seed))
    spreads = {}
    factors = {'mix_post_g': 3.142,
     'ssd_conv_b': 8.0,
     'ssd_d': 4.067,
     'ssd_norm_g': 5.751,
     'ffn_pre_g': 2.766,
     'ffn_post_g': 3.667,
     'ffn_conv_b': 6.587,
     'b_ada_2': 3.939,
     'attn_norm_2': 8.0,
     'ffn_norm_2': 4.12,
     'nsa_q_norm_2': 8.0,
     'nsa_kc_norm_2': 8.0,
     'nsa_ks_norm_2': 8.0,
     'nsa_kw_norm_2': 8.0,
     'cmp_k_pe_2': 5.66,
     'mla_cq_norm_2': 8.0,
     'mla_ckv_norm_2': 8.0,
     'mla_q_norm_2': 8.0,
     'mla_k_norm_2': 8.0,
     'b_conv_2': 22.541}
    for name, (base, spread) in spreads.items():
        noise = np.random.default_rng([zlib.crc32(name.encode()), seed]).standard_normal(out[name].shape)
        drawn = base * np.exp(spread * noise) if base else spread * noise
        out[name] = __import__('jax').numpy.asarray(drawn.astype(out[name].dtype))
    for name, factor in factors.items():
        out[name] = (out[name] * factor).astype(out[name].dtype)
    return out
```

```python
from contextlib import ExitStack, contextmanager

import concourse.bass as bass
import numpy as np
from concourse import mybir

P = 128
T = 256
D = 1024
KD = D // P
FF = 2816
KF = FF // P
EPS = 1e-6

NXBC = 24
NZ = 16
HEADS1 = 32
NGRP = 4
NH = 8
NCMP = 15
HD = 128
QK = 192
ROPE = 64

SLOTS = 4
SLOT = 16 * P
ADA_SLOTS = 4
ADA_COLS = 1024
ADA_GROUPS = 6 * D // ADA_COLS


class Stream:

    def __init__(self):
        self.cols, self.done_after, self.units, self.at = [], [], 0, {}

    def add(self, name, chunks, cols, units_per_chunk):
        self.at[name] = (len(self.cols), self.units)
        for c in range(chunks):
            self.cols.append(cols)
            self.done_after.append(self.units + int(np.ceil((c + 1) * units_per_chunk)))
        self.units += int(round(chunks * units_per_chunk))

    def bare(self, name, units):
        self.at[name] = (len(self.cols), self.units)
        self.units += units


PLAN = Stream()
PLAN.add("in1", 40, SLOT, 2)
PLAN.add("ssd_out", 8, SLOT, 1)
PLAN.add("sc_out", 4, SLOT, 2)
PLAN.add("o1", 4, SLOT, 2)
PLAN.add("up1", 22, SLOT, 2)
PLAN.add("down1", 16, 11 * P, 0.5)
PLAN.add("tok2", 9, SLOT, 2)
PLAN.add("mix2", 1, 88 * KD + SLOT // 2, 3)
PLAN.add("feat2", 11, SLOT, 2)
PLAN.add("uq", 3, 3 * 512, 2)
PLAN.add("ukv", 2, SLOT, 4)
PLAN.add("cmp", 8, SLOT, 0.5)
PLAN.bare("cmp_scores", 1)
PLAN.bare("nsa_scores", 2 * NH)
PLAN.bare("mla_scores", NH)
PLAN.add("o2", 4, SLOT, 2)
PLAN.add("up2", 22, SLOT, 2)
PLAN.add("down2", 16, 11 * P, 0.5)
CHUNKS = len(PLAN.cols)

SCRATCH = {}
_n = 0
for _name, _count in [("stat_mix", 1), ("mod_a", 1), ("dt", 1), ("mod_b", 1), ("dt_turn", 1), ("x_turn", 8),
                      ("scores", 4), ("gnorm", 4), ("stat_o1", 1), ("stat_ffn1", 1), ("stat_down1", 1),
                      ("mod_2", 1), ("stat_attn", 1), ("stat_cq", 1), ("stat_ckv", 1), ("nsa_turn", 7),
                      ("kc", 1), ("kc_turn", 1), ("vc", 1), ("cmp_turn", 4), ("nsa_p", 16),
                      ("mla_turn", 16), ("mla_p", 8), ("stat_ffn2", 1)]:
    SCRATCH[_name] = _n
    _n += _count

OUT_Y, OUT_NSA, OUT_MLA = 0, 16, 24

PAR_SPEC = [
    ("c", 8), ("c_2", 8), ("ada_b", 48), ("mix_pre_g", 8), ("mix_post_g", 8),
    ("xconv_w", 4 * NXBC), ("xconv_b", NXBC), ("dskip", 16), ("ssd_norm_g", 16), ("sconv_w", 24),
    ("ffn_pre_g", 8), ("ffn_post_g", 8), ("fconv_w", 132), ("fconv_b", 44),
    ("dt_bias", 1), ("a_log", 1), ("w_dt", KD * HEADS1),
    ("b_ada_2", 48), ("attn_norm_2", 8), ("ffn_norm_2", 8), ("fconv_w_2", 132), ("fconv_b_2", 44),
    ("k_pe", 32), ("v_pe", 32), ("k_w2", 256), ("v_w2", 256), ("cq_g", 3), ("ckv_g", 2),
    ("q_gain", 128), ("ks_gain", 128), ("kw_gain", 128), ("kc_gain", 128), ("mq_gain", QK), ("mk_gain", QK),
    ("ident", P), ("ones", P), ("causal_add", P), ("causal01", P),
    ("cos", 2 * 128), ("sin", 2 * 128), ("mcos", 2 * 64), ("msin", 2 * 64),
    ("cmask_add", 2 * NCMP), ("cmask01", 2 * NCMP),
]
PAR = {}
_n = 0
for _name, _count in PAR_SPEC:
    PAR[_name] = (_n, _count)
    _n += _count
NPAR = _n


def build(nc, x_t, par_in, ada_w, wts, out_t):
    F32, BF16 = mybir.dt.float32, mybir.dt.bfloat16
    ALU, ACT, AX = mybir.AluOpType, mybir.ActivationFunctionType, mybir.AxisListType
    MUL, ADD, SUB = ALU.mult, ALU.add, ALU.subtract
    ctx = ExitStack()
    with ctx:
        def sb(name, shape, dt=F32):
            return ctx.enter_context(nc.sbuf_tensor(name, shape, dt))

        def sem(name):
            return ctx.enter_context(nc.semaphore(name))

        ring = sb("ring", [P, SLOTS, SLOT])
        adaring = sb("adaring", [P, ADA_SLOTS, ADA_COLS])
        acc = sb("acc", [P, 6 * D])
        par = sb("par", [P, NPAR])
        X = sb("X", [P, KD, T])
        H = sb("H", [P, KD, T])
        SQ = sb("SQ", [P, 2048])
        R = sb("R", [P, 22528])
        CT = sb("CT", [P, 4, T])
        RS = sb("RS", [P, 2, T])
        mod = sb("mod", [P, 48])
        lead = sb("lead", [P, 32])
        csil = sb("csil", [P, 16])
        CD = sb("CD", [P, 4, 32])
        sm = sb("sm", [P, 96])
        GT = sb("GT", [P, 2, 24])
        eps_col = sb("eps_col", [P, 1])
        mlars = sb("mlars", [P, 32])
        cmx = sb("cmx", [P, 36])
        kct = sb("kct", [P, 30])
        identb = sb("identb", [P, P], BF16)
        maskb = sb("maskb", [P, P], BF16)
        psL = ctx.enter_context(nc.psum_tensor("psL", [P, 4, 512], F32))
        psS = ctx.enter_context(nc.psum_tensor("psS", [P, 2, 512], F32))
        psO = ctx.enter_context(nc.psum_tensor("psO", [P, 2, 512], F32))
        cum_dram = nc.dram_tensor("cum_dram", (HEADS1, T), F32, kind="Internal").ap()

        def pv(name, lo=0, n=None):
            at, cols = PAR[name]
            return par[:, at + lo:at + (cols if n is None else lo + n)]

        def region(buf, lo, **dims):
            a, b = dims["a"], dims["b"]
            return buf[:, lo:lo + a * b].rearrange("p (a b) -> p a b", b=b)

        Z = region(R, 0, a=NZ, b=T)
        XBC = region(R, 4096, a=NXBC, b=T)
        G1 = region(R, 10240, a=16, b=T)
        SCQ = region(R, 14336, a=8, b=T)
        YSC = region(R, 16384, a=8, b=T)
        XTOK = region(R, 18432, a=2, b=2048)
        dts = R[0:32, 18432:19968].rearrange("p (a b) -> p a b", b=T)
        MIXIN = region(R, 14336, a=8, b=T)
        MIX = region(R, 4096, a=8, b=T)
        CUMB = region(acc, 0, a=2, b=2048)
        SE = region(acc, 4096, a=2, b=384)
        SM = region(acc, 4864, a=2, b=384)
        SCM = region(SQ, 0, a=4, b=384)
        FA = region(R, 0, a=KF, b=T)
        FO = region(R, 8192, a=8, b=T)
        QTOK = region(R, 0, a=2, b=1024)
        KTOK = region(R, 2048, a=2, b=768)
        VTOK = region(R, 3584, a=2, b=512)
        KR = region(R, 4608, a=2, b=64)
        VC = region(R, 4864, a=2, b=T)
        CQ = region(R, 5376, a=3, b=T)
        CKV = region(R, 6144, a=2, b=T)
        G2 = region(R, 6656, a=16, b=T)
        QT = region(R, 10752, a=8, b=T)
        KT = region(R, 12800, a=6, b=T)
        QB = region(R, 14336, a=2, b=1536)
        KB = region(R, 17408, a=2, b=1536)
        VB = region(R, 20480, a=2, b=1024)
        OM = region(acc, 0, a=8, b=T)
        CB = [region(acc, 2048, a=32, b=30), region(acc, 3072, a=32, b=30)]
        PR = region(acc, 4096, a=2, b=384)
        PT = region(acc, 4864, a=2, b=384)
        HID = region(acc, 5632, a=4, b=30)
        VCMP = acc[0:NCMP, 5760:6016].rearrange("p (a b) -> p a b", b=P)
        KCT = kct[:, :]
        KCD = acc[0:30, 6016:6144]
        CS = RS[:, 0, 0:240]
        KCN = RS[0:30, 1, 0:P]
        PTC = H
        MQN = region(R, 0, a=8, b=T)
        MQR = region(R, 2048, a=8, b=T)
        MKR = region(R, 4096, a=8, b=T)
        MKN = region(R, 10752, a=8, b=T)

        par_in_sem, x_in = sem("par_in"), sem("x_in")
        w_arrived = [sem(f"w_arrived{i}") for i in range(SLOTS)]
        ada_arrived = [sem(f"ada_arrived{i}") for i in range(ADA_SLOTS)]
        ada_used = sem("ada_used")
        lin_done = sem("lin_done")
        lin_free = [sem(f"lin_free{i}") for i in range(4)]
        s_done = sem("s_done")
        s_free = [sem(f"s_free{i}") for i in range(2)]
        o_done = sem("o_done")
        o_free = [sem(f"o_free{i}") for i in range(2)]
        act_step, dve_step, pool_step = sem("act_step"), sem("dve_step"), sem("pool_step")
        consts_ready = sem("consts_ready")
        csil_ready = sem("csil_ready")
        sq_ready = sem("sq_ready")
        rs_ready = sem("rs_ready")
        h_ready = sem("h_ready")
        dtx_ready, dtw_ready, dtl_ready, dt_ready = sem("dtx"), sem("dtw"), sem("dtl"), sem("dt_ready")
        cum_stored, cum_in = sem("cum_stored"), [sem("cum_in0"), sem("cum_in1")]
        conv_begun, conv_done, xbc_ready = sem("conv_begun"), sem("conv_done"), sem("xbc_ready")
        z_ready, sc_c_ready, ysc_ready, gates_ready = sem("z_ready"), sem("sc_c_ready"), sem("ysc_ready"), sem("gates_ready")
        xtok_ready, cd_ready, scm_ready = sem("xtok_ready"), sem("cd_ready"), sem("scm_ready")
        diff_ready, decay_ready, m_ready, m_used = sem("diff"), sem("decay"), sem("m_ready"), sem("m_used")
        y_ready, yn_ready, mixin_ready, mix_ready = sem("y_ready"), sem("yn_ready"), sem("mixin_ready"), sem("mix_ready")
        x_ready = sem("x_ready")
        f_begun, f_conv, f_silu, f_act = sem("f_begun"), sem("f_conv"), sem("f_silu"), sem("f_act")
        tok_sq, tok_ready, feat_ready, ng_ready = sem("tok_sq"), sem("tok_ready"), sem("feat_ready"), sem("ng_ready")
        cqn_ready, mla_tok, mla_sq = sem("cqn_ready"), sem("mla_tok"), sem("mla_sq")
        tsum, trs, troped = sem("tsum"), sem("trs"), sem("troped")
        turned = sem("turned")
        cb_ready, hid_ready, kcn_ready, vcmp_ready = sem("cb_ready"), sem("hid_ready"), sem("kcn_ready"), sem("vcmp_ready")
        kc_sum, kc_rs = sem("kc_sum"), sem("kc_rs")
        cs_ready, ce_ready, cp_ready, ptc_ready = sem("cs_ready"), sem("ce_ready"), sem("cp_ready"), sem("ptc_ready")
        max_ready, exp_ready, p_ready, p_used = sem("max_ready"), sem("exp_ready"), sem("p_ready"), sem("p_used")
        pt_ready, pt_used, om_ready = sem("pt_ready"), sem("pt_used"), sem("om_ready")
        out_sem = sem("out_stored")

        class Steps:

            def __init__(self, eng, s):
                self.eng, self.s, self.n, self.loop = eng, s, 0, 0

            def mark(self, ins):
                self.n += 1
                ins.then_inc(self.s, 1)
                return self.loop + self.n

            def link(self, ins):
                self.eng.wait_ge(self.s, self.mark(ins))

            @contextmanager
            def repeat(self, times, per):
                before = self.n
                with self.eng.Fori(0, times, 1) as i:
                    if per:
                        self.loop = i * per
                    yield i
                    assert self.n - before == per, (self.n - before, per)
                self.loop = 0
                self.n = before + per * times

        def sbank(name, i=0):
            return psS[:, (SCRATCH[name] + i) % 2, :]

        block = ctx.enter_context(nc.Block())

        @block.sync
        def _(sp):
            sp.dma_start(par[:, :], par_in).then_inc(par_in_sem, 16)
            sp.dma_start(X[:, :, :], x_t).then_inc(x_in, 16)

            def load(c, shift=0, count=0):
                if c >= SLOTS:
                    sp.wait_ge(lin_done, PLAN.done_after[c - SLOTS] + count)
                n = PLAN.cols[c]
                sp.dma_start(ring[:, c % SLOTS, 0:n],
                             wts[bass.ds(c * P + shift * P, P), 0:n]).then_inc(w_arrived[c % SLOTS], 16)

            names = [n for n in PLAN.at if not n.endswith("scores")]
            for a, name in enumerate(names):
                first = PLAN.at[name][0]
                last = PLAN.at[names[a + 1]][0] if a + 1 < len(names) else CHUNKS
                c = first
                while c < min(first + SLOTS, last):
                    load(c)
                    c += 1
                rounds = (last - c) // SLOTS
                if rounds >= 2:
                    per = PLAN.done_after[c] - PLAN.done_after[c - SLOTS]
                    with sp.Fori(0, rounds, 1) as i:
                        for k in range(SLOTS):
                            load(c + k, i * SLOTS, i * per)
                    c += rounds * SLOTS
                while c < last:
                    load(c)
                    c += 1
            for j in range(KD):
                sp.wait_ge(x_ready, 3 * KD + j + 1)
                sp.dma_start(out_t[:, j * T:(j + 1) * T], X[:, j, :]).then_inc(out_sem, 16)
            sp.wait_ge(out_sem, 16 * KD)

        @block.gpsimd
        def _(pool):
            def load(n, shift=0, extra=0):
                if n >= ADA_SLOTS:
                    pool.wait_ge(ada_used, n - ADA_SLOTS + 1 + 8 + extra + shift)
                pool.dma_start(adaring[:, n % ADA_SLOTS, :],
                               ada_w[bass.ds(n * P + shift * P, P), :]).then_inc(ada_arrived[n % ADA_SLOTS], 16)

            for n in range(ADA_SLOTS):
                load(n)
            with pool.Fori(0, 11, 1) as i:
                for k in range(ADA_SLOTS):
                    load(ADA_SLOTS + k, i * ADA_SLOTS)
            pool.wait_ge(dt_ready, 1)
            pool.dma_start(cum_dram, dts[:, 5, :]).then_inc(cum_stored, 16)
            pool.wait_ge(cum_stored, 16)
            pool.wait_ge(s_done, SCRATCH["mod_b"] + 1)
            for g in range(NGRP):
                if g >= 2:
                    pool.wait_ge(diff_ready, 8 * (g - 1))
                pool.dma_start(CUMB[:, g % 2, :],
                               cum_dram[8 * g:8 * g + 8, :].rearrange("h t -> (h t)").partition_broadcast(P)
                               ).then_inc(cum_in[g % 2], 16)
            for n in range(48, 52):
                load(n)
            with pool.Fori(0, 11, 1) as i:
                for k in range(ADA_SLOTS):
                    load(52 + k, i * ADA_SLOTS, 8)

        @block.tensor
        def _(pe):
            def mm(out, lhsT, rhs, start, stop):
                return nc.tensor.matmul(out, lhsT, rhs, start=start, stop=stop)

            def chunk_wait(c, rounds=0):
                pe.wait_ge(w_arrived[c % SLOTS], 16 * (c // SLOTS + 1) + 16 * rounds)

            def bank_wait(u, rounds=0):
                if u >= 4:
                    pe.wait_ge(lin_free[u % 4], u // 4 + rounds)

            def scratch(name, i=0):
                n = SCRATCH[name] + i
                if n >= 2:
                    pe.wait_ge(s_free[n % 2], n // 2)
                return psS[:, n % 2, :]

            def obank(n):
                if n >= 2:
                    pe.wait_ge(o_free[n % 2], n // 2)
                return psO[:, n % 2, :]

            def unit(u, blocks, rhs, rounds=0, M=P):
                bank_wait(u, rounds)
                n = len(blocks)
                for k in range(n):
                    last = mm(psL[0:M, u % 4, 0:T], blocks[k], rhs(k), k == 0, k == n - 1)
                last.then_inc(lin_done, 1)

            def blk(c, b):
                return ring[:, c % SLOTS, b * P:(b + 1) * P]

            def linear8(name, chunks, rhs, first=0):
                c0, u0 = PLAN.at[name]
                c0, u0 = c0 + first, u0 + 2 * first

                def chunk(c, i=0):
                    chunk_wait(c0 + c, i)
                    for b in range(2):
                        unit(u0 + 2 * c + b, [blk(c0 + c, 8 * b + k) for k in range(8)], rhs, i * 2)

                done = SLOTS if u0 == 0 else 0
                for c in range(done):
                    chunk(c)
                rounds = (chunks - done) // SLOTS
                if rounds >= 2:
                    with pe.Fori(0, rounds, 1) as i:
                        for c in range(SLOTS):
                            chunk(done + c, i)
                    done += rounds * SLOTS
                for c in range(done, chunks):
                    chunk(c)

            def stat(name, squares, n, i=0):
                out = scratch(name, i)
                for k in range(n):
                    last = mm(out[:, 0:T], pv("ones"), squares(k), k == 0, k == n - 1)
                last.then_inc(s_done, 1)

            def mod_columns(name, lo, hi):
                out = scratch(name)
                for j in range(lo, hi):
                    last = mm(out[:, j - lo:j - lo + 1], acc[:, j * P:(j + 1) * P], pv("ones", 0, 1), True, True)
                last.then_inc(s_done, 1)

            def sq_at(k):
                return SQ[:, k * T:(k + 1) * T]

            def down(name):
                c0, u0 = PLAN.at[name]
                for m in range(8):
                    bank_wait(u0 + m)
                    for half in range(2):
                        c = c0 + 2 * m + half
                        chunk_wait(c)
                        for k in range(11):
                            kk = 11 * half + k
                            last = mm(psL[:, (u0 + m) % 4, 0:T], blk(c, k), FA[:, kk, :], kk == 0, kk == KF - 1)
                    last.then_inc(lin_done, 1)

            pe.wait_ge(par_in_sem, 16)
            pe.wait_ge(consts_ready, 3)
            pe.wait_ge(sq_ready, 1)
            stat("stat_mix", sq_at, 8)
            pe.wait_ge(ada_used, 8 + 16)
            mod_columns("mod_a", 0, 16)
            pe.wait_ge(h_ready, 8)
            out = scratch("dt")
            for k in range(KD):
                last = mm(out[0:32, 0:T], pv("w_dt", k * 32, 32), H[:, k, :], k == 0, k == 7)
            last.then_inc(s_done, 1)
            linear8("in1", 40, lambda k: H[:, k, :])
            pe.wait_ge(ada_used, 8 + 48)
            mod_columns("mod_b", 16, 48)
            pe.wait_ge(dt_ready, 1)
            out = scratch("dt_turn")
            for n, row in enumerate((5, 5, 3, 3)):
                last = nc.tensor.transpose(out[:, 32 * n:32 * n + 32], dts[:, row, (n % 2) * P:(n % 2 + 1) * P],
                                           pv("ident", 0, 32)[0:32, :])
            last.then_inc(s_done, 1)
            pe.wait_ge(xbc_ready, 6)
            for i in range(8):
                t, q = divmod(i, 4)
                out = scratch("x_turn", i)
                for b in range(4):
                    last = nc.tensor.transpose(out[:, b * P:(b + 1) * P], XBC[:, 4 * q + b, t * P:(t + 1) * P], pv("ident"))
                last.then_inc(s_done, 1)
            for g in range(NGRP):
                out = scratch("scores", g)
                mm(out[:, 0:256], XBC[:, 16 + g, 0:P], XBC[:, 20 + g, :], True, True)
                mm(out[:, 256:384], XBC[:, 16 + g, P:T], XBC[:, 20 + g, P:T], True, True).then_inc(s_done, 1)
            pe.wait_ge(xtok_ready, 8)
            for h in range(HEADS1):
                if h % 2 == 0:
                    ob = obank(OUT_Y + h // 2)
                pe.wait_ge(m_ready, h + 1)
                rows = slice(64 * (h % 2), 64 * (h % 2) + 64)
                cols = slice(64 * h, 64 * h + 64)
                mm(ob[rows, 0:T], XTOK[:, 0, cols], SM[:, h % 2, 0:256], True, False)
                last = mm(ob[rows, P:T], XTOK[:, 1, cols], SM[:, h % 2, 256:384], False, True)
                last.then_inc(m_used, 1)
            for g in range(NGRP):
                pe.wait_ge(sq_ready, 2 + g)
                stat("gnorm", lambda k: SQ[:, (g % 2) * 1024 + k * T:(g % 2) * 1024 + (k + 1) * T], 4, g)
            c0, u0 = PLAN.at["ssd_out"]
            pe.wait_ge(yn_ready, 16)
            for m in range(8):
                chunk_wait(c0 + m)
                unit(u0 + m, [blk(c0 + m, k) for k in range(16)], lambda k: Z[:, k, :])
            pe.wait_ge(ysc_ready, 8)
            linear8("sc_out", 4, lambda k: YSC[:, k, :])
            pe.wait_ge(mixin_ready, 8)
            linear8("o1", 4, lambda k: MIXIN[:, k, :])
            pe.wait_ge(sq_ready, 5 + 8)
            stat("stat_o1", sq_at, 8)
            pe.wait_ge(sq_ready, 14)
            stat("stat_ffn1", sq_at, 8)
            pe.wait_ge(h_ready, 16)
            linear8("up1", 22, lambda k: H[:, k, :])
            pe.wait_ge(f_act, KF)
            down("down1")
            pe.wait_ge(sq_ready, 14 + 8)
            stat("stat_down1", sq_at, 8)
            pe.wait_ge(ada_used, 16 + 96)
            mod_columns("mod_2", 0, 48)

            pe.wait_ge(sq_ready, 23)
            stat("stat_attn", sq_at, 8)
            pe.wait_ge(h_ready, 24)
            c0, u0 = PLAN.at["tok2"]
            for c in range(9):
                chunk_wait(c0 + c)
                for t in range(2):
                    u = u0 + 2 * c + t
                    bank_wait(u)
                    for k in range(KD):
                        last = mm(psL[:, u % 4, 0:256], H[:, k, t * P:(t + 1) * P],
                                  ring[:, (c0 + c) % SLOTS, k * 256:(k + 1) * 256], k == 0, k == 7)
                    last.then_inc(lin_done, 1)
            c0, u0 = PLAN.at["mix2"]
            chunk_wait(c0)
            for t in range(2):
                bank_wait(u0 + t)
                for k in range(KD):
                    last = mm(psL[:, (u0 + t) % 4, 0:88], H[:, k, t * P:(t + 1) * P],
                              ring[:, c0 % SLOTS, k * 88:(k + 1) * 88], k == 0, k == 7)
                last.then_inc(lin_done, 1)
            unit(u0 + 2, [ring[:, c0 % SLOTS, 704 + k * P:704 + (k + 1) * P] for k in range(8)], lambda k: H[:, k, :])
            linear8("feat2", 11, lambda k: H[:, k, :])
            pe.wait_ge(sq_ready, 24)
            stat("stat_cq", sq_at, 3)
            stat("stat_ckv", lambda k: sq_at(3 + k), 2)
            pe.wait_ge(cqn_ready, 5)
            c0, u0 = PLAN.at["uq"]
            for c in range(3):
                chunk_wait(c0 + c)
                for t in range(2):
                    u = u0 + 2 * c + t
                    bank_wait(u)
                    for k in range(3):
                        last = mm(psL[:, u % 4, :], CQ[:, k, t * P:(t + 1) * P],
                                  ring[:, (c0 + c) % SLOTS, k * 512:(k + 1) * 512], k == 0, k == 2)
                    last.then_inc(lin_done, 1)
            c0, u0 = PLAN.at["ukv"]
            for c in range(2):
                chunk_wait(c0 + c)
                for n in range(4):
                    u, piece, t = u0 + 4 * c + n, n // 2, n % 2
                    bank_wait(u)
                    for k in range(2):
                        last = mm(psL[:, u % 4, :], CKV[:, k, t * P:(t + 1) * P],
                                  ring[:, (c0 + c) % SLOTS, piece * 1024 + k * 512:piece * 1024 + (k + 1) * 512],
                                  k == 0, k == 1)
                    last.then_inc(lin_done, 1)
            for i in range(7):
                if i == 0:
                    pe.wait_ge(troped, 4)
                out = scratch("nsa_turn", i)
                for n in range(4):
                    hh, t = divmod(n, 2)
                    src = (QTOK[:, t, (2 * i + hh) * HD:(2 * i + hh + 1) * HD] if i < 4 else
                           KTOK[:, t, (2 * (i - 4) + hh) * HD:(2 * (i - 4) + hh + 1) * HD])
                    last = nc.tensor.transpose(out[:, n * P:(n + 1) * P], src, pv("ident"))
                last.then_inc(s_done, 1)
            c0, u0 = PLAN.at["cmp"]
            for kv in range(2):
                pe.wait_ge(cb_ready, kv + 1)
                for half in range(2):
                    u = u0 + 2 * kv + half
                    bank_wait(u)
                    for l in range(32):
                        c = c0 + 4 * kv + 2 * half + l // 16
                        if l % 16 == 0:
                            chunk_wait(c)
                        last = mm(psL[:, u % 4, 0:30], blk(c, l % 16), CB[kv][:, l, :], l == 0, l == 31)
                    last.then_inc(lin_done, 1)
            pe.wait_ge(hid_ready, 2)
            out = scratch("kc")
            for half in range(2):
                last = mm(out[0:30, 0:P], HID[:, half, :], pv("k_w2", half * P, P), half == 0, half == 1)
            last.then_inc(s_done, 1)
            pe.wait_ge(kcn_ready, 1)
            out = scratch("kc_turn")
            nc.tensor.transpose(out[:, 0:30], KCN, pv("ident", 0, 30)[0:30, :]).then_inc(s_done, 1)
            pe.wait_ge(hid_ready, 4)
            out = scratch("vc")
            for g in range(2):
                for half in range(2):
                    last = mm(out[0:NCMP, g * P:(g + 1) * P], HID[:, 2 + half, g * NCMP:(g + 1) * NCMP],
                              pv("v_w2", half * P, P), half == 0, half == 1)
            last.then_inc(s_done, 1)
            u = PLAN.at["cmp_scores"][1]
            bank_wait(u)
            pe.wait_ge(turned, 7 + 1)
            for h in range(NH):
                for t in range(2):
                    o = (2 * h + t) * NCMP
                    last = mm(psL[:, u % 4, o:o + NCMP], QT[:, h, t * P:(t + 1) * P],
                              KCT[:, (h // 4) * NCMP:(h // 4 + 1) * NCMP], True, True)
            last.then_inc(lin_done, 1)

            def attend(name, pname, obase, count, score, value, lead_in, p0):
                u0 = PLAN.at[name][1]
                for i in range(count + 2):
                    if i < count:
                        u = u0 + i
                        bank_wait(u)
                        out = psL[:, u % 4, :]
                        score(i, out[:, 0:P], 0, P, True)
                        mm(out[:, 0:P], identb[:, :], maskb[:, :], False, True)
                        score(i, out[:, P:384], P, T, True)
                        mm(out[:, 256:384], identb[:, :], maskb[:, :], False, True).then_inc(lin_done, 1)
                    if 1 <= i <= count:
                        n = i - 1
                        out = scratch(pname, n)
                        pe.wait_ge(p_ready, p0 + n + 1)
                        pr = PR[:, (p0 + n) % 2, :]
                        for b in range(3):
                            last = nc.tensor.transpose(out[:, b * P:(b + 1) * P], pr[:, b * P:(b + 1) * P], pv("ident"))
                        last.then_inc(s_done, 1)
                    if i >= 2:
                        n = i - 2
                        per = 2 if name == "nsa_scores" else 1
                        if n % per == 0:
                            ob = obank(obase + n // per)
                            if lead_in:
                                lead_in(n // per, ob)
                        pe.wait_ge(pt_ready, p0 + n + 1)
                        v0, v1 = value(n)
                        mm(ob[:, 0:T], v0, PT[:, (p0 + n) % 2, 0:256], n % per == 0 and not lead_in, False)
                        last = mm(ob[:, P:T], v1, PT[:, (p0 + n) % 2, 256:384], False, n % per == per - 1)
                        last.then_inc(pt_used, 1)

            for j in range(4):
                out = scratch("cmp_turn", j)
                pe.wait_ge(cp_ready, 1)
                for n in range(4):
                    o = (4 * j + n) * NCMP
                    last = nc.tensor.transpose(out[0:NCMP, n * P:(n + 1) * P], CS[:, o:o + NCMP], pv("ident"))
                last.then_inc(s_done, 1)
            pe.wait_ge(ptc_ready, 4)
            pe.wait_ge(vcmp_ready, 1)

            def nsa_score(i, out, q0, n_keys, start):
                h, b = divmod(i, 2)
                mm(out, QT[:, h, q0:q0 + P], KT[:, 2 * b + h // 4, 0:n_keys], start, False)

            def nsa_value(n):
                h, b = divmod(n, 2)
                o = b * 256 + (h // 4) * HD
                return VTOK[:, 0, o:o + HD], VTOK[:, 1, o:o + HD]

            def cmp_value(h, ob):
                mm(ob[:, 0:T], VCMP[:, h // 4, :], PTC[0:NCMP, h, :], True, False)

            attend("nsa_scores", "nsa_p", OUT_NSA, 16, nsa_score, nsa_value, cmp_value, 0)

            for i in range(16):
                kind, pair = divmod(i, 4)
                src, lo, wd = ((QB, 0, HD), (QB, HD, ROPE), (KB, 0, HD), (KB, HD, ROPE))[kind]
                if i == 0:
                    pe.wait_ge(troped, 8)
                out = scratch("mla_turn", i)
                for n in range(4):
                    hh, t = divmod(n, 2)
                    o = (2 * pair + hh) * QK + lo
                    last = nc.tensor.transpose(out[0:wd, n * P:(n + 1) * P], src[:, t, o:o + wd], pv("ident"))
                last.then_inc(s_done, 1)
            pe.wait_ge(turned, 8 + 16)

            def mla_score(i, out, q0, n_keys, start):
                mm(out, MQN[:, i, q0:q0 + P], MKN[:, i, 0:n_keys], start, False)
                mm(out, MQR[0:ROPE, i, q0:q0 + P], MKR[0:ROPE, i, 0:n_keys], False, False)

            def mla_value(n):
                return VB[:, 0, n * HD:(n + 1) * HD], VB[:, 1, n * HD:(n + 1) * HD]

            attend("mla_scores", "mla_p", OUT_MLA, 8, mla_score, mla_value, None, 16)
            pe.wait_ge(om_ready, 16)
            linear8("o2", 4, lambda k: OM[:, k, :])
            pe.wait_ge(sq_ready, 25)
            stat("stat_ffn2", sq_at, 8)
            pe.wait_ge(h_ready, 32)
            linear8("up2", 22, lambda k: H[:, k, :])
            pe.wait_ge(f_act, 2 * KF)
            down("down2")

        @block.scalar
        def _(act):
            st = Steps(act, act_step)
            A = nc.scalar.activation

            def stat_root(name, width, dst, i=0):
                act.wait_ge(s_done, SCRATCH[name] + i + 1)
                n = SCRATCH[name] + i
                A(dst, sbank(name, i)[:, 0:T], ACT.Ln, scale=1.0 / width, bias=eps_col[:, :]).then_inc(s_free[n % 2], 1)
                act.wait_ge(s_free[n % 2], n // 2 + 1)
                A(dst, dst, ACT.Exp, scale=-0.5).then_inc(rs_ready, 1)

            act.wait_ge(par_in_sem, 16)
            act.wait_ge(consts_ready, 3)
            A(csil[:, :], par[:, 0:16], ACT.Silu).then_inc(csil_ready, 1)
            act.wait_ge(x_in, 16)
            A(SQ[:, :], X[:, :, :].rearrange("p a b -> p (a b)"), ACT.Square).then_inc(sq_ready, 1)
            stat_root("stat_mix", D, RS[:, 0, :])
            n = SCRATCH["dt"]
            act.wait_ge(s_done, n + 1)
            A(dts[:, 0, :], psS[0:32, n % 2, 0:T], ACT.Identity, bias=pv("dt_bias")[0:32, :]).then_inc(s_free[n % 2], 1)
            act.wait_ge(s_free[n % 2], n // 2 + 1)
            st.link(A(dts[:, 1, :], dts[:, 0, :], ACT.Abs))
            st.link(A(dts[:, 1, :], dts[:, 1, :], ACT.Exp, scale=-1.0))
            A(sm[0:32, 95:96], pv("a_log")[0:32, :], ACT.Exp).then_inc(dtx_ready, 1)
            act.wait_ge(dtw_ready, 1)
            A(dts[:, 4, :], dts[:, 2, :], ACT.Ln).then_inc(dtl_ready, 1)
            u0 = PLAN.at["in1"][1]
            c_w, c_b = PAR["xconv_w"][0], PAR["xconv_b"][0]
            with st.repeat(6, 0) as i:
                for k in range(4):
                    m = i * 4 + k
                    act.wait_ge(lin_done, m + u0 + 1)
                    A(XBC[:, bass.ds(m, 1), :].rearrange("p a b -> p (a b)"), psL[:, (u0 + k) % 4, 0:T], ACT.Identity,
                      scale=par[:, bass.ds(m + (c_w + 3 * NXBC), 1)], bias=par[:, bass.ds(m + c_b, 1)]).then_inc(conv_begun, 1)
            for q in range(6):
                act.wait_ge(conv_done, 4 * (q + 1))
                piece = XBC[:, 4 * q:4 * q + 4, :].rearrange("p a b -> p (a b)")
                A(piece, piece, ACT.Silu).then_inc(xbc_ready, 1)

            def evacuate(u, n, dst, func, signal):
                with st.repeat(n // 4, 0) as i:
                    for k in range(4):
                        act.wait_ge(lin_done, i * 4 + (u + k + 1))
                        A(dst[:, bass.ds(i * 4 + k, 1), :].rearrange("p a b -> p (a b)"), psL[:, (u + k) % 4, 0:T],
                          func).then_inc(lin_free[(u + k) % 4], 1)
                for k in range(4):
                    act.wait_ge(lin_free[(u + k) % 4], (u + k) // 4 + n // 4)
                act.sem_inc(signal, 1)

            evacuate(u0 + 24, 16, Z, ACT.Silu, z_ready)
            evacuate(u0 + 40, 8, SCQ, ACT.Copy, sc_c_ready)
            evacuate(u0 + 64, 16, G1, ACT.Sigmoid, gates_ready)
            n = SCRATCH["dt_turn"]
            act.wait_ge(s_done, n + 1)
            A(CD[:, :, :].rearrange("p a b -> p (a b)"), psS[:, n % 2, 0:128], ACT.Copy).then_inc(s_free[n % 2], 1)
            act.wait_ge(s_free[n % 2], n // 2 + 1)
            act.sem_inc(cd_ready, 1)
            act.wait_ge(cum_stored, 16)
            for i in range(8):
                n = SCRATCH["x_turn"] + i
                t, q = divmod(i, 4)
                act.wait_ge(s_done, n + 1)
                A(XTOK[:, t, 512 * q:512 * q + 512], psS[:, n % 2, :], ACT.Copy).then_inc(s_free[n % 2], 1)
                act.wait_ge(s_free[n % 2], n // 2 + 1)
                act.sem_inc(xtok_ready, 1)
            for h in range(HEADS1):
                act.wait_ge(diff_ready, h + 1)
                A(SE[:, h % 2, :], SE[:, h % 2, :], ACT.Exp).then_inc(decay_ready, 1)
            for g in range(NGRP):
                act.wait_ge(y_ready, 4 * (g + 1))
                if g == 0:
                    act.wait_ge(m_ready, HEADS1)
                if g >= 2:
                    act.wait_ge(s_done, SCRATCH["gnorm"] + g - 1)
                A(SQ[:, (g % 2) * 1024:(g % 2 + 1) * 1024], Z[:, 4 * g:4 * g + 4, :].rearrange("p a b -> p (a b)"),
                  ACT.Square).then_inc(sq_ready, 1)
                if g >= 1:
                    if g >= 3:
                        act.wait_ge(yn_ready, 4 * (g - 2))
                    stat_root("gnorm", 512, RS[:, (g - 1) % 2, :], g - 1)
            act.wait_ge(yn_ready, 8)
            stat_root("gnorm", 512, RS[:, 1, :], 3)

            def copy_and_square(name, dst):
                u0 = PLAN.at[name][1]
                for m in range(8):
                    u = u0 + m
                    act.wait_ge(lin_done, u + 1)
                    if m == 0:
                        act.wait_ge(sq_free, sq_uses[name])
                    st.mark(A(dst[:, m, :], psL[:, u % 4, 0:T], ACT.Copy))
                    A(SQ[:, m * T:(m + 1) * T], psL[:, u % 4, 0:T], ACT.Square).then_inc(lin_free[u % 4], 1)
                    act.wait_ge(lin_free[u % 4], u // 4 + 1)
                    act.wait_ge(act_step, st.n)
                    act.sem_inc(sq_ready, 1)

            def square_x(after):
                act.wait_ge(x_ready, after)
                A(SQ[:, :], X[:, :, :].rearrange("p a b -> p (a b)"), ACT.Square).then_inc(sq_ready, 1)

            sq_free, sq_uses = s_done, {"o1": SCRATCH["gnorm"] + 4, "down1": SCRATCH["stat_ffn1"] + 1}
            copy_and_square("o1", MIX)
            stat_root("stat_o1", D, RS[:, 0, :])
            square_x(8)
            stat_root("stat_ffn1", D, RS[:, 1, :])

            def ffn(name, wname, bname, base):
                u0 = PLAN.at[name][1]
                w0, b0 = PAR[wname][0], PAR[bname][0]

                def begin(j, slot, it=0):
                    for b in range(2):
                        u = u0 + 2 * j + b
                        act.wait_ge(lin_done, u + 1 + it * 2)
                        if b == 0 and (j + base >= 2):
                            act.wait_ge(f_act, base + j - 1 + it)
                        A(CT[:, 2 * slot + b, :], psL[:, u % 4, 0:T], ACT.Identity,
                          scale=par[:, bass.ds(w0 + 2 * 44 + b * KF + j + it, 1)],
                          bias=par[:, bass.ds(b0 + b * KF + j + it, 1)]).then_inc(f_begun, 1)

                def silu(j, slot, it=0):
                    act.wait_ge(f_conv, base + j + 1 + it)
                    A(CT[:, 2 * slot, :], CT[:, 2 * slot, :], ACT.Silu).then_inc(f_silu, 1)

                begin(0, 0)
                begin(1, 1)
                silu(0, 0)
                with st.repeat(10, 0) as i:
                    begin(2, 0, i * 2)
                    silu(1, 1, i * 2)
                    begin(3, 1, i * 2)
                    silu(2, 0, i * 2)
                silu(21, 1)

            ffn("up1", "fconv_w", "fconv_b", 0)
            copy_and_square("down1", FO)
            stat_root("stat_down1", D, RS[:, 0, :])

            square_x(16)
            stat_root("stat_attn", D, RS[:, 1, :])
            u0 = PLAN.at["tok2"][1]
            act.wait_ge(s_done, SCRATCH["stat_attn"] + 1)
            for c in range(6):
                for t in range(2):
                    u = u0 + 2 * c + t
                    act.wait_ge(lin_done, u + 1)
                    for hh in range(2):
                        n = 4 * c + 2 * t + hh
                        if n >= 16:
                            act.wait_ge(tok_sq, n - 15)
                        A(SQ[:, n % 16 * P:(n % 16 + 1) * P], psL[:, u % 4, hh * P:(hh + 1) * P], ACT.Square,
                          accum_out=sm[:, t * 12 + 2 * c + hh:t * 12 + 2 * c + hh + 1]).then_inc(tok_sq, 1)
            for c in range(3):
                for t in range(2):
                    u = u0 + 2 * (6 + c) + t
                    act.wait_ge(lin_done, u + 1)
                    dst = KTOK[:, t, 512:768] if c == 0 else VTOK[:, t, (c - 1) * 256:c * 256]
                    A(dst, psL[:, u % 4, 0:256], ACT.Copy).then_inc(lin_free[u % 4], 1)
                    act.wait_ge(lin_free[u % 4], u // 4 + 1)
            act.sem_inc(tok_ready, 1)
            act.wait_ge(tok_sq, 24)
            st.link(A(sm[:, 0:24], sm[:, 0:24], ACT.Ln, scale=1.0 / HD, bias=eps_col[:, :]))
            A(sm[:, 0:24], sm[:, 0:24], ACT.Exp, scale=-0.5).then_inc(trs, 1)
            u0 = PLAN.at["mix2"][1]
            for t in range(2):
                u = u0 + t
                act.wait_ge(lin_done, u + 1)
                st.mark(A(KR[:, t, :], psL[:, u % 4, 0:64], ACT.Copy))
                st.mark(A(SQ[:, 64 * t:64 * t + 64], psL[:, u % 4, 0:64], ACT.Square, accum_out=sm[:, 24 + t:25 + t]))
                A(GT[:, t, :], psL[:, u % 4, 64:88], ACT.Sigmoid).then_inc(lin_free[u % 4], 1)
                act.wait_ge(lin_free[u % 4], u // 4 + 1)
            act.wait_ge(act_step, st.n)
            act.sem_inc(ng_ready, 1)
            for m in range(7):
                u = u0 + 2 + m
                dst = VC[:, m, :] if m < 2 else CQ[:, m - 2, :] if m < 5 else CKV[:, m - 5, :]
                act.wait_ge(lin_done, u + 1)
                if m >= 2:
                    st.mark(A(SQ[:, (m - 2) * T:(m - 1) * T], psL[:, u % 4, 0:T], ACT.Square))
                A(dst, psL[:, u % 4, 0:T], ACT.Copy).then_inc(lin_free[u % 4], 1)
                act.wait_ge(lin_free[u % 4], u // 4 + 1)
            act.wait_ge(act_step, st.n)
            act.sem_inc(sq_ready, 1)
            act.sem_inc(feat_ready, 1)
            evacuate(u0 + 9, 16, G2, ACT.Sigmoid, gates_ready)
            act.wait_ge(h_ready, 24)
            stat_root("stat_cq", 384, RS[:, 0, :])
            stat_root("stat_ckv", 256, RS[:, 1, :])
            u0 = PLAN.at["uq"][1]
            for c in range(3):
                for t in range(2):
                    u = u0 + 2 * c + t
                    act.wait_ge(lin_done, u + 1)
                    A(QB[:, t, c * 512:(c + 1) * 512], psL[:, u % 4, :], ACT.Copy).then_inc(lin_free[u % 4], 1)
                    act.wait_ge(lin_free[u % 4], u // 4 + 1)
            u0 = PLAN.at["ukv"][1]
            for n in range(8):
                c, t = n // 2, n % 2
                u = u0 + n
                act.wait_ge(lin_done, u + 1)
                src = psL[:, u % 4, :].rearrange("p (h w) -> p h w", w=256)
                st.mark(A(KB[:, t, :].rearrange("p (h w) -> p h w", w=QK)[:, 2 * c:2 * c + 2, 0:HD], src[:, :, 0:HD], ACT.Copy))
                A(VB[:, t, :].rearrange("p (h w) -> p h w", w=HD)[:, 2 * c:2 * c + 2, :], src[:, :, HD:256],
                  ACT.Copy).then_inc(lin_free[u % 4], 1)
                act.wait_ge(lin_free[u % 4], u // 4 + 1)
            act.wait_ge(act_step, st.n)
            act.sem_inc(mla_tok, 1)
            for i in range(7):
                n = SCRATCH["nsa_turn"] + i
                act.wait_ge(s_done, n + 1)
                dst = (QT[:, 2 * i:2 * i + 2, :] if i < 4 else KT[:, 2 * (i - 4):2 * (i - 4) + 2, :])
                A(dst.rearrange("p a b -> p (a b)"), psS[:, n % 2, :], ACT.Copy).then_inc(s_free[n % 2], 1)
                act.wait_ge(s_free[n % 2], n // 2 + 1)
                act.sem_inc(turned, 1)
            act.wait_ge(tsum, 1)
            st.link(A(mlars[:, :], mlars[:, :], ACT.Ln, scale=1.0 / QK, bias=eps_col[:, :]))
            A(mlars[:, :], mlars[:, :], ACT.Exp, scale=-0.5).then_inc(mla_sq, 1)
            u0 = PLAN.at["cmp"][1]
            for n in range(4):
                u = u0 + n
                act.wait_ge(lin_done, u + 1)
                A(HID[:, n, :], psL[:, u % 4, 0:30], ACT.Silu).then_inc(lin_free[u % 4], 1)
                act.wait_ge(lin_free[u % 4], u // 4 + 1)
                act.sem_inc(hid_ready, 1)
            n = SCRATCH["kc"]
            act.wait_ge(s_done, n + 1)
            st.link(A(KCD, psS[0:30, n % 2, 0:P], ACT.Square, accum_out=sm[0:30, 60:61]))
            st.link(A(sm[0:30, 60:61], sm[0:30, 60:61], ACT.Ln, scale=1.0 / HD, bias=eps_col[0:30, :]))
            A(sm[0:30, 60:61], sm[0:30, 60:61], ACT.Exp, scale=-0.5).then_inc(kc_rs, 1)
            n = SCRATCH["kc_turn"]
            act.wait_ge(s_done, n + 1)
            A(KCT, psS[:, n % 2, 0:30], ACT.Copy).then_inc(s_free[n % 2], 1)
            act.wait_ge(s_free[n % 2], n // 2 + 1)
            act.sem_inc(turned, 1)
            n = SCRATCH["vc"]
            act.wait_ge(s_done, n + 1)
            A(VCMP.rearrange("p a b -> p (a b)"), psS[0:NCMP, n % 2, 0:256], ACT.Copy).then_inc(s_free[n % 2], 1)
            act.wait_ge(s_free[n % 2], n // 2 + 1)
            act.sem_inc(vcmp_ready, 1)
            act.wait_ge(cs_ready, 1)
            A(CS, CS, ACT.Exp).then_inc(ce_ready, 1)
            act.wait_ge(lin_done, PLAN.at["uq"][1])
            for j in range(4):
                n = SCRATCH["cmp_turn"] + j
                act.wait_ge(s_done, n + 1)
                A(PTC[0:NCMP, 2 * j:2 * j + 2, :].rearrange("p a b -> p (a b)"), psS[0:NCMP, n % 2, :],
                  ACT.Copy).then_inc(s_free[n % 2], 1)
                act.wait_ge(s_free[n % 2], n // 2 + 1)
                act.sem_inc(ptc_ready, 1)

            def softmax(pname, count, p0):
                for i in range(count + 1):
                    if i < count:
                        n = p0 + i
                        u = PLAN.at["nsa_scores"][1] + n
                        act.wait_ge(max_ready, n + 1)
                        if n >= 2:
                            act.wait_ge(s_done, SCRATCH["nsa_p"] + n - 1 if n - 2 < 16 else SCRATCH["mla_p"] + n - 16 - 1)
                        st.mark(A(PR[:, n % 2, 0:P], psL[:, u % 4, 0:P], ACT.Exp, bias=sm[:, 26 + 4 * (n % 2):27 + 4 * (n % 2)],
                                  accum_out=sm[:, 28 + 4 * (n % 2):29 + 4 * (n % 2)]))
                        A(PR[:, n % 2, P:384], psL[:, u % 4, P:384], ACT.Exp, bias=sm[:, 27 + 4 * (n % 2):28 + 4 * (n % 2)],
                          accum_out=sm[:, 29 + 4 * (n % 2):30 + 4 * (n % 2)]).then_inc(lin_free[u % 4], 1)
                        act.wait_ge(lin_free[u % 4], u // 4 + 1)
                        act.wait_ge(act_step, st.n)
                        act.sem_inc(exp_ready, 1)
                    if i >= 1:
                        m = p0 + i - 1
                        n = SCRATCH[pname] + i - 1
                        act.wait_ge(s_done, n + 1)
                        if m >= 2:
                            act.wait_ge(pt_used, m - 1)
                        A(PT[:, m % 2, :], psS[:, n % 2, 0:384], ACT.Copy).then_inc(s_free[n % 2], 1)
                        act.wait_ge(s_free[n % 2], n // 2 + 1)
                        act.sem_inc(pt_ready, 1)

            softmax("nsa_p", 16, 0)
            act.wait_ge(pt_used, 16)
            for i in range(16):
                kind, pair = divmod(i, 4)
                dst, wd = ((MQN, HD), (MQR, ROPE), (MKN, HD), (MKR, ROPE))[kind]
                n = SCRATCH["mla_turn"] + i
                act.wait_ge(s_done, n + 1)
                A(dst[0:wd, 2 * pair:2 * pair + 2, :].rearrange("p a b -> p (a b)"), psS[0:wd, n % 2, :],
                  ACT.Copy).then_inc(s_free[n % 2], 1)
                act.wait_ge(s_free[n % 2], n // 2 + 1)
                act.sem_inc(turned, 1)
            softmax("mla_p", 8, 16)
            square_x(24)
            stat_root("stat_ffn2", D, RS[:, 0, :])
            ffn("up2", "fconv_w_2", "fconv_b_2", KF)

        @block.vector
        def _(dve):
            st = Steps(dve, dve_step)
            V = nc.vector

            def scratch_wait(name, i=0):
                n = SCRATCH[name] + i
                dve.wait_ge(s_done, n + 1)
                return psS[:, n % 2, :], s_free[n % 2]

            def lin(u, rounds=0):
                dve.wait_ge(lin_done, u + 1 + rounds)
                return psL[:, u % 4, 0:T]

            V.memset(eps_col[:, :], EPS).then_inc(consts_ready, 1)
            V.memset(acc[:, :], 0.0).then_inc(ada_used, 8)
            dve.wait_ge(par_in_sem, 16)
            V.tensor_copy(identb[:, :], pv("ident")).then_inc(consts_ready, 1)
            V.tensor_copy(maskb[:, :], pv("causal_add")).then_inc(consts_ready, 1)
            dve.wait_ge(csil_ready, 1)
            dve.wait_ge(ada_used, 8)

            def ada_step(n, group, col, cleared, groups, rounds=0, total=0):
                dve.wait_ge(ada_arrived[n % ADA_SLOTS], 16 * (n // ADA_SLOTS + 1) + rounds * (16 * total // ADA_SLOTS))
                dve.wait_ge(ada_used, cleared + n - groups + 1 + rounds * total)
                a = acc[:, group * ADA_COLS:(group + 1) * ADA_COLS]
                V.scalar_tensor_tensor(a, adaring[:, n % ADA_SLOTS, :], col, a, MUL, ADD).then_inc(ada_used, 1)

            with st.repeat(4, 0) as i:
                for kk in range(2):
                    for g in range(2):
                        ada_step(2 * kk + g, g, csil[:, bass.ds(i * 2 + kk, 1)], 8, 2, i, 4)

            def make_h(shift, gains, rs):
                for j in range(KD):
                    st.link(V.scalar_tensor_tensor(H[:, j, :], X[:, j, :], gains[:, j:j + 1], rs, MUL, MUL))
                    V.tensor_scalar(H[:, j, :], H[:, j, :], shift[:, j:j + 1], None, ADD).then_inc(h_ready, 1)

            ps, free = scratch_wait("mod_a")
            V.tensor_tensor(mod[:, 0:16], ps[:, 0:16], pv("ada_b", 0, 16), ADD).then_inc(free, 1)
            dve.wait_ge(free, SCRATCH["mod_a"] // 2 + 1)
            st.link(V.scalar_tensor_tensor(lead[:, 0:8], mod[:, 8:16], 1.0, pv("mix_pre_g"), ADD, MUL))
            dve.wait_ge(x_in, 16)
            dve.wait_ge(rs_ready, 1)
            make_h(mod[:, 0:8], lead[:, 0:8], RS[:, 0, :])

            dve.wait_ge(dtx_ready, 1)
            V.tensor_scalar(dts[:, 2, :], dts[:, 1, :], 1.0, None, ADD).then_inc(dtw_ready, 1)
            dve.wait_ge(dtw_ready, 1)
            st.link(V.tensor_scalar(dts[:, 3, :], dts[:, 2, :], 1.0, 1e-30, SUB, ALU.max))
            st.link(V.reciprocal(dts[:, 3, :], dts[:, 3, :]))
            st.link(V.tensor_tensor(dts[:, 3, :], dts[:, 3, :], dts[:, 1, :], MUL))
            dve.wait_ge(dtl_ready, 1)
            st.mark(V.scalar_tensor_tensor(dts[:, 5, :], dts[:, 2, :], 1.0, dts[:, 1, :], ALU.is_equal, MUL))
            st.link(V.tensor_tensor(dts[:, 3, :], dts[:, 3, :], dts[:, 4, :], MUL))
            st.link(V.tensor_tensor(dts[:, 3, :], dts[:, 3, :], dts[:, 5, :], ADD))
            st.link(V.scalar_tensor_tensor(dts[:, 3, :], dts[:, 0, :], 0.0, dts[:, 3, :], ALU.max, ADD))
            st.mark(V.memset(dts[:, 2, :], 1.0))
            st.link(V.tensor_scalar(dts[:, 4, :], dts[:, 3, :], sm[0:32, 95:96], -1.0, MUL, MUL))
            V.tensor_tensor_scan(dts[:, 5, :], dts[:, 2, :], dts[:, 4, :], 0.0, MUL, ADD).then_inc(dt_ready, 1)

            u0 = PLAN.at["in1"][1]
            c_w = PAR["xconv_w"][0]
            with st.repeat(6, 8) as i:
                for k in range(4):
                    m = i * 4 + k
                    dve.wait_ge(conv_begun, m + 1)
                    dst = XBC[:, bass.ds(m, 1), :].rearrange("p a b -> p (a b)")
                    for back in (1, 2, 3):
                        ins = V.scalar_tensor_tensor(
                            XBC[:, bass.ds(m, 1), back:T].rearrange("p a b -> p (a b)"), psL[:, (u0 + k) % 4, 0:T - back],
                            par[:, bass.ds(m + (c_w + (3 - back) * NXBC), 1)],
                            XBC[:, bass.ds(m, 1), back:T].rearrange("p a b -> p (a b)"), MUL, ADD)
                        if back < 3:
                            st.link(ins)
                        else:
                            ins.then_inc(lin_free[(u0 + k) % 4], 1)
                    dve.wait_ge(lin_free[(u0 + k) % 4], (u0 + k) // 4 + 1 + i)
                    dve.sem_inc(conv_done, 1)
            with st.repeat(4, 0) as i:
                for kk in range(2):
                    for g in range(4):
                        ada_step(16 + 4 * kk + g, 2 + g, csil[:, bass.ds(i * 2 + kk, 1)], 8, 4, i, 8)
            dve.wait_ge(sc_c_ready, 1)
            s_w = PAR["sconv_w"][0]

            def col(buf, j, lo=0, hi=T):
                return buf[:, bass.ds(j, 1), lo:hi].rearrange("p a b -> p (a b)")

            with st.repeat(2, 12) as i:
                for k in range(4):
                    j = i * 4 + k
                    u = u0 + 48 + k
                    dve.wait_ge(lin_done, u + 1 + i * 4)
                    V.tensor_tensor(CT[:, k % 2, :], col(SCQ, j), psL[:, u % 4, 0:T], MUL).then_inc(lin_free[u % 4], 1)
                    dve.wait_ge(lin_free[u % 4], u // 4 + 1 + i)
                    st.link(V.tensor_scalar(col(SCQ, j), CT[:, k % 2, :], par[:, bass.ds(j + (s_w + 16), 1)], None, MUL))
                    st.link(V.scalar_tensor_tensor(col(SCQ, j, 1), CT[:, k % 2, 0:T - 1], par[:, bass.ds(j + (s_w + 8), 1)],
                                                   col(SCQ, j, 1), MUL, ADD))
                    st.link(V.scalar_tensor_tensor(col(SCQ, j, 2), CT[:, k % 2, 0:T - 2], par[:, bass.ds(j + s_w, 1)],
                                                   col(SCQ, j, 2), MUL, ADD))
            with st.repeat(2, 0) as i:
                for k in range(4):
                    j = i * 4 + k
                    u = u0 + 56 + k
                    dve.wait_ge(lin_done, u + 1 + i * 4)
                    V.tensor_tensor(col(YSC, j), col(SCQ, j), psL[:, u % 4, 0:T], MUL).then_inc(lin_free[u % 4], 1)
            for k in range(4):
                u = u0 + 60 + k
                dve.wait_ge(lin_free[u % 4], u // 4 + 1)
            dve.sem_inc(ysc_ready, 8)
            ps, free = scratch_wait("mod_b")
            V.tensor_tensor(mod[:, 16:48], ps[:, 0:32], pv("ada_b", 16, 32), ADD).then_inc(free, 1)
            dve.wait_ge(free, SCRATCH["mod_b"] // 2 + 1)
            st.mark(V.tensor_tensor(lead[:, 8:16], mod[:, 16:24], pv("mix_post_g"), MUL))
            st.mark(V.scalar_tensor_tensor(lead[:, 16:24], mod[:, 32:40], 1.0, pv("ffn_pre_g"), ADD, MUL))
            st.link(V.tensor_tensor(lead[:, 24:32], mod[:, 40:48], pv("ffn_post_g"), MUL))

            for g in range(NGRP):
                ps, free = scratch_wait("scores", g)
                st.mark(V.tensor_tensor(SCM[:, g, 0:P], ps[:, 0:P], pv("causal01"), MUL))
                st.mark(V.tensor_copy(SCM[:, g, P:256], ps[:, P:256]))
                V.tensor_tensor(SCM[:, g, 256:384], ps[:, 256:384], pv("causal01"), MUL).then_inc(free, 1)
                dve.wait_ge(free, (SCRATCH["scores"] + g) // 2 + 1)
            dve.wait_ge(dve_step, st.n)
            dve.wait_ge(cd_ready, 1)
            dve.wait_ge(xbc_ready, 6)
            dve.wait_ge(z_ready, 1)
            dve.wait_ge(s_done, SCRATCH["mod_b"] + 1)

            def y_out(j):
                n = OUT_Y + j
                dve.wait_ge(m_used, 2 * j + 2)
                V.scalar_tensor_tensor(XBC[:, j, :], XBC[:, j, :], pv("dskip", j, 1), psO[:, n % 2, 0:T], MUL,
                                       ADD).then_inc(o_free[n % 2], 1)
                dve.wait_ge(o_free[n % 2], n // 2 + 1)
                V.tensor_tensor(Z[:, j, :], XBC[:, j, :], Z[:, j, :], MUL).then_inc(y_ready, 1)

            def yn(g):
                dve.wait_ge(rs_ready, 2 + g)
                dve.wait_ge(y_ready, 4 * g + 4)
                for j in range(4 * g, 4 * g + 4):
                    V.scalar_tensor_tensor(Z[:, j, :], Z[:, j, :], pv("ssd_norm_g", j, 1), RS[:, g % 2, :], MUL,
                                           MUL).then_inc(yn_ready, 1)

            for h in range(HEADS1 + 1):
                if h < HEADS1:
                    g = h // 8
                    if h % 8 == 0:
                        dve.wait_ge(cum_in[g % 2], 16 * (g // 2 + 1))
                    if h >= 2:
                        dve.wait_ge(m_ready, h - 1)
                    bc = CUMB[:, g % 2, (h % 8) * T:(h % 8 + 1) * T]
                    st.mark(V.tensor_scalar(SE[:, h % 2, 0:256], bc, CD[:, 0, h:h + 1], 0.0, SUB, ALU.min))
                    st.link(V.tensor_scalar(SE[:, h % 2, 256:384], bc[:, P:T], CD[:, 1, h:h + 1], 0.0, SUB, ALU.min))
                    dve.sem_inc(diff_ready, 1)
                if h >= 1:
                    n = h - 1
                    g = n // 8
                    dve.wait_ge(decay_ready, n + 1)
                    if n >= 2:
                        dve.wait_ge(m_used, n - 1)
                    st.mark(V.scalar_tensor_tensor(SM[:, n % 2, 0:256], SE[:, n % 2, 0:256], CD[:, 2, n:n + 1],
                                                   SCM[:, g, 0:256], MUL, MUL))
                    st.link(V.scalar_tensor_tensor(SM[:, n % 2, 256:384], SE[:, n % 2, 256:384], CD[:, 3, n:n + 1],
                                                   SCM[:, g, 256:384], MUL, MUL))
                    dve.sem_inc(m_ready, 1)
                if h >= 4 and h % 2 == 0:
                    y_out(h // 2 - 2)
            y_out(15)
            for g in range(NGRP):
                yn(g)

            u0 = PLAN.at["ssd_out"][1]
            dve.wait_ge(gates_ready, 1)
            for m in range(8):
                u = u0 + m
                V.tensor_tensor(MIXIN[:, m, :], G1[:, m, :], lin(u), MUL).then_inc(lin_free[u % 4], 1)
                dve.wait_ge(lin_free[u % 4], u // 4 + 1)
            u0 = PLAN.at["sc_out"][1]
            for m in range(8):
                u = u0 + m
                V.tensor_tensor(CT[:, m % 2, :], G1[:, 8 + m, :], lin(u), MUL).then_inc(lin_free[u % 4], 1)
                dve.wait_ge(lin_free[u % 4], u // 4 + 1)
                V.tensor_tensor(MIXIN[:, m, :], MIXIN[:, m, :], CT[:, m % 2, :], ADD).then_inc(mixin_ready, 1)

            def add_normed(src, gains, rs):
                for j in range(KD):
                    st.link(V.scalar_tensor_tensor(CT[:, j % 2, :], src[:, j, :], gains[:, j:j + 1], rs, MUL, MUL))
                    V.tensor_tensor(X[:, j, :], X[:, j, :], CT[:, j % 2, :], ADD).then_inc(x_ready, 1)

            dve.wait_ge(mixin_ready, 8)
            dve.wait_ge(rs_ready, 6)
            add_normed(MIX, lead[:, 8:16], RS[:, 0, :])
            dve.wait_ge(x_ready, 8)
            dve.wait_ge(rs_ready, 7)
            make_h(mod[:, 24:32], lead[:, 16:24], RS[:, 1, :])

            def ffn(name, wname, base, between):
                u0 = PLAN.at[name][1]
                w0 = PAR[wname][0]

                def conv(j, slot, it=0):
                    us = [u0 + 2 * j, u0 + 2 * j + 1]
                    for back in (1, 2):
                        for b in range(2):
                            if back == 1:
                                dve.wait_ge(f_begun, 2 * base + 2 * j + b + 1 + it * 2)
                            dst = CT[:, 2 * slot + b, back:T]
                            ins = V.scalar_tensor_tensor(
                                dst, psL[:, us[b] % 4, 0:T - back],
                                par[:, bass.ds(w0 + (2 - back) * 44 + b * KF + j + it, 1)], dst, MUL, ADD)
                            if back == 1:
                                st.mark(ins)
                            else:
                                ins.then_inc(lin_free[us[b] % 4], 1)
                        if back == 1:
                            dve.wait_ge(dve_step, st.loop + st.n)
                    for b in range(2):
                        dve.wait_ge(lin_free[us[b] % 4], us[b] // 4 + 1 + (it_half if it is not 0 else 0))
                    dve.sem_inc(f_conv, 1)

                def product(j, slot, it=0):
                    dve.wait_ge(f_silu, base + j + 1 + it)
                    V.tensor_tensor(FA[:, bass.ds(j + it, 1), :].rearrange("p a b -> p (a b)"), CT[:, 2 * slot, :],
                                    CT[:, 2 * slot + 1, :], MUL).then_inc(f_act, 1)

                it_half = 0
                conv(0, 0)
                conv(1, 1)
                product(0, 0)
                if between:
                    rounds = 4
                    with st.repeat(rounds, 8) as i:
                        for q in range(2):
                            it_half = i * 2
                            conv(2 + 2 * q, 0, i * 4)
                            product(1 + 2 * q, 1, i * 4)
                            between(i, 2 * q)
                            conv(3 + 2 * q, 1, i * 4)
                            product(2 + 2 * q, 0, i * 4)
                            between(i, 2 * q + 1)
                    for j in range(18, 22):
                        conv(j, j % 2)
                        product(j - 1, (j - 1) % 2)
                else:
                    with st.repeat(10, 4) as i:
                        it_half = i
                        conv(2, 0, i * 2)
                        product(1, 1, i * 2)
                        conv(3, 1, i * 2)
                        product(2, 0, i * 2)
                product(21, 1)

            V.memset(acc[:, :], 0.0).then_inc(ada_used, 8)
            dve.wait_ge(ada_used, 16 + 48)

            def ada_between(i, q):
                for s in range(3):
                    n = 3 * q + s
                    ada_step(48 + n, n % 6, csil[:, bass.ds(i * 2 + (8 + n // 6), 1)], 16, 6, i, 12)

            ffn("up1", "fconv_w", 0, ada_between)
            dve.wait_ge(rs_ready, 8)
            dve.wait_ge(f_act, KF)
            add_normed(FO, lead[:, 24:32], RS[:, 0, :])

            ps, free = scratch_wait("mod_2")
            V.tensor_tensor(mod[:, :], ps[:, 0:48], pv("b_ada_2"), ADD).then_inc(free, 1)
            dve.wait_ge(free, SCRATCH["mod_2"] // 2 + 1)
            st.mark(V.scalar_tensor_tensor(lead[:, 0:8], mod[:, 8:16], 1.0, pv("attn_norm_2"), ADD, MUL))
            st.link(V.scalar_tensor_tensor(lead[:, 8:16], mod[:, 32:40], 1.0, pv("ffn_norm_2"), ADD, MUL))
            dve.wait_ge(x_ready, 16)
            dve.wait_ge(rs_ready, 9)
            make_h(mod[:, 0:8], lead[:, 0:8], RS[:, 1, :])
            u0 = PLAN.at["tok2"][1]
            for c in range(6):
                for t in range(2):
                    u = u0 + 2 * c + t
                    dve.wait_ge(tok_sq, 4 * c + 2 * t + 2)
                    gain = pv("q_gain" if c < 4 else "ks_gain" if c == 4 else "kw_gain")
                    dst = QTOK[:, t, c * 256:(c + 1) * 256] if c < 4 else KTOK[:, t, (c - 4) * 256:(c - 3) * 256]
                    V.tensor_tensor(dst.rearrange("p (h d) -> p h d", d=HD),
                                    psL[:, u % 4, 0:256].rearrange("p (h d) -> p h d", d=HD),
                                    gain.unsqueeze(1).to_broadcast([P, 2, HD]), MUL).then_inc(lin_free[u % 4], 1)
                    dve.wait_ge(lin_free[u % 4], u // 4 + 1)
            dve.wait_ge(tok_ready, 1)
            dve.wait_ge(trs, 1)
            for t in range(2):
                st.mark(V.tensor_scalar(sm[:, t * 12:t * 12 + 8], sm[:, t * 12:t * 12 + 8], float(HD) ** -0.5, None, MUL))
            dve.wait_ge(dve_step, st.n)

            def rope(buf, heads, width, cos, sin):
                half = width // 2
                tmp = SQ[:, 0:heads * width].rearrange("p (h d) -> p h d", d=width)
                st.mark(V.tensor_tensor(tmp[:, :, 0:half], buf[:, :, half:width],
                                        sin[:, 0:half].unsqueeze(1).to_broadcast([P, heads, half]), MUL))
                st.link(V.tensor_tensor(tmp[:, :, half:width], buf[:, :, 0:half],
                                        sin[:, half:width].unsqueeze(1).to_broadcast([P, heads, half]), MUL))
                st.link(V.tensor_tensor(buf, buf, cos.unsqueeze(1).to_broadcast([P, heads, width]), MUL))
                return V.tensor_tensor(buf, buf, tmp, ADD)

            def heads_of(ap, d):
                return ap.rearrange("p (h d) -> p h d", d=d)

            dve.wait_ge(s_done, SCRATCH["stat_ckv"] + 1)
            dve.wait_ge(feat_ready, 1)
            dve.wait_ge(rs_ready, 11)
            for j in range(3):
                V.scalar_tensor_tensor(CQ[:, j, :], CQ[:, j, :], pv("cq_g", j, 1), RS[:, 0, :], MUL, MUL).then_inc(cqn_ready, 1)
            for j in range(2):
                V.scalar_tensor_tensor(CKV[:, j, :], CKV[:, j, :], pv("ckv_g", j, 1), RS[:, 1, :], MUL, MUL).then_inc(cqn_ready, 1)

            for t in range(2):
                cos, sin = pv("cos", t * HD, HD), pv("sin", t * HD, HD)
                q3 = heads_of(QTOK[:, t, :], HD)
                st.link(V.tensor_tensor(q3, q3, sm[:, t * 12:t * 12 + 8].unsqueeze(2).to_broadcast([P, 8, HD]), MUL))
                rope(q3, 8, HD, cos, sin).then_inc(troped, 1)
                dve.wait_ge(troped, 2 * t + 1)
                k3 = heads_of(KTOK[:, t, :], HD)
                st.link(V.tensor_tensor(k3[:, 0:4, :], k3[:, 0:4, :],
                                        sm[:, t * 12 + 8:t * 12 + 12].unsqueeze(2).to_broadcast([P, 4, HD]), MUL))
                rope(k3, 6, HD, cos, sin).then_inc(troped, 1)
                dve.wait_ge(troped, 2 * t + 2)

            for kv in range(2):
                if kv == 0:
                    dve.wait_ge(turned, 7)
                for g in range(2):
                    src = KT[:, 4 + g, :] if kv == 0 else VC[:, g, :]
                    pe_cols = "k_pe" if kv == 0 else "v_pe"
                    for part in range(2):
                        dst = CB[kv][:, 16 * part:16 * part + 16, g * NCMP:(g + 1) * NCMP]
                        win = src[:, 16 * part:16 * part + 240].rearrange("p (n l) -> p l n", l=16)
                        ins = V.tensor_tensor(dst, win, pv(pe_cols, 16 * part, 16).unsqueeze(2).to_broadcast([P, 16, NCMP]), ADD)
                        st.mark(ins)
                dve.wait_ge(dve_step, st.n)
                dve.sem_inc(cb_ready, 1)

            dve.wait_ge(mla_tok, 1)
            dve.wait_ge(ng_ready, 1)
            for t in range(2):
                q3 = heads_of(QB[:, t, :], QK)
                sq3 = heads_of(SQ[:, 0:1536], QK)
                st.link(V.tensor_tensor(sq3, q3, q3, MUL))
                st.link(V.tensor_reduce(mlars[:, 16 * t:16 * t + 8], sq3, AX.X, ADD))
                k3 = heads_of(KB[:, t, :], QK)
                sk3 = heads_of(SQ[:, 0:1024], HD)
                st.link(V.tensor_tensor(sk3, k3[:, :, 0:HD], k3[:, :, 0:HD], MUL))
                st.link(V.tensor_reduce(mlars[:, 16 * t + 8:16 * t + 16], sk3, AX.X, ADD))
                st.link(V.tensor_scalar(mlars[:, 16 * t + 8:16 * t + 16], mlars[:, 16 * t + 8:16 * t + 16],
                                        sm[:, 24 + t:25 + t], None, ADD))
            dve.sem_inc(tsum, 1)
            dve.wait_ge(mla_sq, 1)
            st.mark(V.tensor_scalar(mlars[:, 0:8], mlars[:, 0:8], float(QK) ** -0.5, None, MUL))
            st.link(V.tensor_scalar(mlars[:, 16:24], mlars[:, 16:24], float(QK) ** -0.5, None, MUL))
            for t in range(2):
                cos, sin = pv("mcos", t * ROPE, ROPE), pv("msin", t * ROPE, ROPE)
                q3 = heads_of(QB[:, t, :], QK)
                st.link(V.tensor_tensor(q3, q3, pv("mq_gain").unsqueeze(1).to_broadcast([P, 8, QK]), MUL))
                st.link(V.tensor_tensor(q3, q3, mlars[:, 16 * t:16 * t + 8].unsqueeze(2).to_broadcast([P, 8, QK]), MUL))
                st.link(rope(q3[:, :, HD:QK], 8, ROPE, cos, sin))
                dve.sem_inc(troped, 1)
                k3 = heads_of(KB[:, t, :], QK)
                st.link(V.tensor_tensor(k3[:, :, 0:HD], k3[:, :, 0:HD],
                                        pv("mk_gain", 0, HD).unsqueeze(1).to_broadcast([P, 8, HD]), MUL))
                kr = KR[:, t, :].unsqueeze(1)
                st.link(V.tensor_tensor(KR[:, t, :], KR[:, t, :], pv("mk_gain", HD, ROPE), MUL))
                st.link(rope(kr, 1, ROPE, cos, sin))
                st.link(V.tensor_copy(k3[:, :, HD:QK], kr.to_broadcast([P, 8, ROPE])))
                st.link(V.tensor_tensor(k3, k3, mlars[:, 16 * t + 8:16 * t + 16].unsqueeze(2).to_broadcast([P, 8, QK]), MUL))
                dve.sem_inc(troped, 1)

            ps, free = scratch_wait("kc")
            dve.wait_ge(kc_rs, 1)
            V.scalar_tensor_tensor(KCN, ps[0:30, 0:P], sm[0:30, 60:61], pv("kc_gain")[0:30, :], MUL, MUL).then_inc(free, 1)
            dve.wait_ge(free, SCRATCH["kc"] // 2 + 1)
            dve.sem_inc(kcn_ready, 1)
            u = PLAN.at["cmp_scores"][1]
            dve.wait_ge(lin_done, u + 1)
            cs4 = CS.rearrange("p (h t n) -> p h t n", t=2, n=NCMP)
            cs3 = CS.rearrange("p (m n) -> p m n", n=NCMP)
            V.tensor_tensor(cs4, psL[:, u % 4, 0:240].rearrange("p (h t n) -> p h t n", t=2, n=NCMP),
                            pv("cmask_add").rearrange("p (t n) -> p t n", n=NCMP).unsqueeze(1).to_broadcast([P, 8, 2, NCMP]),
                            ADD).then_inc(lin_free[u % 4], 1)
            dve.wait_ge(lin_free[u % 4], u // 4 + 1)
            st.link(V.tensor_reduce(cmx[:, 0:16], cs3, AX.X, ALU.max))
            st.link(V.tensor_tensor(cs3, cs3, cmx[:, 0:16].unsqueeze(2).to_broadcast([P, 16, NCMP]), SUB))
            dve.sem_inc(cs_ready, 1)
            dve.wait_ge(ce_ready, 1)
            st.link(V.tensor_reduce(cmx[:, 0:16], cs3, AX.X, ADD))
            st.link(V.reciprocal(cmx[:, 16:32], cmx[:, 0:16]))
            gate0 = GT[:, :, :].rearrange("p t (h b) -> p h t b", b=3)[:, :, :, 0]
            st.link(V.tensor_tensor(cmx[:, 0:16].rearrange("p (h t) -> p h t", t=2),
                                    cmx[:, 16:32].rearrange("p (h t) -> p h t", t=2), gate0, MUL))
            st.link(V.tensor_tensor(cs3, cs3, cmx[:, 0:16].unsqueeze(2).to_broadcast([P, 16, NCMP]), MUL))
            st.link(V.tensor_tensor(cs4, cs4,
                                    pv("cmask01").rearrange("p (t n) -> p t n", n=NCMP).unsqueeze(1).to_broadcast([P, 8, 2, NCMP]),
                                    MUL))
            dve.sem_inc(cp_ready, 1)

            def softmax(count, p0, gated, outs):
                for i in range(count + 1):
                    if i < count:
                        n = p0 + i
                        u = PLAN.at["nsa_scores"][1] + n
                        dve.wait_ge(lin_done, u + 1)
                        b = 26 + 4 * (n % 2)
                        st.mark(V.tensor_reduce(sm[:, b:b + 1], psL[:, u % 4, 0:P], AX.X, ALU.max, negate=True))
                        st.link(V.tensor_reduce(sm[:, b + 1:b + 2], psL[:, u % 4, P:384], AX.X, ALU.max, negate=True))
                        dve.sem_inc(max_ready, 1)
                    if i >= 1:
                        n = p0 + i - 1
                        b = 28 + 4 * (n % 2)
                        rc = cmx[:, 32 + 2 * (n % 2):34 + 2 * (n % 2)]
                        dve.wait_ge(exp_ready, n + 1)
                        st.link(V.reciprocal(rc, sm[:, b:b + 2]))
                        if gated:
                            h, br = divmod(n, 2)
                            st.link(V.tensor_tensor(rc, rc, GT[:, :, 3 * h + 1 + br], MUL))
                        st.mark(V.tensor_scalar(PR[:, n % 2, 0:P], PR[:, n % 2, 0:P], rc[:, 0:1], None, MUL))
                        st.link(V.tensor_scalar(PR[:, n % 2, P:384], PR[:, n % 2, P:384], rc[:, 1:2], None, MUL))
                        dve.sem_inc(p_ready, 1)
                    outs(i)

            def nsa_outs(i):
                if i >= 3 and i % 2 == 1 or i == 16:
                    h = (i - 3) // 2 if i < 16 else 7
                    n = OUT_NSA + h
                    dve.wait_ge(pt_used, 2 * h + 2)
                    V.tensor_tensor(OM[:, h, :], G2[:, h, :], psO[:, n % 2, 0:T], MUL).then_inc(o_free[n % 2], 1)

            def mla_outs(i):
                hs = [i - 2] if i < 8 else [6, 7]
                for h in hs:
                    if h < 0:
                        continue
                    n = OUT_MLA + h
                    dve.wait_ge(pt_used, 16 + h + 1)
                    V.tensor_tensor(CT[:, h % 2, :], G2[:, 8 + h, :], psO[:, n % 2, 0:T], MUL).then_inc(o_free[n % 2], 1)
                    dve.wait_ge(o_free[n % 2], n // 2 + 1)
                    V.tensor_tensor(OM[:, h, :], OM[:, h, :], CT[:, h % 2, :], ADD).then_inc(om_ready, 1)

            dve.wait_ge(gates_ready, 2)
            softmax(16, 0, True, nsa_outs)
            for n in (OUT_NSA + 6, OUT_NSA + 7):
                dve.wait_ge(o_free[n % 2], n // 2 + 1)
            dve.sem_inc(om_ready, 8)
            softmax(8, 16, False, mla_outs)

            def add_gated(name, gates):
                u0 = PLAN.at[name][1]
                for m in range(8):
                    u = u0 + m
                    V.scalar_tensor_tensor(X[:, m, :], lin(u), gates[:, m:m + 1], X[:, m, :], MUL, ADD
                                           ).then_inc(lin_free[u % 4], 1)
                    dve.wait_ge(lin_free[u % 4], u // 4 + 1)
                    dve.sem_inc(x_ready, 1)

            add_gated("o2", mod[:, 16:24])
            dve.wait_ge(rs_ready, 12)
            make_h(mod[:, 24:32], lead[:, 8:16], RS[:, 0, :])
            ffn("up2", "fconv_w_2", KF, None)
            add_gated("down2", mod[:, 40:48])


def _pack(w):
    k, n = w.shape
    return w.reshape(k // P, P, n).transpose(1, 0, 2).reshape(P, -1)


def _cols(v):
    return v.reshape(-1, P).T


def _swap(a):
    return np.concatenate([a[..., FF:], a[..., :FF]], axis=-1)


def _weights(i):
    chunks = []

    def m_blocks(w, per):
        for c in range(w.shape[1] // (P * per)):
            chunks.append(np.concatenate([_pack(w[:, (c * per + b) * P:(c * per + b + 1) * P]) for b in range(per)], axis=1))

    def up(w):
        for j in range(KF):
            chunks.append(np.concatenate([_pack(w[:, j * P:(j + 1) * P]), _pack(w[:, FF + j * P:FF + (j + 1) * P])], axis=1))

    def down(w):
        for m in range(KD):
            for half in range(2):
                chunks.append(_pack(w[half * 11 * P:(half + 1) * 11 * P, m * P:(m + 1) * P]))

    w = i["w_in"][0]
    m_blocks(np.concatenate([w[:, 2048:5120], w[:, 0:2048], w[:, 6176:7200], w[:, 7200:8224], w[:, 5152:6176],
                             w[:, 8224:10272]], axis=1), 2)
    m_blocks(i["w_ssd_out"][0], 1)
    m_blocks(i["w_sc_out"][0], 2)
    m_blocks(i["w_o"][0], 2)
    up(i["w_up"][0])
    down(i["w_down"][0])
    w = i["w_in_2"][0]
    q, kc, vc, ks, vs, kw, vw = (w[:, 0:1024],) + tuple(w[:, 1024 + 256 * n:1280 + 256 * n] for n in range(6))
    ng, cq, ckv, kr, bg = w[:, 2560:2584], w[:, 2584:2968], w[:, 2968:3224], w[:, 3224:3288], w[:, 3288:5336]
    tok = np.concatenate([q, ks, kw, kc, vs, vw], axis=1)
    for c in range(9):
        chunks.append(_pack(tok[:, c * 256:(c + 1) * 256]))
    chunks.append(np.concatenate([_pack(np.concatenate([kr, ng], axis=1)), _pack(vc[:, 0:P])], axis=1))
    m_blocks(np.concatenate([vc[:, P:], cq, ckv, bg], axis=1), 2)
    for c in range(3):
        chunks.append(_pack(i["w_uq_2"][0][:, c * 512:(c + 1) * 512]))
    for c in range(2):
        chunks.append(np.concatenate([_pack(i["w_ukv_2"][0][:, (2 * c + n) * 512:(2 * c + n + 1) * 512]) for n in range(2)], axis=1))
    for name in ("cmp_k_w1_2", "cmp_v_w1_2"):
        for half in range(2):
            for part in range(2):
                chunks.append(_pack(i[name][0][part * 16 * P:(part + 1) * 16 * P, half * P:(half + 1) * P]))
    m_blocks(i["w_o_2"][0], 2)
    up(_swap(i["w_up_2"][0]))
    down(i["w_down_2"][0])
    assert len(chunks) == CHUNKS and all(c.shape[1] == n for c, n in zip(chunks, PLAN.cols))
    out = np.zeros((CHUNKS, P, SLOT), np.float32)
    for c, a in enumerate(chunks):
        out[c, :, :a.shape[1]] = a
    return out.reshape(CHUNKS * P, SLOT)


def _ada(i):
    a, b = (w.reshape(KD, P, ADA_GROUPS, ADA_COLS).transpose(0, 2, 1, 3) for w in (i["ada_w"][0], i["w_ada_2"][0]))
    return np.concatenate([a[:, :2].reshape(-1, ADA_COLS), a[:, 2:].reshape(-1, ADA_COLS), b.reshape(-1, ADA_COLS)])


def _rope(width):
    half = width // 2
    inv = (10000.0 ** (-np.arange(half, dtype=np.float32) * np.float32(2.0) / width)).astype(np.float32)
    ang = (np.arange(T, dtype=np.float32)[:, None] * inv[None, :]).astype(np.float32)
    cos, sin = np.cos(ang), np.sin(ang)
    tile = lambda a: a.reshape(2, P, width).transpose(1, 0, 2).reshape(P, -1).astype(np.float32)
    return tile(np.concatenate([cos, cos], axis=1)), tile(np.concatenate([-sin, sin], axis=1))


def _params(i):
    def rows(v):
        out = np.zeros((P, 1), np.float32)
        out[:len(v), 0] = v
        return out

    def taps(w):
        return np.concatenate([_cols(row) for row in w], axis=1)

    def wide(v):
        return np.broadcast_to(v, (P, len(v)))

    q, k = np.arange(P)[:, None], np.arange(P)[None, :]
    ends = 16 * np.arange(NCMP) + 31
    seen = (ends[None, None, :] <= (np.arange(2)[None, :, None] * P + np.arange(P)[:, None, None])).reshape(P, -1)
    cos, sin = _rope(HD)
    mcos, msin = _rope(ROPE)
    f = lambda a: a.astype(np.float32)
    v = {
        "c": _cols(i["c"][0]), "c_2": _cols(i["c_2"][0]), "ada_b": _cols(i["ada_b"][0]),
        "mix_pre_g": _cols(i["mix_pre_g"][0]), "mix_post_g": _cols(i["mix_post_g"][0]),
        "xconv_w": taps(i["ssd_conv_w"][0]), "xconv_b": _cols(i["ssd_conv_b"][0]),
        "dskip": _cols(np.repeat(i["ssd_d"][0], 64)), "ssd_norm_g": _cols(i["ssd_norm_g"][0]),
        "sconv_w": taps(i["sc_conv_w"][0]), "ffn_pre_g": _cols(i["ffn_pre_g"][0]), "ffn_post_g": _cols(i["ffn_post_g"][0]),
        "fconv_w": taps(i["ffn_conv_w"][0]), "fconv_b": _cols(i["ffn_conv_b"][0]),
        "dt_bias": rows(i["ssd_dt_bias"][0]), "a_log": rows(i["ssd_a_log"][0]), "w_dt": _pack(i["w_in"][0][:, 5120:5152]),
        "b_ada_2": _cols(i["b_ada_2"][0]), "attn_norm_2": _cols(i["attn_norm_2"][0]), "ffn_norm_2": _cols(i["ffn_norm_2"][0]),
        "fconv_w_2": taps(_swap(i["w_conv_2"][0])), "fconv_b_2": _cols(_swap(i["b_conv_2"][0])),
        "k_pe": i["cmp_k_pe_2"][0].T, "v_pe": i["cmp_v_pe_2"][0].T,
        "k_w2": _pack(i["cmp_k_w2_2"][0]), "v_w2": _pack(i["cmp_v_w2_2"][0]),
        "cq_g": _cols(i["mla_cq_norm_2"][0]), "ckv_g": _cols(i["mla_ckv_norm_2"][0]),
        "q_gain": wide(i["nsa_q_norm_2"][0]), "ks_gain": wide(i["nsa_ks_norm_2"][0]), "kw_gain": wide(i["nsa_kw_norm_2"][0]),
        "kc_gain": wide(i["nsa_kc_norm_2"][0]), "mq_gain": wide(i["mla_q_norm_2"][0]), "mk_gain": wide(i["mla_k_norm_2"][0]),
        "ident": np.eye(P, dtype=np.float32), "ones": np.ones((P, P), np.float32),
        "causal_add": f(np.where(k <= q, 0.0, -1e30)), "causal01": f(k >= q),
        "cos": cos, "sin": sin, "mcos": mcos, "msin": msin,
        "cmask_add": f(np.where(seen, 0.0, -1e30)), "cmask01": f(seen),
    }
    assert all(v[n].shape == (P, c) for n, c in PAR_SPEC), [(n, v[n].shape) for n, c in PAR_SPEC if v[n].shape != (P, c)]
    return np.ascontiguousarray(np.concatenate([v[n] for n, _ in PAR_SPEC], axis=1))


def kernel(**inputs):
    import concourse.bacc as bacc
    from concourse.bass_utils import run_bass_kernel_spmd

    inputs = {k: np.asarray(v) for k, v in inputs.items()}
    arrays = {
        "x_t": np.ascontiguousarray(inputs["x"][0].reshape(T, KD, P).transpose(2, 1, 0)),
        "params": _params(inputs), "ada_w": np.ascontiguousarray(_ada(inputs)), "wts": _weights(inputs),
    }
    nc = bacc.Bacc("TRN2", target_bir_lowering=False, num_devices=1)
    aps = [nc.dram_tensor(n, a.shape, mybir.dt.from_np(a.dtype), kind="ExternalInput").ap() for n, a in arrays.items()]
    out = nc.dram_tensor("out_t", (P, KD * T), mybir.dt.float32, kind="ExternalOutput").ap()
    build(nc, *aps, out)
    r = run_bass_kernel_spmd(nc, [arrays], core_ids=[0])
    y = r.results[0]["out_t"].reshape(P, KD, T).transpose(2, 1, 0).reshape(1, T, D)
    return np.ascontiguousarray(y)
```

```python
from contextlib import ExitStack, contextmanager

import concourse.bass as bass
import numpy as np
from concourse import mybir

P = 128
T = 256
D = 1024
KD = D // P
FF = 2816
KF = FF // P
EPS = 1e-6

NXBC = 24
NZ = 16
HEADS1 = 32
NGRP = 4
NH = 8
NCMP = 15
HD = 128
QK = 192
ROPE = 64

SLOTS = 4
SLOT = 8 * P
ADA_SLOTS = 4
ADA_COLS = 1024
ADA_GROUPS = 6 * D // ADA_COLS


class Stream:

    def __init__(self):
        self.cols, self.done_after, self.split_at, self.chunk_of, self.units, self.at = [], [], [], [], 0, {}

    def add(self, name, groups, cols, units=1, plain=False):
        self.at[name] = (len(self.cols), self.units)
        for _ in range(groups):
            self.units += units
            for n in cols:
                if not plain:
                    self.chunk_of.append(len(self.cols))
                self.split_at.append(None if plain else len(self.chunk_of) - 1)
                self.cols.append(n)
                self.done_after.append(self.units)

    def bare(self, name, units):
        self.at[name] = (len(self.cols), self.units)
        self.units += units

    def q(self, name):
        return self.split_at[self.at[name][0]]

    def splittable(self, q):
        if q < SLOTS:
            return 0
        before = self.chunk_of[q] - SLOTS
        return max(self.done_after[self.chunk_of[q - SLOTS]], self.done_after[before])


PLAN = Stream()
PLAN.add("in1", 80, [SLOT])
PLAN.add("ssd_out", 8, [SLOT, SLOT])
PLAN.add("sc_out", 8, [SLOT])
PLAN.add("o1", 8, [SLOT])
PLAN.add("up1", 44, [SLOT])
PLAN.add("down1", 8, [SLOT, SLOT, 6 * P])
PLAN.add("tok2", 9, [SLOT, SLOT], 2)
PLAN.add("mix2", 1, [88 * KD], 2)
PLAN.add("feat2", 23, [SLOT])
PLAN.add("uq", 8, [3 * QK], 1, True)
PLAN.add("ukv", 4, [SLOT], 2, True)
PLAN.add("cmp", 4, [SLOT] * 4, 1, True)
PLAN.bare("cmp_scores", 1)
PLAN.bare("nsa_scores", 2 * NH)
PLAN.bare("mla_scores", NH)
PLAN.add("o2", 8, [SLOT])
PLAN.add("up2", 44, [SLOT])
PLAN.add("down2", 8, [SLOT, SLOT, 6 * P])
CHUNKS, SPLITS = len(PLAN.cols), len(PLAN.chunk_of)
assert all((c - q) % SLOTS == 0 for q, c in enumerate(PLAN.chunk_of))

SCRATCH = {}
_n = 0
for _name, _count in [("stat_mix", 1), ("mod_a", 1), ("dt", 1), ("mod_b", 1), ("dt_turn", 1), ("x_turn", 8),
                      ("scores", 4), ("gnorm", 4), ("stat_o1", 1), ("stat_ffn1", 1), ("stat_down1", 1),
                      ("mod_2", 1), ("stat_attn", 1), ("stat_cq", 1), ("stat_ckv", 1), ("nsa_turn", 7),
                      ("kc", 1), ("kc_turn", 1), ("vc", 1), ("cmp_turn", 4), ("nsa_p", 16),
                      ("mla_turn", 16), ("mla_p", 8), ("stat_ffn2", 1)]:
    SCRATCH[_name] = _n
    _n += _count

OUT_Y, OUT_NSA, OUT_MLA = 0, 16, 24

PAR_SPEC = [
    ("c", 8), ("c_2", 8), ("ada_b", 48), ("mix_pre_g", 8), ("mix_post_g", 8),
    ("xconv_w", 4 * NXBC), ("xconv_b", NXBC), ("dskip", 16), ("ssd_norm_g", 16), ("sconv_w", 24),
    ("ffn_pre_g", 8), ("ffn_post_g", 8), ("fconv_w", 132), ("fconv_b", 44),
    ("dt_bias", 1), ("a_log", 1), ("w_dt", KD * HEADS1),
    ("b_ada_2", 48), ("attn_norm_2", 8), ("ffn_norm_2", 8), ("fconv_w_2", 132), ("fconv_b_2", 44),
    ("k_pe", 32), ("v_pe", 32), ("k_w2", 256), ("v_w2", 256), ("cq_g", 3), ("ckv_g", 2),
    ("q_gain", 128), ("ks_gain", 128), ("kw_gain", 128), ("kc_gain", 128), ("mq_gain", QK), ("mk_gain", QK),
    ("ident", P), ("ones", P), ("causal_add", P), ("causal01", P),
    ("cos", 2 * 128), ("sin", 2 * 128), ("mcos", 2 * 64), ("msin", 2 * 64),
    ("cmask_add", 2 * NCMP), ("cmask01", 2 * NCMP),
]
PAR = {}
_n = 0
for _name, _count in PAR_SPEC:
    PAR[_name] = (_n, _count)
    _n += _count
NPAR = _n


def build(nc, x_t, par_in, ada_w, wts, out_t):
    F32, F32R, BF16 = mybir.dt.float32, mybir.dt.float32r, mybir.dt.bfloat16
    ALU, ACT, AX = mybir.AluOpType, mybir.ActivationFunctionType, mybir.AxisListType
    MUL, ADD, SUB = ALU.mult, ALU.add, ALU.subtract
    ctx = ExitStack()
    with ctx:
        def sb(name, shape, dt=F32):
            return ctx.enter_context(nc.sbuf_tensor(name, shape, dt))

        def sem(name):
            return ctx.enter_context(nc.semaphore(name))

        ring = sb("ring", [P, SLOTS, SLOT])
        WH = sb("WH", [P, SLOTS, SLOT], F32R)
        WL = sb("WL", [P, SLOTS, SLOT], F32R)
        adaring = sb("adaring", [P, ADA_SLOTS * ADA_COLS])
        par = sb("par", [P, NPAR])
        X = sb("X", [P, KD, T])
        SQ = sb("SQ", [P, 2048])
        with nc.sbuf_tensor("HR", [P, 4096], F32R) as HR:
            pass
        HX = sb("HX", [P, 4096])
        with nc.sbuf_tensor("RR", [P, 22528], F32R) as RR:
            pass
        R = sb("R", [P, 22528])
        CT = sb("CT", [P, 4, T])
        RS = sb("RS", [P, 2, T])
        mod = sb("mod", [P, 48])
        lead = sb("lead", [P, 32])
        csil = sb("csil", [P, 16])
        CD = sb("CD", [P, 4, 32])
        sm = sb("sm", [P, 96])
        GT = sb("GT", [P, 2, 24])
        eps_col = sb("eps_col", [P, 1])
        mlars = sb("mlars", [P, 32])
        cmx = sb("cmx", [P, 36])
        kct = sb("kct", [P, 30])
        identb = sb("identb", [P, P], BF16)
        maskb = sb("maskb", [P, P], BF16)
        psL = ctx.enter_context(nc.psum_tensor("psL", [P, 4, 512], F32))
        psS = ctx.enter_context(nc.psum_tensor("psS", [P, 2, 512], F32))
        psO = ctx.enter_context(nc.psum_tensor("psO", [P, 2, 512], F32))
        cum_dram = nc.dram_tensor("cum_dram", (HEADS1, T), F32, kind="Internal").ap()

        def pv(name, lo=0, n=None):
            at, cols = PAR[name]
            return par[:, at + lo:at + (cols if n is None else lo + n)]

        def region(buf, lo, **dims):
            a, b = dims["a"], dims["b"]
            return buf[:, lo:lo + a * b].rearrange("p (a b) -> p a b", b=b)

        HH, HL = region(HR, 0, a=8, b=T), region(HR, 2048, a=8, b=T)
        Z = region(R, 0, a=NZ, b=T)
        XBC = region(R, 4096, a=NXBC, b=T)
        G1 = region(R, 10240, a=16, b=T)
        SCQ = region(R, 14336, a=8, b=T)
        YSC = region(R, 16384, a=8, b=T)
        XTOK = region(R, 18432, a=2, b=2048)
        ACC1 = R[:, 18432:22528]
        WDT = region(RR, 14336, a=2, b=KD * HEADS1)
        CUMB = region(R, 14336, a=2, b=1024)
        SE = region(R, 8192, a=2, b=768)
        SM = region(adaring, 0, a=2, b=768)
        dts = SQ[0:32, 0:1536].rearrange("p (a b) -> p a b", b=T)
        SCM = region(SQ, 0, a=4, b=384)
        ZH, ZL = region(RR, 4096, a=16, b=T), region(RR, 18432, a=16, b=T)
        YH, YL = region(RR, 14336, a=8, b=T), region(RR, 8192, a=8, b=T)
        MIXIN = region(R, 0, a=8, b=T)
        MH, ML = region(RR, 2048, a=8, b=T), region(RR, 16384, a=8, b=T)
        MIX = region(R, 4096, a=8, b=T)
        FAH, FAL = region(RR, 0, a=KF, b=T), region(RR, KF * T, a=KF, b=T)
        FO = region(R, 12288, a=8, b=T)
        ACC2 = R[:, 14336:20480]
        QTOK = region(R, 0, a=2, b=1024)
        KTOK = region(R, 2048, a=2, b=768)
        VTOK = region(R, 3584, a=2, b=512)
        KR = region(R, 4608, a=2, b=64)
        VC = region(R, 4864, a=2, b=T)
        CQ = region(R, 5376, a=3, b=T)
        CKV = region(R, 6144, a=2, b=T)
        G2 = region(R, 6656, a=16, b=T)
        QT = region(R, 10752, a=8, b=T)
        KT = region(R, 12800, a=6, b=T)
        QB = region(R, 14336, a=2, b=1536)
        KB = region(R, 17408, a=2, b=1536)
        VB = region(R, 20480, a=2, b=1024)
        OM = region(HX, 0, a=8, b=T)
        CB = [region(HX, 2048, a=32, b=30), region(HX, 3072, a=32, b=30)]
        PR = region(SQ, 0, a=3, b=384)
        HID = region(SQ, 1536, a=4, b=30)
        VCMP = SQ[0:NCMP, 1664:1920].rearrange("p (a b) -> p a b", b=P)
        KCD = SQ[0:30, 1920:2048]
        PT = region(R, 4608, a=2, b=384)
        KCT = kct[:, :]
        CS = RS[:, 0, 0:240]
        KCN = RS[0:30, 1, 0:P]
        PTC = region(R, 0, a=8, b=T)
        MQN = region(R, 0, a=8, b=T)
        MQR = region(R, 2048, a=8, b=T)
        MKR = region(R, 6656, a=8, b=T)
        MKN = region(R, 10752, a=8, b=T)
        OMH, OML = region(RR, 0, a=8, b=T), region(RR, 2048, a=8, b=T)

        par_in_sem, x_in = sem("par_in"), sem("x_in")
        w_arrived = [sem(f"w_arrived{i}") for i in range(SLOTS)]
        ada_arrived = [sem(f"ada_arrived{i}") for i in range(ADA_SLOTS)]
        ada_used = sem("ada_used")
        acc_cleared = sem("acc_cleared")
        hi_done = sem("hi_done")
        lo_done = sem("lo_done")
        lin_done = sem("lin_done")
        lin_free = [sem(f"lin_free{i}") for i in range(4)]
        s_done = sem("s_done")
        s_free = [sem(f"s_free{i}") for i in range(2)]
        o_done = sem("o_done")
        o_free = [sem(f"o_free{i}") for i in range(2)]
        act_step, dve_step, pool_step = sem("act_step"), sem("dve_step"), sem("pool_step")
        consts_ready = sem("consts_ready")
        csil_ready = sem("csil_ready")
        sq_ready = sem("sq_ready")
        rs_ready = sem("rs_ready")
        h_ready = sem("h_ready")
        dtx_ready, dtw_ready, dtl_ready, dt_ready = sem("dtx"), sem("dtw"), sem("dtl"), sem("dt_ready")
        cum_stored, cum_in = sem("cum_stored"), [sem("cum_in0"), sem("cum_in1")]
        conv_begun, conv_done, xbc_ready = sem("conv_begun"), sem("conv_done"), sem("xbc_ready")
        z_ready, sc_c_ready, ysc_ready, gates_ready = sem("z_ready"), sem("sc_c_ready"), sem("ysc_ready"), sem("gates_ready")
        xtok_ready, cd_ready, scm_ready = sem("xtok_ready"), sem("cd_ready"), sem("scm_ready")
        diff_ready, decay_ready, m_ready, m_used = sem("diff"), sem("decay"), sem("m_ready"), sem("m_used")
        y_ready, yn_ready, mixin_ready, mix_ready = sem("y_ready"), sem("yn_ready"), sem("mixin_ready"), sem("mix_ready")
        x_ready = sem("x_ready")
        t_ready, hh_ready = sem("t_ready"), sem("hh_ready")
        wdt_hi, wdt_ready = sem("wdt_hi"), sem("wdt_ready")
        zh_ready, yh_ready, mh_ready, omh_ready = sem("zh_ready"), sem("yh_ready"), sem("mh_ready"), sem("omh_ready")
        zl_ready, yl_ready, ml_ready, oml_ready = sem("zl_ready"), sem("yl_ready"), sem("ml_ready"), sem("oml_ready")
        f_prod, f_hi = sem("f_prod"), sem("f_hi")
        f_begun, f_conv, f_silu, f_act = sem("f_begun"), sem("f_conv"), sem("f_silu"), sem("f_act")
        tok_sq, tok_ready, feat_ready, ng_ready = sem("tok_sq"), sem("tok_ready"), sem("feat_ready"), sem("ng_ready")
        cqn_ready, mla_tok, mla_sq = sem("cqn_ready"), sem("mla_tok"), sem("mla_sq")
        tsum, trs, troped = sem("tsum"), sem("trs"), sem("troped")
        turned = sem("turned")
        cb_ready, hid_ready, kcn_ready, vcmp_ready = sem("cb_ready"), sem("hid_ready"), sem("kcn_ready"), sem("vcmp_ready")
        kc_sum, kc_rs = sem("kc_sum"), sem("kc_rs")
        cs_ready, ce_ready, cp_ready, ptc_ready = sem("cs_ready"), sem("ce_ready"), sem("cp_ready"), sem("ptc_ready")
        max_ready, exp_ready, p_ready, p_used = sem("max_ready"), sem("exp_ready"), sem("p_ready"), sem("p_used")
        pt_ready, pt_used, om_ready = sem("pt_ready"), sem("pt_used"), sem("om_ready")
        out_sem = sem("out_stored")

        class Steps:

            def __init__(self, eng, s):
                self.eng, self.s, self.n, self.loop = eng, s, 0, 0

            def mark(self, ins):
                self.n += 1
                ins.then_inc(self.s, 1)
                return self.loop + self.n

            def link(self, ins):
                self.eng.wait_ge(self.s, self.mark(ins))

            @contextmanager
            def repeat(self, times, per):
                before = self.n
                with self.eng.Fori(0, times, 1) as i:
                    if per:
                        self.loop = i * per
                    yield i
                    assert self.n - before == per, (self.n - before, per)
                self.loop = 0
                self.n = before + per * times

        def sbank(name, i=0):
            return psS[:, (SCRATCH[name] + i) % 2, :]

        block = ctx.enter_context(nc.Block())

        @block.sync
        def _(sp):
            def load(c, i=0, per=SLOTS):
                before = c - SLOTS
                if before >= 0:
                    if PLAN.split_at[before] is None:
                        sp.wait_ge(lin_done, PLAN.done_after[before])
                    else:
                        sp.wait_ge(lo_done, PLAN.split_at[before] + 1 + i * per)
                n = PLAN.cols[c]
                sp.dma_start(ring[:, c % SLOTS, 0:n],
                             wts[bass.ds(c * P + i * (per * P), P), 0:n]).then_inc(w_arrived[c % SLOTS], 16)

            def load_ada(n, i=0, per=0):
                if n >= ADA_SLOTS:
                    sp.wait_ge(ada_used, n - ADA_SLOTS + 1 + 8 + i * per)
                k = n % ADA_SLOTS
                sp.dma_start(adaring[:, k * ADA_COLS:(k + 1) * ADA_COLS],
                             ada_w[bass.ds(n * P + i * (per * P), P), :]).then_inc(ada_arrived[k], 16)

            sp.dma_start(par[:, :], par_in).then_inc(par_in_sem, 16)
            for n in range(4):
                load_ada(n)
            sp.dma_start(X[:, :, :], x_t).then_inc(x_in, 16)
            for n in range(4, 12):
                load_ada(n)
            for c in range(SLOTS):
                load(c)
            for n in range(12, 16):
                load_ada(n)
            with sp.Fori(0, 8, 1) as i:
                for k in range(4):
                    load_ada(16 + k, i, 4)
                for k in range(4):
                    load(4 + k, i)
            up = PLAN.at["up1"][0]
            with sp.Fori(0, (up + 4 - 36) // 4, 1) as i:
                for k in range(4):
                    load(36 + k, i)
            sp.wait_ge(m_used, HEADS1 // 2)
            for n in range(48, 52):
                load_ada(n)
            for k in range(8):
                load(up + 4 + k)
            with sp.Fori(0, 3, 1) as i:
                for q in range(4):
                    for k in range(3):
                        load_ada(52 + 3 * q + k, i, 12)
                    for k in range(2):
                        load(up + 12 + 2 * q + k, i, 8)
            for q in range(3):
                for k in range(3):
                    if 88 + 3 * q + k < 96:
                        load_ada(88 + 3 * q + k)
                for k in range(2):
                    load(up + 36 + 2 * q + k)
            c = up + 42
            while c < CHUNKS:
                n = 0
                while (c + n < CHUNKS and PLAN.cols[c + n] == PLAN.cols[c]
                       and PLAN.split_at[c + n - SLOTS] is not None):
                    n += 1
                rounds = n // SLOTS
                if rounds >= 2:
                    with sp.Fori(0, rounds, 1) as i:
                        for k in range(SLOTS):
                            load(c + k, i)
                    c += rounds * SLOTS
                else:
                    load(c)
                    c += 1
            for j in range(KD):
                sp.wait_ge(x_ready, 3 * KD + j + 1)
                sp.dma_start(out_t[:, j * T:(j + 1) * T], X[:, j, :]).then_inc(out_sem, 16)
            sp.wait_ge(out_sem, 16 * KD)

        @block.gpsimd
        def _(pool):
            def low(q, i=0):
                pool.wait_ge(hi_done, q + 1 + i * SLOTS)
                n = PLAN.cols[PLAN.chunk_of[q]]
                k = q % SLOTS
                nc.gpsimd.tensor_tensor(WL[:, k, 0:n], ring[:, k, 0:n], WH[:, k, 0:n].bitcast(F32), SUB
                                        ).then_inc(lo_done, 1)

            for q in range(SLOTS):
                low(q)
            def lows(q, last):
                while q < last:
                    n = 0
                    while q + n < last and PLAN.cols[PLAN.chunk_of[q + n]] == PLAN.cols[PLAN.chunk_of[q]]:
                        n += 1
                    rounds = n // SLOTS
                    if rounds >= 2:
                        with pool.Fori(0, rounds, 1) as i:
                            for k in range(SLOTS):
                                low(q + k, i)
                        q += rounds * SLOTS
                    else:
                        low(q)
                        q += 1

            lows(SLOTS, SPLITS)

        @block.tensor
        def _(pe):
            def mm(out, lhsT, rhs, start, stop):
                return nc.tensor.matmul(out, lhsT, rhs, start=start, stop=stop)

            def chunk_wait(c, rounds=0):
                pe.wait_ge(w_arrived[c % SLOTS], 16 * (c // SLOTS + 1) + 16 * rounds)

            def split_wait(q, rounds=0):
                pe.wait_ge(lo_done, q + 1 + SLOTS * rounds)

            def bank_wait(u, rounds=0):
                if u >= 4:
                    pe.wait_ge(lin_free[u % 4], u // 4 + rounds)

            def scratch(name, i=0):
                n = SCRATCH[name] + i
                if n >= 2:
                    pe.wait_ge(s_free[n % 2], n // 2)
                return psS[:, n % 2, :]

            def obank(n):
                if n >= 2:
                    pe.wait_ge(o_free[n % 2], n // 2)
                return psO[:, n % 2, :]

            def triple(out, wh, wl, hi, lo, first, last):
                mm(out, wh, hi, first, False)
                mm(out, wh, lo, False, False)
                return mm(out, wl, hi, False, last)

            def unit(u, q, nchunks, hi, lo, rounds=0, sizes=(8, 8, 6)):
                bank_wait(u, rounds)
                kk = 0
                for c in range(nchunks):
                    split_wait(q + c, rounds)
                    s = (q + c) % SLOTS
                    for b in range(sizes[c]):
                        end = c == nchunks - 1 and b == sizes[c] - 1
                        last = triple(psL[:, u % 4, 0:T], WH[:, s, b * P:(b + 1) * P], WL[:, s, b * P:(b + 1) * P],
                                      hi(kk), lo(kk), kk == 0, end)
                        kk += 1
                last.then_inc(lin_done, 1)

            def blk(c, b):
                return ring[:, c % SLOTS, b * P:(b + 1) * P]

            def linear8(name, first, count, hi, lo):
                q0, u0 = PLAN.q(name) + first, PLAN.at[name][1] + first
                done = SLOTS if u0 == 0 else 0
                for c in range(done):
                    unit(u0 + c, q0 + c, 1, hi, lo)
                rounds = (count - done) // SLOTS
                if rounds >= 2:
                    with pe.Fori(0, rounds, 1) as i:
                        for c in range(done, done + SLOTS):
                            unit(u0 + c, q0 + c, 1, hi, lo, i)
                    done += rounds * SLOTS
                for c in range(done, count):
                    unit(u0 + c, q0 + c, 1, hi, lo)

            def stat(name, squares, n, i=0):
                out = scratch(name, i)
                for k in range(n):
                    last = mm(out[:, 0:T], pv("ones"), squares(k), k == 0, k == n - 1)
                last.then_inc(s_done, 1)

            def mod_columns(name, acc, lo, hi):
                out = scratch(name)
                for j in range(lo, hi):
                    last = mm(out[:, j - lo:j - lo + 1], acc[:, (j - lo) * P:(j - lo + 1) * P], pv("ones", 0, 1), True, True)
                last.then_inc(s_done, 1)

            def sq_at(k):
                return SQ[:, k * T:(k + 1) * T]

            def down(name):
                for m in range(8):
                    unit(PLAN.at[name][1] + m, PLAN.q(name) + 3 * m, 3, lambda k: FAH[:, k, :], lambda k: FAL[:, k, :])

            h_hi, h_lo = (lambda k: HH[:, k, :]), (lambda k: HL[:, k, :])

            pe.wait_ge(par_in_sem, 16)
            pe.wait_ge(consts_ready, 3)
            pe.wait_ge(sq_ready, 1)
            stat("stat_mix", sq_at, 8)
            pe.wait_ge(ada_used, 8 + 16)
            mod_columns("mod_a", ACC1, 0, 16)
            pe.wait_ge(h_ready, 8)
            pe.wait_ge(wdt_ready, 1)
            out = scratch("dt")
            for k in range(KD):
                wh, wl = (WDT[:, part, k * 32:(k + 1) * 32] for part in range(2))
                last = triple(out[0:32, 0:T], wh, wl, HH[:, k, :], HL[:, k, :], k == 0, k == 7)
            last.then_inc(s_done, 1)
            linear8("in1", 0, 64, h_hi, h_lo)
            pe.wait_ge(ada_used, 8 + 48)
            mod_columns("mod_b", ACC1, 16, 48)
            pe.wait_ge(dt_ready, 1)
            out = scratch("dt_turn")
            for n, row in enumerate((5, 5, 3, 3)):
                last = nc.tensor.transpose(out[:, 32 * n:32 * n + 32], dts[:, row, (n % 2) * P:(n % 2 + 1) * P],
                                           pv("ident", 0, 32)[0:32, :])
            last.then_inc(s_done, 1)
            pe.wait_ge(xbc_ready, 8)
            for i in range(8):
                t, q = divmod(i, 4)
                out = scratch("x_turn", i)
                for b in range(4):
                    last = nc.tensor.transpose(out[:, b * P:(b + 1) * P], XBC[:, 4 * q + b, t * P:(t + 1) * P], pv("ident"))
                last.then_inc(s_done, 1)
            for g in range(NGRP):
                out = scratch("scores", g)
                mm(out[:, 0:256], XBC[:, 16 + g, 0:P], XBC[:, 20 + g, :], True, True)
                mm(out[:, 256:384], XBC[:, 16 + g, P:T], XBC[:, 20 + g, P:T], True, True).then_inc(s_done, 1)
            for p in range(HEADS1 // 2 + 1):
                if p < HEADS1 // 2:
                    unit(PLAN.at["in1"][1] + 64 + p, PLAN.q("in1") + 64 + p, 1, h_hi, h_lo)
                if p >= 1:
                    n = p - 1
                    ob = obank(OUT_Y + n)
                    if n == 0:
                        pe.wait_ge(xtok_ready, 8)
                    pe.wait_ge(m_ready, n + 1)
                    for e in range(2):
                        rows = slice(64 * e, 64 * e + 64)
                        cols = slice(P * n + 64 * e, P * n + 64 * e + 64)
                        mm(ob[rows, 0:T], XTOK[:, 0, cols], SM[:, n % 2, 384 * e:384 * e + 256], True, False)
                        last = mm(ob[rows, P:T], XTOK[:, 1, cols], SM[:, n % 2, 384 * e + 256:384 * e + 384], False, True)
                    last.then_inc(m_used, 1)
            for g in range(NGRP):
                pe.wait_ge(sq_ready, 2 + g)
                stat("gnorm", lambda k: SQ[:, (g % 2) * 1024 + k * T:(g % 2) * 1024 + (k + 1) * T], 4, g)
            for m in range(8):
                if m == 0:
                    pe.wait_ge(zl_ready, 4)
                unit(PLAN.at["ssd_out"][1] + m, PLAN.q("ssd_out") + 2 * m, 2, lambda k: ZH[:, k, :], lambda k: ZL[:, k, :])
            pe.wait_ge(yl_ready, 1)
            linear8("sc_out", 0, 8, lambda k: YH[:, k, :], lambda k: YL[:, k, :])
            pe.wait_ge(ml_ready, 8)
            linear8("o1", 0, 8, lambda k: MH[:, k, :], lambda k: ML[:, k, :])
            pe.wait_ge(sq_ready, 5 + 8)
            stat("stat_o1", sq_at, 8)
            pe.wait_ge(sq_ready, 14)
            stat("stat_ffn1", sq_at, 8)
            pe.wait_ge(h_ready, 16)
            linear8("up1", 0, 44, h_hi, h_lo)
            pe.wait_ge(f_act, KF)
            down("down1")
            pe.wait_ge(sq_ready, 14 + 8)
            stat("stat_down1", sq_at, 8)
            pe.wait_ge(ada_used, 8 + 96)
            mod_columns("mod_2", ACC2, 0, 48)

            pe.wait_ge(sq_ready, 23)
            stat("stat_attn", sq_at, 8)
            pe.wait_ge(h_ready, 24)
            q0, u0 = PLAN.q("tok2"), PLAN.at["tok2"][1]
            for c in range(9):
                for t in range(2):
                    bank_wait(u0 + 2 * c + t)
                for part in range(2):
                    split_wait(q0 + 2 * c + part)
                    s = (q0 + 2 * c + part) % SLOTS
                    for t in range(2):
                        out = psL[:, (u0 + 2 * c + t) % 4, 0:256]
                        for b in range(4):
                            k = 4 * part + b
                            hh, hl = (x[:, k, t * P:(t + 1) * P] for x in (HH, HL))
                            wh, wl = (x[:, s, b * 256:(b + 1) * 256] for x in (WH, WL))
                            mm(out, hh, wh, k == 0, False)
                            mm(out, hh, wl, False, False)
                            last = mm(out, hl, wh, False, k == 7)
                        if part == 1:
                            last.then_inc(lin_done, 1)
            q0, u0 = PLAN.q("mix2"), PLAN.at["mix2"][1]
            split_wait(q0)
            for t in range(2):
                bank_wait(u0 + t)
                out = psL[:, (u0 + t) % 4, 0:88]
                for k in range(KD):
                    hh, hl = (x[:, k, t * P:(t + 1) * P] for x in (HH, HL))
                    wh, wl = (x[:, q0 % SLOTS, k * 88:(k + 1) * 88] for x in (WH, WL))
                    mm(out, hh, wh, k == 0, False)
                    mm(out, hh, wl, False, False)
                    last = mm(out, hl, wh, False, k == 7)
                last.then_inc(lin_done, 1)
            linear8("feat2", 0, 23, h_hi, h_lo)
            pe.wait_ge(sq_ready, 24)
            stat("stat_cq", sq_at, 3)
            stat("stat_ckv", lambda k: sq_at(3 + k), 2)
            pe.wait_ge(cqn_ready, 5)
            c0, u0 = PLAN.at["uq"]
            for h in range(NH):
                chunk_wait(c0 + h)
                bank_wait(u0 + h)
                for t in range(2):
                    for k in range(3):
                        last = mm(psL[:, (u0 + h) % 4, t * QK:(t + 1) * QK], CQ[:, k, t * P:(t + 1) * P],
                                  ring[:, (c0 + h) % SLOTS, k * QK:(k + 1) * QK], k == 0, k == 2)
                last.then_inc(lin_done, 1)
            c0, u0 = PLAN.at["ukv"]
            for c in range(4):
                chunk_wait(c0 + c)
                for t in range(2):
                    u = u0 + 2 * c + t
                    bank_wait(u)
                    for k in range(2):
                        last = mm(psL[:, u % 4, :], CKV[:, k, t * P:(t + 1) * P],
                                  ring[:, (c0 + c) % SLOTS, k * 512:(k + 1) * 512], k == 0, k == 1)
                    last.then_inc(lin_done, 1)
            for i in range(7):
                if i == 0:
                    pe.wait_ge(troped, 4)
                out = scratch("nsa_turn", i)
                for n in range(4):
                    hh, t = divmod(n, 2)
                    src = (QTOK[:, t, (2 * i + hh) * HD:(2 * i + hh + 1) * HD] if i < 4 else
                           KTOK[:, t, (2 * (i - 4) + hh) * HD:(2 * (i - 4) + hh + 1) * HD])
                    last = nc.tensor.transpose(out[:, n * P:(n + 1) * P], src, pv("ident"))
                last.then_inc(s_done, 1)
            c0, u0 = PLAN.at["cmp"]
            for kv in range(2):
                pe.wait_ge(cb_ready, kv + 1)
                for half in range(2):
                    u = u0 + 2 * kv + half
                    bank_wait(u)
                    for l in range(32):
                        c = c0 + 8 * kv + 4 * half + l // 8
                        if l % 8 == 0:
                            chunk_wait(c)
                        last = mm(psL[:, u % 4, 0:30], blk(c, l % 8), CB[kv][:, l, :], l == 0, l == 31)
                    last.then_inc(lin_done, 1)
            pe.wait_ge(hid_ready, 2)
            out = scratch("kc")
            for half in range(2):
                last = mm(out[0:30, 0:P], HID[:, half, :], pv("k_w2", half * P, P), half == 0, half == 1)
            last.then_inc(s_done, 1)
            pe.wait_ge(kcn_ready, 1)
            out = scratch("kc_turn")
            nc.tensor.transpose(out[:, 0:30], KCN, pv("ident", 0, 30)[0:30, :]).then_inc(s_done, 1)
            pe.wait_ge(hid_ready, 4)
            out = scratch("vc")
            for g in range(2):
                for half in range(2):
                    last = mm(out[0:NCMP, g * P:(g + 1) * P], HID[:, 2 + half, g * NCMP:(g + 1) * NCMP],
                              pv("v_w2", half * P, P), half == 0, half == 1)
            last.then_inc(s_done, 1)
            u = PLAN.at["cmp_scores"][1]
            bank_wait(u)
            pe.wait_ge(turned, 7 + 1)
            for h in range(NH):
                for t in range(2):
                    o = (2 * h + t) * NCMP
                    last = mm(psL[:, u % 4, o:o + NCMP], QT[:, h, t * P:(t + 1) * P],
                              KCT[:, (h // 4) * NCMP:(h // 4 + 1) * NCMP], True, True)
            last.then_inc(lin_done, 1)

            def attend(name, pname, obase, count, score, value, lead_in, p0):
                u0 = PLAN.at[name][1]
                for i in range(count + 3):
                    if i < count:
                        u = u0 + i
                        bank_wait(u)
                        out = psL[:, u % 4, :]
                        score(i, out[:, 0:P], 0, P, True)
                        mm(out[:, 0:P], identb[:, :], maskb[:, :], False, True)
                        score(i, out[:, P:384], P, T, True)
                        mm(out[:, 256:384], identb[:, :], maskb[:, :], False, True).then_inc(lin_done, 1)
                    if 2 <= i <= count + 1:
                        n = i - 2
                        out = scratch(pname, n)
                        pe.wait_ge(p_ready, p0 + n + 1)
                        pr = PR[:, (p0 + n) % 3, :]
                        for b in range(3):
                            last = nc.tensor.transpose(out[:, b * P:(b + 1) * P], pr[:, b * P:(b + 1) * P], pv("ident"))
                        last.then_inc(s_done, 1)
                    if i >= 3:
                        n = i - 3
                        per = 2 if name == "nsa_scores" else 1
                        if n % per == 0:
                            ob = obank(obase + n // per)
                            if lead_in:
                                lead_in(n // per, ob)
                        pe.wait_ge(pt_ready, p0 + n + 1)
                        v0, v1 = value(n)
                        mm(ob[:, 0:T], v0, PT[:, (p0 + n) % 2, 0:256], n % per == 0 and not lead_in, False)
                        last = mm(ob[:, P:T], v1, PT[:, (p0 + n) % 2, 256:384], False, n % per == per - 1)
                        last.then_inc(pt_used, 1)

            for j in range(4):
                out = scratch("cmp_turn", j)
                pe.wait_ge(cp_ready, 1)
                for n in range(4):
                    o = (4 * j + n) * NCMP
                    last = nc.tensor.transpose(out[0:NCMP, n * P:(n + 1) * P], CS[:, o:o + NCMP], pv("ident"))
                last.then_inc(s_done, 1)
            pe.wait_ge(ptc_ready, 4)
            pe.wait_ge(vcmp_ready, 1)

            def nsa_score(i, out, q0, n_keys, start):
                h, b = divmod(i, 2)
                mm(out, QT[:, h, q0:q0 + P], KT[:, 2 * b + h // 4, 0:n_keys], start, False)

            def nsa_value(n):
                h, b = divmod(n, 2)
                o = b * 256 + (h // 4) * HD
                return VTOK[:, 0, o:o + HD], VTOK[:, 1, o:o + HD]

            def cmp_value(h, ob):
                mm(ob[:, 0:T], VCMP[:, h // 4, :], PTC[0:NCMP, h, :], True, False)

            attend("nsa_scores", "nsa_p", OUT_NSA, 16, nsa_score, nsa_value, cmp_value, 0)

            for i in range(16):
                kind, pair = divmod(i, 4)
                src, lo, wd = ((QB, 0, HD), (QB, HD, ROPE), (KB, 0, HD), (KB, HD, ROPE))[kind]
                if i == 0:
                    pe.wait_ge(troped, 8)
                out = scratch("mla_turn", i)
                for n in range(4):
                    hh, t = divmod(n, 2)
                    o = (2 * pair + hh) * QK + lo
                    last = nc.tensor.transpose(out[0:wd, n * P:(n + 1) * P], src[:, t, o:o + wd], pv("ident"))
                last.then_inc(s_done, 1)
            pe.wait_ge(turned, 8 + 16)

            def mla_score(i, out, q0, n_keys, start):
                mm(out, MQN[:, i, q0:q0 + P], MKN[:, i, 0:n_keys], start, False)
                mm(out, MQR[0:ROPE, i, q0:q0 + P], MKR[0:ROPE, i, 0:n_keys], False, False)

            def mla_value(n):
                return VB[:, 0, n * HD:(n + 1) * HD], VB[:, 1, n * HD:(n + 1) * HD]

            attend("mla_scores", "mla_p", OUT_MLA, 8, mla_score, mla_value, None, 16)
            pe.wait_ge(oml_ready, 8)
            linear8("o2", 0, 8, lambda k: OMH[:, k, :], lambda k: OML[:, k, :])
            pe.wait_ge(sq_ready, 25)
            stat("stat_ffn2", sq_at, 8)
            pe.wait_ge(h_ready, 32)
            linear8("up2", 0, 44, h_hi, h_lo)
            pe.wait_ge(f_act, 2 * KF)
            down("down2")

        @block.scalar
        def _(act):
            st = Steps(act, act_step)
            A = nc.scalar.activation

            def stat_root(name, width, dst, i=0):
                act.wait_ge(s_done, SCRATCH[name] + i + 1)
                n = SCRATCH[name] + i
                A(dst, sbank(name, i)[:, 0:T], ACT.Ln, scale=1.0 / width, bias=eps_col[:, :]).then_inc(s_free[n % 2], 1)
                act.wait_ge(s_free[n % 2], n // 2 + 1)
                A(dst, dst, ACT.Exp, scale=-0.5).then_inc(rs_ready, 1)

            fed = [0]

            def high(q, i=0):
                c = PLAN.chunk_of[q]
                k, n = q % SLOTS, PLAN.cols[c]
                act.wait_ge(w_arrived[k], 16 * (c // SLOTS + 1) + 16 * i)
                A(WH[:, k, 0:n], ring[:, k, 0:n], ACT.Copy).then_inc(hi_done, 1)

            def feed(u):
                while fed[0] < SPLITS and PLAN.splittable(fed[0]) <= u + 1:
                    high(fed[0])
                    fed[0] += 1

            def units(name, first, count, evacuate):
                u0, q0 = PLAN.at[name][1] + first, PLAN.q(name) + first
                assert count % 4 == 0 and fed[0] == q0 + SLOTS, (name, fed, q0)
                with st.repeat(count // 4, 0) as i:
                    for k in range(4):
                        u = u0 + k
                        act.wait_ge(lin_done, u + 1 + i * 4)
                        if evacuate:
                            evacuate(k, u, i)
                        high(q0 + k + SLOTS, i)
                fed[0] += count

            def col(buf, j, n=1):
                return buf[:, bass.ds(j, n), :].rearrange("p a b -> p (a b)")

            def wide(view):
                return view.rearrange("p a b -> p (a b)")

            def make_hh(shift, base):
                for j in range(KD):
                    act.wait_ge(t_ready, base + j + 1)
                    A(HH[:, j, :], CT[:, j % 4, :], ACT.Identity, bias=shift[:, j:j + 1]).then_inc(hh_ready, 1)

            act.wait_ge(par_in_sem, 16)
            act.wait_ge(consts_ready, 3)
            A(csil[:, :], par[:, 0:16], ACT.Silu).then_inc(csil_ready, 1)
            A(WDT[:, 0, :], pv("w_dt"), ACT.Copy).then_inc(wdt_hi, 1)
            act.wait_ge(x_in, 16)
            A(SQ[:, :], wide(X[:, :, :]), ACT.Square).then_inc(sq_ready, 1)
            stat_root("stat_mix", D, RS[:, 0, :])
            feed(-1)
            make_hh(mod[:, 0:8], 0)
            n = SCRATCH["dt"]
            act.wait_ge(s_done, n + 1)
            A(dts[:, 0, :], psS[0:32, n % 2, 0:T], ACT.Identity, bias=pv("dt_bias")[0:32, :]).then_inc(s_free[n % 2], 1)
            act.wait_ge(s_free[n % 2], n // 2 + 1)
            st.link(A(dts[:, 1, :], dts[:, 0, :], ACT.Abs))
            st.link(A(dts[:, 1, :], dts[:, 1, :], ACT.Exp, scale=-1.0))
            A(sm[0:32, 95:96], pv("a_log")[0:32, :], ACT.Exp).then_inc(dtx_ready, 1)
            act.wait_ge(dtw_ready, 1)
            A(dts[:, 4, :], dts[:, 2, :], ACT.Ln).then_inc(dtl_ready, 1)
            c_w, c_b = PAR["xconv_w"][0], PAR["xconv_b"][0]

            def begin_xbc(k, u, i):
                m = i * 4 + k
                A(col(XBC, m), psL[:, u % 4, 0:T], ACT.Identity, scale=par[:, bass.ds(m + (c_w + 3 * NXBC), 1)],
                  bias=par[:, bass.ds(m + c_b, 1)]).then_inc(conv_begun, 1)

            units("in1", 0, 24, begin_xbc)
            act.wait_ge(dt_ready, 1)
            act.dma_start(cum_dram, dts[:, 5, :]).then_inc(cum_stored, 16)
            def z_bank(k, u, i):
                A(col(Z, i * 4 + k), psL[:, u % 4, 0:T], ACT.Silu).then_inc(lin_free[u % 4], 1)
                if k % 2 == 1:
                    m = i * 6 + 3 * (k // 2)
                    act.wait_ge(conv_done, m + 3)
                    A(col(XBC, m, 3), col(XBC, m, 3), ACT.Silu).then_inc(xbc_ready, 1)

            units("in1", 24, 16, z_bank)

            def sc_c_bank(k, u, i):
                A(col(SCQ, i * 4 + k), psL[:, u % 4, 0:T], ACT.Copy).then_inc(sc_c_ready, 1)
                act.wait_ge(sc_c_ready, i * 4 + (k + 1))
                act.sem_inc(lin_free[u % 4], 1)

            units("in1", 40, 8, sc_c_bank)
            units("in1", 48, 16, None)
            n = SCRATCH["dt_turn"]
            act.wait_ge(s_done, n + 1)
            A(CD[:, :, :].rearrange("p a b -> p (a b)"), psS[:, n % 2, 0:128], ACT.Copy).then_inc(s_free[n % 2], 1)
            def load_cum(i):
                act.dma_start(CUMB[:, i % 2, :],
                              cum_dram[4 * i:4 * i + 4, :].rearrange("h t -> (h t)").partition_broadcast(P)
                              ).then_inc(cum_in[i % 2], 16)

            act.wait_ge(cum_stored, 16)
            act.wait_ge(ysc_ready, 8)
            load_cum(0)
            load_cum(1)
            act.wait_ge(s_free[n % 2], n // 2 + 1)
            act.sem_inc(cd_ready, 1)
            for i in range(8):
                n = SCRATCH["x_turn"] + i
                t, q = divmod(i, 4)
                act.wait_ge(s_done, n + 1)
                A(XTOK[:, t, 512 * q:512 * q + 512], psS[:, n % 2, :], ACT.Copy).then_inc(s_free[n % 2], 1)
                act.wait_ge(s_free[n % 2], n // 2 + 1)
                act.sem_inc(xtok_ready, 1)
            for p in range(HEADS1 // 2):
                u = PLAN.at["in1"][1] + 64 + p
                act.wait_ge(diff_ready, p + 1)
                A(SE[:, p % 2, :], SE[:, p % 2, :], ACT.Exp).then_inc(decay_ready, 1)
                if p % 2 == 1 and p // 2 + 2 < 8:
                    load_cum(p // 2 + 2)
                act.wait_ge(lin_done, u + 1)
                A(G1[:, p, :], psL[:, u % 4, 0:T], ACT.Copy).then_inc(lin_free[u % 4], 1)
                feed(u)
            for g in range(NGRP):
                act.wait_ge(y_ready, 4 * (g + 1))
                if g == 0:
                    act.wait_ge(m_ready, HEADS1 // 2)
                if g >= 2:
                    act.wait_ge(s_done, SCRATCH["gnorm"] + g - 1)
                A(SQ[:, (g % 2) * 1024:(g % 2 + 1) * 1024], wide(Z[:, 4 * g:4 * g + 4, :]),
                  ACT.Square).then_inc(sq_ready, 1)
                if g >= 1:
                    if g >= 3:
                        act.wait_ge(yn_ready, 4 * (g - 2))
                    stat_root("gnorm", 512, RS[:, (g - 1) % 2, :], g - 1)
            act.wait_ge(yn_ready, 8)
            stat_root("gnorm", 512, RS[:, 1, :], 3)
            for g in range(NGRP):
                act.wait_ge(yn_ready, 4 * g + 4)
                A(wide(ZH[:, 4 * g:4 * g + 4, :]), wide(Z[:, 4 * g:4 * g + 4, :]), ACT.Copy).then_inc(zh_ready, 1)
            act.wait_ge(diff_ready, HEADS1 // 2)
            A(wide(YH), wide(YSC), ACT.Copy).then_inc(yh_ready, 1)
            for n in range(4):
                act.wait_ge(lin_free[n], PLAN.at["ssd_out"][1] // 4)
            for half in range(2):
                A(wide(G1[:, 8 * half:8 * half + 8, :]), wide(G1[:, 8 * half:8 * half + 8, :]), ACT.Sigmoid
                  ).then_inc(gates_ready, 1)

            def follow(name, first=0, count=8):
                for m in range(first, first + count):
                    u = PLAN.at[name][1] + m
                    act.wait_ge(lin_done, u + 1)
                    feed(u)

            follow("ssd_out")
            follow("sc_out", 0, 7)
            for m in range(8):
                act.wait_ge(mixin_ready, m + 1)
                A(MH[:, m, :], MIXIN[:, m, :], ACT.Copy).then_inc(mh_ready, 1)
            follow("sc_out", 7, 1)

            def copy_and_square(name, dst, sq_free_after):
                u0 = PLAN.at[name][1]
                act.wait_ge(s_done, sq_free_after + 1)
                for m in range(8):
                    u = u0 + m
                    act.wait_ge(lin_done, u + 1)
                    st.mark(A(dst[:, m, :], psL[:, u % 4, 0:T], ACT.Copy))
                    A(SQ[:, m * T:(m + 1) * T], psL[:, u % 4, 0:T], ACT.Square).then_inc(lin_free[u % 4], 1)
                    act.wait_ge(lin_free[u % 4], u // 4 + 1)
                    act.wait_ge(act_step, st.n)
                    act.sem_inc(sq_ready, 1)
                    feed(u)

            def square_x(after):
                act.wait_ge(x_ready, after)
                A(SQ[:, :], wide(X[:, :, :]), ACT.Square).then_inc(sq_ready, 1)

            copy_and_square("o1", MIX, SCRATCH["gnorm"] + 3)
            stat_root("stat_o1", D, RS[:, 0, :])
            square_x(8)
            stat_root("stat_ffn1", D, RS[:, 1, :])
            make_hh(mod[:, 24:32], 8)

            def ffn(name, wname, bname, base):
                u0, q0 = PLAN.at[name][1], PLAN.q(name)
                w0, b0 = PAR[wname][0], PAR[bname][0]
                assert fed[0] == q0 + SLOTS

                def begin(j, slot, it=0):
                    for b in range(2):
                        u = u0 + 2 * j + b
                        act.wait_ge(lin_done, u + 1 + it * 2)
                        if b == 0 and (j + base >= 2):
                            act.wait_ge(f_act, base + j - 1 + it)
                        A(CT[:, 2 * slot + b, :], psL[:, u % 4, 0:T], ACT.Identity,
                          scale=par[:, bass.ds(w0 + 2 * 44 + b * KF + j + it, 1)],
                          bias=par[:, bass.ds(b0 + b * KF + j + it, 1)]).then_inc(f_begun, 1)
                        q = q0 + 2 * j + b + SLOTS
                        c = PLAN.chunk_of[q]
                        act.wait_ge(w_arrived[q % SLOTS], 16 * (c // SLOTS + 1) + (it * 8))
                        n = PLAN.cols[c]
                        A(WH[:, q % SLOTS, 0:n], ring[:, q % SLOTS, 0:n], ACT.Copy).then_inc(hi_done, 1)

                def silu(j, slot, it=0):
                    act.wait_ge(f_conv, base + j + 1 + it)
                    A(CT[:, 2 * slot, :], CT[:, 2 * slot, :], ACT.Silu).then_inc(f_silu, 1)

                def product_high(j, slot, it=0):
                    act.wait_ge(f_prod, base + j + 1 + it)
                    A(col(FAH, j + it), CT[:, 2 * slot, :], ACT.Copy).then_inc(f_hi, 1)

                begin(0, 0)
                begin(1, 1)
                silu(0, 0)
                product_high(0, 0)
                with st.repeat(9, 0) as i:
                    begin(2, 0, i * 2)
                    silu(1, 1, i * 2)
                    product_high(1, 1, i * 2)
                    begin(3, 1, i * 2)
                    silu(2, 0, i * 2)
                    product_high(2, 0, i * 2)
                for j in (20, 21):
                    begin(j, j % 2)
                    silu(j - 1, (j - 1) % 2)
                    product_high(j - 1, (j - 1) % 2)
                silu(21, 1)
                product_high(21, 1)
                fed[0] += 44

            ffn("up1", "fconv_w", "fconv_b", 0)
            copy_and_square("down1", FO, SCRATCH["stat_ffn1"])
            stat_root("stat_down1", D, RS[:, 0, :])

            square_x(16)
            stat_root("stat_attn", D, RS[:, 1, :])
            make_hh(mod[:, 0:8], 16)
            u0 = PLAN.at["tok2"][1]
            for c in range(6):
                for t in range(2):
                    u = u0 + 2 * c + t
                    act.wait_ge(lin_done, u + 1)
                    for hh in range(2):
                        n = 4 * c + 2 * t + hh
                        if n >= 16:
                            act.wait_ge(tok_sq, n - 15)
                        A(SQ[:, n % 16 * P:(n % 16 + 1) * P], psL[:, u % 4, hh * P:(hh + 1) * P], ACT.Square,
                          accum_out=sm[:, t * 12 + 2 * c + hh:t * 12 + 2 * c + hh + 1]).then_inc(tok_sq, 1)
                    feed(u)
            for c in range(3):
                for t in range(2):
                    u = u0 + 2 * (6 + c) + t
                    act.wait_ge(lin_done, u + 1)
                    dst = KTOK[:, t, 512:768] if c == 0 else VTOK[:, t, (c - 1) * 256:c * 256]
                    A(dst, psL[:, u % 4, 0:256], ACT.Copy).then_inc(lin_free[u % 4], 1)
                    act.wait_ge(lin_free[u % 4], u // 4 + 1)
                    feed(u)
            act.sem_inc(tok_ready, 1)
            act.wait_ge(tok_sq, 24)
            st.link(A(sm[:, 0:24], sm[:, 0:24], ACT.Ln, scale=1.0 / HD, bias=eps_col[:, :]))
            A(sm[:, 0:24], sm[:, 0:24], ACT.Exp, scale=-0.5).then_inc(trs, 1)
            u0 = PLAN.at["mix2"][1]
            for t in range(2):
                u = u0 + t
                act.wait_ge(lin_done, u + 1)
                st.mark(A(KR[:, t, :], psL[:, u % 4, 0:64], ACT.Copy))
                st.mark(A(SQ[:, 64 * t:64 * t + 64], psL[:, u % 4, 0:64], ACT.Square, accum_out=sm[:, 24 + t:25 + t]))
                A(GT[:, t, :], psL[:, u % 4, 64:88], ACT.Sigmoid).then_inc(lin_free[u % 4], 1)
                act.wait_ge(lin_free[u % 4], u // 4 + 1)
                feed(u)
            act.wait_ge(act_step, st.n)
            act.sem_inc(ng_ready, 1)
            for m in range(7):
                u = u0 + 2 + m
                dst = VC[:, m, :] if m < 2 else CQ[:, m - 2, :] if m < 5 else CKV[:, m - 5, :]
                act.wait_ge(lin_done, u + 1)
                if m >= 2:
                    st.mark(A(SQ[:, (m - 2) * T:(m - 1) * T], psL[:, u % 4, 0:T], ACT.Square))
                A(dst, psL[:, u % 4, 0:T], ACT.Copy).then_inc(lin_free[u % 4], 1)
                act.wait_ge(lin_free[u % 4], u // 4 + 1)
                feed(u)
            act.wait_ge(act_step, st.n)
            act.sem_inc(sq_ready, 1)
            act.sem_inc(feat_ready, 1)
            for m in range(16):
                u = u0 + 9 + m
                act.wait_ge(lin_done, u + 1)
                A(G2[:, m, :], psL[:, u % 4, 0:T], ACT.Sigmoid).then_inc(lin_free[u % 4], 1)
                feed(u)
            for n in range(4):
                act.wait_ge(lin_free[(u - n) % 4], (u - n) // 4 + 1)
            act.sem_inc(gates_ready, 1)
            act.wait_ge(h_ready, 24)
            stat_root("stat_cq", 384, RS[:, 0, :])
            stat_root("stat_ckv", 256, RS[:, 1, :])
            u0 = PLAN.at["uq"][1]
            for h in range(NH):
                u = u0 + h
                act.wait_ge(lin_done, u + 1)
                A(QB[:, :, h * QK:(h + 1) * QK], psL[:, u % 4, 0:2 * QK].rearrange("p (t d) -> p t d", d=QK),
                  ACT.Copy).then_inc(lin_free[u % 4], 1)
                act.wait_ge(lin_free[u % 4], u // 4 + 1)
            u0 = PLAN.at["ukv"][1]
            for n in range(8):
                c, t = n // 2, n % 2
                u = u0 + n
                act.wait_ge(lin_done, u + 1)
                src = psL[:, u % 4, :].rearrange("p (h w) -> p h w", w=256)
                st.mark(A(KB[:, t, :].rearrange("p (h w) -> p h w", w=QK)[:, 2 * c:2 * c + 2, 0:HD], src[:, :, 0:HD], ACT.Copy))
                A(VB[:, t, :].rearrange("p (h w) -> p h w", w=HD)[:, 2 * c:2 * c + 2, :], src[:, :, HD:256],
                  ACT.Copy).then_inc(lin_free[u % 4], 1)
                act.wait_ge(lin_free[u % 4], u // 4 + 1)
            act.wait_ge(act_step, st.n)
            act.sem_inc(mla_tok, 1)
            for i in range(7):
                n = SCRATCH["nsa_turn"] + i
                act.wait_ge(s_done, n + 1)
                dst = (QT[:, 2 * i:2 * i + 2, :] if i < 4 else KT[:, 2 * (i - 4):2 * (i - 4) + 2, :])
                A(dst.rearrange("p a b -> p (a b)"), psS[:, n % 2, :], ACT.Copy).then_inc(s_free[n % 2], 1)
                act.wait_ge(s_free[n % 2], n // 2 + 1)
                act.sem_inc(turned, 1)
            act.wait_ge(tsum, 1)
            st.link(A(mlars[:, :], mlars[:, :], ACT.Ln, scale=1.0 / QK, bias=eps_col[:, :]))
            A(mlars[:, :], mlars[:, :], ACT.Exp, scale=-0.5).then_inc(mla_sq, 1)
            u0 = PLAN.at["cmp"][1]
            for n in range(4):
                u = u0 + n
                act.wait_ge(lin_done, u + 1)
                A(HID[:, n, :], psL[:, u % 4, 0:30], ACT.Silu).then_inc(lin_free[u % 4], 1)
                act.wait_ge(lin_free[u % 4], u // 4 + 1)
                act.sem_inc(hid_ready, 1)
                feed(u)
            n = SCRATCH["kc"]
            act.wait_ge(s_done, n + 1)
            st.link(A(KCD, psS[0:30, n % 2, 0:P], ACT.Square, accum_out=sm[0:30, 60:61]))
            st.link(A(sm[0:30, 60:61], sm[0:30, 60:61], ACT.Ln, scale=1.0 / HD, bias=eps_col[0:30, :]))
            A(sm[0:30, 60:61], sm[0:30, 60:61], ACT.Exp, scale=-0.5).then_inc(kc_rs, 1)
            n = SCRATCH["kc_turn"]
            act.wait_ge(s_done, n + 1)
            A(KCT, psS[:, n % 2, 0:30], ACT.Copy).then_inc(s_free[n % 2], 1)
            act.wait_ge(s_free[n % 2], n // 2 + 1)
            act.sem_inc(turned, 1)
            n = SCRATCH["vc"]
            act.wait_ge(s_done, n + 1)
            A(VCMP.rearrange("p a b -> p (a b)"), psS[0:NCMP, n % 2, 0:256], ACT.Copy).then_inc(s_free[n % 2], 1)
            act.wait_ge(s_free[n % 2], n // 2 + 1)
            act.sem_inc(vcmp_ready, 1)
            act.wait_ge(cs_ready, 1)
            A(CS, CS, ACT.Exp).then_inc(ce_ready, 1)
            for j in range(4):
                n = SCRATCH["cmp_turn"] + j
                act.wait_ge(s_done, n + 1)
                A(PTC[0:NCMP, 2 * j:2 * j + 2, :].rearrange("p a b -> p (a b)"), psS[0:NCMP, n % 2, :],
                  ACT.Copy).then_inc(s_free[n % 2], 1)
                act.wait_ge(s_free[n % 2], n // 2 + 1)
                act.sem_inc(ptc_ready, 1)

            def softmax(pname, count, p0):
                for i in range(count + 2):
                    if i < count:
                        n = p0 + i
                        u = PLAN.at["nsa_scores"][1] + n
                        act.wait_ge(max_ready, n + 1)
                        if n >= 3:
                            act.wait_ge(s_done, SCRATCH["nsa_p"] + n - 2 if n - 3 < 16 else SCRATCH["mla_p"] + n - 18)
                        st.mark(A(PR[:, n % 3, 0:P], psL[:, u % 4, 0:P], ACT.Exp, bias=sm[:, 26 + 4 * (n % 2):27 + 4 * (n % 2)],
                                  accum_out=sm[:, 28 + 4 * (n % 2):29 + 4 * (n % 2)]))
                        A(PR[:, n % 3, P:384], psL[:, u % 4, P:384], ACT.Exp, bias=sm[:, 27 + 4 * (n % 2):28 + 4 * (n % 2)],
                          accum_out=sm[:, 29 + 4 * (n % 2):30 + 4 * (n % 2)]).then_inc(lin_free[u % 4], 1)
                        act.wait_ge(lin_free[u % 4], u // 4 + 1)
                        act.wait_ge(act_step, st.n)
                        act.sem_inc(exp_ready, 1)
                    if i >= 2:
                        m = p0 + i - 2
                        n = SCRATCH[pname] + i - 2
                        act.wait_ge(s_done, n + 1)
                        if m >= 2:
                            act.wait_ge(pt_used, m - 1)
                        A(PT[:, m % 2, :], psS[:, n % 2, 0:384], ACT.Copy).then_inc(s_free[n % 2], 1)
                        act.wait_ge(s_free[n % 2], n // 2 + 1)
                        act.sem_inc(pt_ready, 1)

            softmax("nsa_p", 16, 0)
            act.wait_ge(pt_used, 16)
            act.wait_ge(om_ready, 8)
            for i in range(16):
                kind, pair = divmod(i, 4)
                dst, wd = ((MQN, HD), (MQR, ROPE), (MKN, HD), (MKR, ROPE))[kind]
                n = SCRATCH["mla_turn"] + i
                act.wait_ge(s_done, n + 1)
                A(dst[0:wd, 2 * pair:2 * pair + 2, :].rearrange("p a b -> p (a b)"), psS[0:wd, n % 2, :],
                  ACT.Copy).then_inc(s_free[n % 2], 1)
                act.wait_ge(s_free[n % 2], n // 2 + 1)
                act.sem_inc(turned, 1)
            softmax("mla_p", 8, 16)
            act.wait_ge(pt_used, 24)
            for h in range(NH):
                act.wait_ge(om_ready, 8 + h + 1)
                A(OMH[:, h, :], OM[:, h, :], ACT.Copy).then_inc(omh_ready, 1)
            follow("o2")
            square_x(24)
            stat_root("stat_ffn2", D, RS[:, 0, :])
            make_hh(mod[:, 24:32], 24)
            ffn("up2", "fconv_w_2", "fconv_b_2", KF)
            follow("down2")

        @block.vector
        def _(dve):
            st = Steps(dve, dve_step)
            V = nc.vector

            def scratch_wait(name, i=0):
                n = SCRATCH[name] + i
                dve.wait_ge(s_done, n + 1)
                return psS[:, n % 2, :], s_free[n % 2]

            def lin(u, rounds=0):
                dve.wait_ge(lin_done, u + 1 + rounds)
                return psL[:, u % 4, 0:T]

            V.memset(eps_col[:, :], EPS).then_inc(consts_ready, 1)
            V.memset(ACC1[:, 0:2048], 0.0).then_inc(ada_used, 8)
            dve.wait_ge(par_in_sem, 16)
            V.tensor_copy(identb[:, :], pv("ident")).then_inc(consts_ready, 1)
            V.tensor_copy(maskb[:, :], pv("causal_add")).then_inc(consts_ready, 1)
            dve.wait_ge(csil_ready, 1)
            dve.wait_ge(ada_used, 8)

            def ada_step(n, a, col, groups, rounds=0, total=0):
                k = n % ADA_SLOTS
                dve.wait_ge(ada_arrived[k], 16 * (n // ADA_SLOTS + 1) + rounds * (16 * total // ADA_SLOTS))
                dve.wait_ge(ada_used, 8 + n - groups + 1 + rounds * total)
                V.scalar_tensor_tensor(a, adaring[:, k * ADA_COLS:(k + 1) * ADA_COLS], col, a, MUL, ADD
                                       ).then_inc(ada_used, 1)

            def part(acc, g):
                return acc[:, g * ADA_COLS:(g + 1) * ADA_COLS]

            with st.repeat(4, 0) as i:
                for kk in range(2):
                    for g in range(2):
                        ada_step(2 * kk + g, part(ACC1, g), csil[:, bass.ds(i * 2 + kk, 1)], 2, i, 4)

            def make_h(shift, gains, rs, base):
                for j in range(KD + 1):
                    if j < KD:
                        if j >= 4:
                            dve.wait_ge(h_ready, base + j - 3)
                        V.scalar_tensor_tensor(CT[:, j % 4, :], X[:, j, :], gains[:, j:j + 1], rs, MUL, MUL
                                               ).then_inc(t_ready, 1)
                    if j >= 1:
                        n = j - 1
                        dve.wait_ge(hh_ready, base + n + 1)
                        V.scalar_tensor_tensor(HL[:, n, :], CT[:, n % 4, :], shift[:, n:n + 1], HH[:, n, :].bitcast(F32),
                                               ADD, SUB).then_inc(h_ready, 1)

            ps, free = scratch_wait("mod_a")
            V.tensor_tensor(mod[:, 0:16], ps[:, 0:16], pv("ada_b", 0, 16), ADD).then_inc(free, 1)
            dve.wait_ge(free, SCRATCH["mod_a"] // 2 + 1)
            st.link(V.scalar_tensor_tensor(lead[:, 0:8], mod[:, 8:16], 1.0, pv("mix_pre_g"), ADD, MUL))
            dve.wait_ge(x_in, 16)
            dve.wait_ge(rs_ready, 1)
            dve.wait_ge(wdt_hi, 1)
            V.tensor_tensor(WDT[:, 1, :], pv("w_dt"), WDT[:, 0, :].bitcast(F32), SUB).then_inc(wdt_ready, 1)
            make_h(mod[:, 0:8], lead[:, 0:8], RS[:, 0, :], 0)
            V.memset(ACC1, 0.0).then_inc(acc_cleared, 1)

            dve.wait_ge(dtx_ready, 1)
            V.tensor_scalar(dts[:, 2, :], dts[:, 1, :], 1.0, None, ADD).then_inc(dtw_ready, 1)
            dve.wait_ge(dtw_ready, 1)
            st.link(V.tensor_scalar(dts[:, 3, :], dts[:, 2, :], 1.0, 1e-30, SUB, ALU.max))
            st.link(V.reciprocal(dts[:, 3, :], dts[:, 3, :]))
            st.link(V.tensor_tensor(dts[:, 3, :], dts[:, 3, :], dts[:, 1, :], MUL))
            dve.wait_ge(dtl_ready, 1)
            st.mark(V.scalar_tensor_tensor(dts[:, 5, :], dts[:, 2, :], 1.0, dts[:, 1, :], ALU.is_equal, MUL))
            st.link(V.tensor_tensor(dts[:, 3, :], dts[:, 3, :], dts[:, 4, :], MUL))
            st.link(V.tensor_tensor(dts[:, 3, :], dts[:, 3, :], dts[:, 5, :], ADD))
            st.link(V.scalar_tensor_tensor(dts[:, 3, :], dts[:, 0, :], 0.0, dts[:, 3, :], ALU.max, ADD))
            st.mark(V.memset(dts[:, 2, :], 1.0))
            st.link(V.tensor_scalar(dts[:, 4, :], dts[:, 3, :], sm[0:32, 95:96], -1.0, MUL, MUL))
            V.tensor_tensor_scan(dts[:, 5, :], dts[:, 2, :], dts[:, 4, :], 0.0, MUL, ADD).then_inc(dt_ready, 1)

            u0 = PLAN.at["in1"][1]
            c_w = PAR["xconv_w"][0]
            dve.wait_ge(acc_cleared, 1)
            with st.repeat(6, 8) as i:
                for k in range(4):
                    m = i * 4 + k
                    dve.wait_ge(conv_begun, m + 1)
                    for back in (1, 2, 3):
                        dst = XBC[:, bass.ds(m, 1), back:T].rearrange("p a b -> p (a b)")
                        ins = V.scalar_tensor_tensor(dst, psL[:, (u0 + k) % 4, 0:T - back],
                                                     par[:, bass.ds(m + (c_w + (3 - back) * NXBC), 1)], dst, MUL, ADD)
                        if back < 3:
                            st.link(ins)
                        else:
                            ins.then_inc(lin_free[(u0 + k) % 4], 1)
                    dve.wait_ge(lin_free[(u0 + k) % 4], (u0 + k) // 4 + 1 + i)
                    dve.sem_inc(conv_done, 1)
                    ada_step(16 + k, part(ACC1, k), csil[:, bass.ds(i, 1)], 4, i, 4)
            for kk in (6, 7):
                for g in range(4):
                    ada_step(16 + 4 * kk + g, part(ACC1, g), csil[:, kk:kk + 1], 4)
            s_w = PAR["sconv_w"][0]

            def col(buf, j, lo=0, hi=T):
                return buf[:, bass.ds(j, 1), lo:hi].rearrange("p a b -> p (a b)")

            with st.repeat(2, 12) as i:
                for k in range(4):
                    j = i * 4 + k
                    u = u0 + 48 + k
                    dve.wait_ge(lin_done, u + 1 + i * 4)
                    dve.wait_ge(sc_c_ready, i * 4 + (k + 1))
                    V.tensor_tensor(CT[:, k % 2, :], col(SCQ, j), psL[:, u % 4, 0:T], MUL).then_inc(lin_free[u % 4], 1)
                    dve.wait_ge(lin_free[u % 4], u // 4 + 1 + i)
                    st.link(V.tensor_scalar(col(SCQ, j), CT[:, k % 2, :], par[:, bass.ds(j + (s_w + 16), 1)], None, MUL))
                    st.link(V.scalar_tensor_tensor(col(SCQ, j, 1), CT[:, k % 2, 0:T - 1], par[:, bass.ds(j + (s_w + 8), 1)],
                                                   col(SCQ, j, 1), MUL, ADD))
                    st.link(V.scalar_tensor_tensor(col(SCQ, j, 2), CT[:, k % 2, 0:T - 2], par[:, bass.ds(j + s_w, 1)],
                                                   col(SCQ, j, 2), MUL, ADD))
            with st.repeat(2, 0) as i:
                for k in range(4):
                    j = i * 4 + k
                    u = u0 + 56 + k
                    dve.wait_ge(lin_done, u + 1 + i * 4)
                    V.tensor_tensor(col(YSC, j), col(SCQ, j), psL[:, u % 4, 0:T], MUL).then_inc(lin_free[u % 4], 1)
            for k in range(4):
                u = u0 + 60 + k
                dve.wait_ge(lin_free[u % 4], u // 4 + 1)
            dve.sem_inc(ysc_ready, 8)
            ps, free = scratch_wait("mod_b")
            V.tensor_tensor(mod[:, 16:48], ps[:, 0:32], pv("ada_b", 16, 32), ADD).then_inc(free, 1)
            dve.wait_ge(free, SCRATCH["mod_b"] // 2 + 1)
            st.mark(V.tensor_tensor(lead[:, 8:16], mod[:, 16:24], pv("mix_post_g"), MUL))
            st.mark(V.scalar_tensor_tensor(lead[:, 16:24], mod[:, 32:40], 1.0, pv("ffn_pre_g"), ADD, MUL))
            st.link(V.tensor_tensor(lead[:, 24:32], mod[:, 40:48], pv("ffn_post_g"), MUL))

            dve.wait_ge(cd_ready, 1)
            dve.wait_ge(cum_stored, 16)
            for g in range(NGRP):
                ps, free = scratch_wait("scores", g)
                st.mark(V.tensor_tensor(SCM[:, g, 0:P], ps[:, 0:P], pv("causal01"), MUL))
                st.mark(V.tensor_copy(SCM[:, g, P:256], ps[:, P:256]))
                V.tensor_tensor(SCM[:, g, 256:384], ps[:, 256:384], pv("causal01"), MUL).then_inc(free, 1)
                dve.wait_ge(free, (SCRATCH["scores"] + g) // 2 + 1)
            dve.wait_ge(dve_step, st.n)
            dve.wait_ge(xbc_ready, 8)
            for n in range(4):
                dve.wait_ge(lin_free[n], 40 // 4)

            def y_out(j):
                n = OUT_Y + j
                dve.wait_ge(m_used, j + 1)
                V.scalar_tensor_tensor(XBC[:, j, :], XBC[:, j, :], pv("dskip", j, 1), psO[:, n % 2, 0:T], MUL,
                                       ADD).then_inc(o_free[n % 2], 1)
                dve.wait_ge(o_free[n % 2], n // 2 + 1)
                V.tensor_tensor(Z[:, j, :], XBC[:, j, :], Z[:, j, :], MUL).then_inc(y_ready, 1)

            def yn(g):
                dve.wait_ge(rs_ready, 2 + g)
                dve.wait_ge(y_ready, 4 * g + 4)
                for j in range(4 * g, 4 * g + 4):
                    V.scalar_tensor_tensor(Z[:, j, :], Z[:, j, :], pv("ssd_norm_g", j, 1), RS[:, g % 2, :], MUL,
                                           MUL).then_inc(yn_ready, 1)

            NPAIR = HEADS1 // 2
            for p in range(NPAIR + 1):
                if p < NPAIR:
                    hg = p // 2
                    if p % 2 == 0:
                        dve.wait_ge(cum_in[hg % 2], 16 * (hg // 2 + 1))
                    if p >= 2:
                        dve.wait_ge(m_ready, p - 1)
                    for e in range(2):
                        h = 2 * p + e
                        bc = CUMB[:, hg % 2, (h % 4) * T:(h % 4 + 1) * T]
                        se = SE[:, p % 2, 384 * e:384 * e + 384]
                        st.mark(V.tensor_scalar(se[:, 0:256], bc, CD[:, 0, h:h + 1], 0.0, SUB, ALU.min))
                        last = V.tensor_scalar(se[:, 256:384], bc[:, P:T], CD[:, 1, h:h + 1], 0.0, SUB, ALU.min)
                        if e == 0:
                            st.mark(last)
                    last.then_inc(diff_ready, 1)
                if p >= 1:
                    n = p - 1
                    g = n // 4
                    dve.wait_ge(decay_ready, n + 1)
                    if n >= 2:
                        dve.wait_ge(m_used, n - 1)
                    for e in range(2):
                        h = 2 * n + e
                        se, m = (x[:, n % 2, 384 * e:384 * e + 384] for x in (SE, SM))
                        st.mark(V.scalar_tensor_tensor(m[:, 0:256], se[:, 0:256], CD[:, 2, h:h + 1], SCM[:, g, 0:256], MUL, MUL))
                        last = V.scalar_tensor_tensor(m[:, 256:384], se[:, 256:384], CD[:, 3, h:h + 1],
                                                      SCM[:, g, 256:384], MUL, MUL)
                        if e == 0:
                            st.mark(last)
                    last.then_inc(m_ready, 1)
                if p >= 2:
                    y_out(p - 2)
            y_out(NPAIR - 1)
            for g in range(NGRP):
                yn(g)
            for g in range(NGRP):
                dve.wait_ge(zh_ready, g + 1)
                V.tensor_tensor(ZL[:, 4 * g:4 * g + 4, :].rearrange("p a b -> p (a b)"),
                                Z[:, 4 * g:4 * g + 4, :].rearrange("p a b -> p (a b)"),
                                ZH[:, 4 * g:4 * g + 4, :].rearrange("p a b -> p (a b)").bitcast(F32), SUB).then_inc(zl_ready, 1)
            dve.wait_ge(yh_ready, 1)
            V.tensor_tensor(YL.rearrange("p a b -> p (a b)"), YSC.rearrange("p a b -> p (a b)"),
                            YH.rearrange("p a b -> p (a b)").bitcast(F32), SUB).then_inc(yl_ready, 1)

            u0 = PLAN.at["ssd_out"][1]
            dve.wait_ge(gates_ready, 2)
            dve.wait_ge(zl_ready, 4)
            for m in range(8):
                u = u0 + m
                V.tensor_tensor(MIXIN[:, m, :], G1[:, m, :], lin(u), MUL).then_inc(lin_free[u % 4], 1)
                dve.wait_ge(lin_free[u % 4], u // 4 + 1)
            u0 = PLAN.at["sc_out"][1]
            for m in range(8):
                u = u0 + m
                V.tensor_tensor(CT[:, m % 2, :], G1[:, 8 + m, :], lin(u), MUL).then_inc(lin_free[u % 4], 1)
                dve.wait_ge(lin_free[u % 4], u // 4 + 1)
                V.tensor_tensor(MIXIN[:, m, :], MIXIN[:, m, :], CT[:, m % 2, :], ADD).then_inc(mixin_ready, 1)

            for m in range(8):
                dve.wait_ge(mh_ready, m + 1)
                if m == 0:
                    dve.wait_ge(yl_ready, 1)
                V.tensor_tensor(ML[:, m, :], MIXIN[:, m, :], MH[:, m, :].bitcast(F32), SUB).then_inc(ml_ready, 1)

            def add_normed(src, gains, rs):
                for j in range(KD):
                    st.link(V.scalar_tensor_tensor(CT[:, j % 2, :], src[:, j, :], gains[:, j:j + 1], rs, MUL, MUL))
                    V.tensor_tensor(X[:, j, :], X[:, j, :], CT[:, j % 2, :], ADD).then_inc(x_ready, 1)

            dve.wait_ge(mixin_ready, 8)
            dve.wait_ge(rs_ready, 6)
            add_normed(MIX, lead[:, 8:16], RS[:, 0, :])
            dve.wait_ge(x_ready, 8)
            dve.wait_ge(rs_ready, 7)
            make_h(mod[:, 24:32], lead[:, 16:24], RS[:, 1, :], 8)

            def ffn(name, wname, base, between):
                u0 = PLAN.at[name][1]
                w0 = PAR[wname][0]

                def conv(j, slot, it=0):
                    us = [u0 + 2 * j, u0 + 2 * j + 1]
                    for back in (1, 2):
                        for b in range(2):
                            if back == 1:
                                dve.wait_ge(f_begun, 2 * base + 2 * j + b + 1 + it * 2)
                            dst = CT[:, 2 * slot + b, back:T]
                            ins = V.scalar_tensor_tensor(
                                dst, psL[:, us[b] % 4, 0:T - back],
                                par[:, bass.ds(w0 + (2 - back) * 44 + b * KF + j + it, 1)], dst, MUL, ADD)
                            if back == 1:
                                st.mark(ins)
                            else:
                                ins.then_inc(lin_free[us[b] % 4], 1)
                        if back == 1:
                            dve.wait_ge(dve_step, st.loop + st.n)
                    for b in range(2):
                        dve.wait_ge(lin_free[us[b] % 4], us[b] // 4 + 1 + (it_half if it is not 0 else 0))
                    dve.sem_inc(f_conv, 1)

                def product(j, slot, it=0):
                    dve.wait_ge(f_silu, base + j + 1 + it)
                    V.tensor_tensor(CT[:, 2 * slot, :], CT[:, 2 * slot, :], CT[:, 2 * slot + 1, :], MUL
                                    ).then_inc(f_prod, 1)
                    dve.wait_ge(f_hi, base + j + 1 + it)
                    V.tensor_tensor(FAL[:, bass.ds(j + it, 1), :].rearrange("p a b -> p (a b)"), CT[:, 2 * slot, :],
                                    FAH[:, bass.ds(j + it, 1), :].rearrange("p a b -> p (a b)").bitcast(F32), SUB
                                    ).then_inc(f_act, 1)

                it_half = 0
                conv(0, 0)
                conv(1, 1)
                product(0, 0)
                if between:
                    rounds = 4
                    with st.repeat(rounds, 8) as i:
                        for q in range(2):
                            it_half = i * 2
                            conv(2 + 2 * q, 0, i * 4)
                            product(1 + 2 * q, 1, i * 4)
                            between(i, 2 * q)
                            conv(3 + 2 * q, 1, i * 4)
                            product(2 + 2 * q, 0, i * 4)
                            between(i, 2 * q + 1)
                    for j in range(18, 22):
                        conv(j, j % 2)
                        product(j - 1, (j - 1) % 2)
                else:
                    with st.repeat(10, 4) as i:
                        it_half = i
                        conv(2, 0, i * 2)
                        product(1, 1, i * 2)
                        conv(3, 1, i * 2)
                        product(2, 0, i * 2)
                product(21, 1)

            V.memset(ACC2, 0.0).then_inc(acc_cleared, 1)
            dve.wait_ge(acc_cleared, 2)

            def ada_between(i, q):
                for s in range(3):
                    n = 3 * q + s
                    ada_step(48 + n, part(ACC2, n % 6), csil[:, bass.ds(i * 2 + (8 + n // 6), 1)], 6, i, 12)

            ffn("up1", "fconv_w", 0, ada_between)
            dve.wait_ge(rs_ready, 8)
            dve.wait_ge(f_act, KF)
            add_normed(FO, lead[:, 24:32], RS[:, 0, :])

            ps, free = scratch_wait("mod_2")
            V.tensor_tensor(mod[:, :], ps[:, 0:48], pv("b_ada_2"), ADD).then_inc(free, 1)
            dve.wait_ge(free, SCRATCH["mod_2"] // 2 + 1)
            st.mark(V.scalar_tensor_tensor(lead[:, 0:8], mod[:, 8:16], 1.0, pv("attn_norm_2"), ADD, MUL))
            st.link(V.scalar_tensor_tensor(lead[:, 8:16], mod[:, 32:40], 1.0, pv("ffn_norm_2"), ADD, MUL))
            dve.wait_ge(x_ready, 16)
            dve.wait_ge(rs_ready, 9)
            make_h(mod[:, 0:8], lead[:, 0:8], RS[:, 1, :], 16)
            u0 = PLAN.at["tok2"][1]
            for c in range(6):
                for t in range(2):
                    u = u0 + 2 * c + t
                    dve.wait_ge(tok_sq, 4 * c + 2 * t + 2)
                    gain = pv("q_gain" if c < 4 else "ks_gain" if c == 4 else "kw_gain")
                    dst = QTOK[:, t, c * 256:(c + 1) * 256] if c < 4 else KTOK[:, t, (c - 4) * 256:(c - 3) * 256]
                    V.tensor_tensor(dst.rearrange("p (h d) -> p h d", d=HD),
                                    psL[:, u % 4, 0:256].rearrange("p (h d) -> p h d", d=HD),
                                    gain.unsqueeze(1).to_broadcast([P, 2, HD]), MUL).then_inc(lin_free[u % 4], 1)
                    dve.wait_ge(lin_free[u % 4], u // 4 + 1)
            dve.wait_ge(tok_ready, 1)
            dve.wait_ge(trs, 1)
            for t in range(2):
                st.mark(V.tensor_scalar(sm[:, t * 12:t * 12 + 8], sm[:, t * 12:t * 12 + 8], float(HD) ** -0.5, None, MUL))
            dve.wait_ge(dve_step, st.n)

            def rope(buf, heads, width, cos, sin):
                half = width // 2
                tmp = SQ[:, 0:heads * width].rearrange("p (h d) -> p h d", d=width)
                st.mark(V.tensor_tensor(tmp[:, :, 0:half], buf[:, :, half:width],
                                        sin[:, 0:half].unsqueeze(1).to_broadcast([P, heads, half]), MUL))
                st.link(V.tensor_tensor(tmp[:, :, half:width], buf[:, :, 0:half],
                                        sin[:, half:width].unsqueeze(1).to_broadcast([P, heads, half]), MUL))
                st.link(V.tensor_tensor(buf, buf, cos.unsqueeze(1).to_broadcast([P, heads, width]), MUL))
                return V.tensor_tensor(buf, buf, tmp, ADD)

            def heads_of(ap, d):
                return ap.rearrange("p (h d) -> p h d", d=d)

            dve.wait_ge(s_done, SCRATCH["stat_ckv"] + 1)
            dve.wait_ge(feat_ready, 1)
            dve.wait_ge(rs_ready, 11)
            for j in range(3):
                V.scalar_tensor_tensor(CQ[:, j, :], CQ[:, j, :], pv("cq_g", j, 1), RS[:, 0, :], MUL, MUL).then_inc(cqn_ready, 1)
            for j in range(2):
                V.scalar_tensor_tensor(CKV[:, j, :], CKV[:, j, :], pv("ckv_g", j, 1), RS[:, 1, :], MUL, MUL).then_inc(cqn_ready, 1)

            for t in range(2):
                cos, sin = pv("cos", t * HD, HD), pv("sin", t * HD, HD)
                q3 = heads_of(QTOK[:, t, :], HD)
                st.link(V.tensor_tensor(q3, q3, sm[:, t * 12:t * 12 + 8].unsqueeze(2).to_broadcast([P, 8, HD]), MUL))
                rope(q3, 8, HD, cos, sin).then_inc(troped, 1)
                dve.wait_ge(troped, 2 * t + 1)
                k3 = heads_of(KTOK[:, t, :], HD)
                st.link(V.tensor_tensor(k3[:, 0:4, :], k3[:, 0:4, :],
                                        sm[:, t * 12 + 8:t * 12 + 12].unsqueeze(2).to_broadcast([P, 4, HD]), MUL))
                rope(k3, 6, HD, cos, sin).then_inc(troped, 1)
                dve.wait_ge(troped, 2 * t + 2)

            for kv in range(2):
                if kv == 0:
                    dve.wait_ge(turned, 7)
                for g in range(2):
                    src = KT[:, 4 + g, :] if kv == 0 else VC[:, g, :]
                    pe_cols = "k_pe" if kv == 0 else "v_pe"
                    for part in range(2):
                        dst = CB[kv][:, 16 * part:16 * part + 16, g * NCMP:(g + 1) * NCMP]
                        win = src[:, 16 * part:16 * part + 240].rearrange("p (n l) -> p l n", l=16)
                        ins = V.tensor_tensor(dst, win, pv(pe_cols, 16 * part, 16).unsqueeze(2).to_broadcast([P, 16, NCMP]), ADD)
                        st.mark(ins)
                dve.wait_ge(dve_step, st.n)
                dve.sem_inc(cb_ready, 1)

            dve.wait_ge(mla_tok, 1)
            dve.wait_ge(ng_ready, 1)
            for t in range(2):
                q3 = heads_of(QB[:, t, :], QK)
                sq3 = heads_of(SQ[:, 0:1536], QK)
                st.link(V.tensor_tensor(sq3, q3, q3, MUL))
                st.link(V.tensor_reduce(mlars[:, 16 * t:16 * t + 8], sq3, AX.X, ADD))
                k3 = heads_of(KB[:, t, :], QK)
                sk3 = heads_of(SQ[:, 0:1024], HD)
                st.link(V.tensor_tensor(sk3, k3[:, :, 0:HD], k3[:, :, 0:HD], MUL))
                st.link(V.tensor_reduce(mlars[:, 16 * t + 8:16 * t + 16], sk3, AX.X, ADD))
                st.link(V.tensor_scalar(mlars[:, 16 * t + 8:16 * t + 16], mlars[:, 16 * t + 8:16 * t + 16],
                                        sm[:, 24 + t:25 + t], None, ADD))
            dve.sem_inc(tsum, 1)
            dve.wait_ge(mla_sq, 1)
            st.mark(V.tensor_scalar(mlars[:, 0:8], mlars[:, 0:8], float(QK) ** -0.5, None, MUL))
            st.link(V.tensor_scalar(mlars[:, 16:24], mlars[:, 16:24], float(QK) ** -0.5, None, MUL))
            for t in range(2):
                cos, sin = pv("mcos", t * ROPE, ROPE), pv("msin", t * ROPE, ROPE)
                q3 = heads_of(QB[:, t, :], QK)
                st.link(V.tensor_tensor(q3, q3, pv("mq_gain").unsqueeze(1).to_broadcast([P, 8, QK]), MUL))
                st.link(V.tensor_tensor(q3, q3, mlars[:, 16 * t:16 * t + 8].unsqueeze(2).to_broadcast([P, 8, QK]), MUL))
                st.link(rope(q3[:, :, HD:QK], 8, ROPE, cos, sin))
                dve.sem_inc(troped, 1)
                k3 = heads_of(KB[:, t, :], QK)
                st.link(V.tensor_tensor(k3[:, :, 0:HD], k3[:, :, 0:HD],
                                        pv("mk_gain", 0, HD).unsqueeze(1).to_broadcast([P, 8, HD]), MUL))
                kr = KR[:, t, :].unsqueeze(1)
                st.link(V.tensor_tensor(KR[:, t, :], KR[:, t, :], pv("mk_gain", HD, ROPE), MUL))
                st.link(rope(kr, 1, ROPE, cos, sin))
                st.link(V.tensor_copy(k3[:, :, HD:QK], kr.to_broadcast([P, 8, ROPE])))
                st.link(V.tensor_tensor(k3, k3, mlars[:, 16 * t + 8:16 * t + 16].unsqueeze(2).to_broadcast([P, 8, QK]), MUL))
                dve.sem_inc(troped, 1)

            ps, free = scratch_wait("kc")
            dve.wait_ge(kc_rs, 1)
            V.scalar_tensor_tensor(KCN, ps[0:30, 0:P], sm[0:30, 60:61], pv("kc_gain")[0:30, :], MUL, MUL).then_inc(free, 1)
            dve.wait_ge(free, SCRATCH["kc"] // 2 + 1)
            dve.sem_inc(kcn_ready, 1)
            u = PLAN.at["cmp_scores"][1]
            dve.wait_ge(lin_done, u + 1)
            cs4 = CS.rearrange("p (h t n) -> p h t n", t=2, n=NCMP)
            cs3 = CS.rearrange("p (m n) -> p m n", n=NCMP)
            V.tensor_tensor(cs4, psL[:, u % 4, 0:240].rearrange("p (h t n) -> p h t n", t=2, n=NCMP),
                            pv("cmask_add").rearrange("p (t n) -> p t n", n=NCMP).unsqueeze(1).to_broadcast([P, 8, 2, NCMP]),
                            ADD).then_inc(lin_free[u % 4], 1)
            dve.wait_ge(lin_free[u % 4], u // 4 + 1)
            st.link(V.tensor_reduce(cmx[:, 0:16], cs3, AX.X, ALU.max))
            st.link(V.tensor_tensor(cs3, cs3, cmx[:, 0:16].unsqueeze(2).to_broadcast([P, 16, NCMP]), SUB))
            dve.sem_inc(cs_ready, 1)
            dve.wait_ge(ce_ready, 1)
            st.link(V.tensor_reduce(cmx[:, 0:16], cs3, AX.X, ADD))
            st.link(V.reciprocal(cmx[:, 16:32], cmx[:, 0:16]))
            gate0 = GT[:, :, :].rearrange("p t (h b) -> p h t b", b=3)[:, :, :, 0]
            st.link(V.tensor_tensor(cmx[:, 0:16].rearrange("p (h t) -> p h t", t=2),
                                    cmx[:, 16:32].rearrange("p (h t) -> p h t", t=2), gate0, MUL))
            st.link(V.tensor_tensor(cs3, cs3, cmx[:, 0:16].unsqueeze(2).to_broadcast([P, 16, NCMP]), MUL))
            st.link(V.tensor_tensor(cs4, cs4,
                                    pv("cmask01").rearrange("p (t n) -> p t n", n=NCMP).unsqueeze(1).to_broadcast([P, 8, 2, NCMP]),
                                    MUL))
            dve.sem_inc(cp_ready, 1)

            def softmax(count, p0, gated, outs):
                for i in range(count + 1):
                    if i < count:
                        n = p0 + i
                        u = PLAN.at["nsa_scores"][1] + n
                        dve.wait_ge(lin_done, u + 1)
                        b = 26 + 4 * (n % 2)
                        st.mark(V.tensor_reduce(sm[:, b:b + 1], psL[:, u % 4, 0:P], AX.X, ALU.max, negate=True))
                        st.link(V.tensor_reduce(sm[:, b + 1:b + 2], psL[:, u % 4, P:384], AX.X, ALU.max, negate=True))
                        dve.sem_inc(max_ready, 1)
                    if i >= 1:
                        n = p0 + i - 1
                        b = 28 + 4 * (n % 2)
                        rc = cmx[:, 32 + 2 * (n % 2):34 + 2 * (n % 2)]
                        dve.wait_ge(exp_ready, n + 1)
                        st.link(V.reciprocal(rc, sm[:, b:b + 2]))
                        if gated:
                            h, br = divmod(n, 2)
                            st.link(V.tensor_tensor(rc, rc, GT[:, :, 3 * h + 1 + br], MUL))
                        st.mark(V.tensor_scalar(PR[:, n % 3, 0:P], PR[:, n % 3, 0:P], rc[:, 0:1], None, MUL))
                        st.link(V.tensor_scalar(PR[:, n % 3, P:384], PR[:, n % 3, P:384], rc[:, 1:2], None, MUL))
                        dve.sem_inc(p_ready, 1)
                    outs(i)

            def nsa_outs(i):
                for h in ([(i - 4) // 2] if i >= 4 and i % 2 == 0 and i < 16 else [6, 7] if i == 16 else []):
                    n = OUT_NSA + h
                    dve.wait_ge(pt_used, 2 * h + 2)
                    V.tensor_tensor(OM[:, h, :], G2[:, h, :], psO[:, n % 2, 0:T], MUL).then_inc(o_free[n % 2], 1)

            def mla_outs(i):
                hs = [i - 3] if i < 8 else [5, 6, 7]
                for h in hs:
                    if h < 0:
                        continue
                    n = OUT_MLA + h
                    dve.wait_ge(pt_used, 16 + h + 1)
                    V.tensor_tensor(CT[:, h % 2, :], G2[:, 8 + h, :], psO[:, n % 2, 0:T], MUL).then_inc(o_free[n % 2], 1)
                    dve.wait_ge(o_free[n % 2], n // 2 + 1)
                    V.tensor_tensor(OM[:, h, :], OM[:, h, :], CT[:, h % 2, :], ADD).then_inc(om_ready, 1)

            dve.wait_ge(gates_ready, 2)
            softmax(16, 0, True, nsa_outs)
            for n in (OUT_NSA + 6, OUT_NSA + 7):
                dve.wait_ge(o_free[n % 2], n // 2 + 1)
            dve.sem_inc(om_ready, 8)
            softmax(8, 16, False, mla_outs)
            for h in range(NH):
                dve.wait_ge(omh_ready, h + 1)
                V.tensor_tensor(OML[:, h, :], OM[:, h, :], OMH[:, h, :].bitcast(F32), SUB).then_inc(oml_ready, 1)

            def add_gated(name, gates):
                u0 = PLAN.at[name][1]
                for m in range(8):
                    u = u0 + m
                    V.scalar_tensor_tensor(X[:, m, :], lin(u), gates[:, m:m + 1], X[:, m, :], MUL, ADD
                                           ).then_inc(lin_free[u % 4], 1)
                    dve.wait_ge(lin_free[u % 4], u // 4 + 1)
                    dve.sem_inc(x_ready, 1)

            add_gated("o2", mod[:, 16:24])
            dve.wait_ge(rs_ready, 12)
            make_h(mod[:, 24:32], lead[:, 8:16], RS[:, 0, :], 24)
            ffn("up2", "fconv_w_2", KF, None)
            add_gated("down2", mod[:, 40:48])


def _pack(w):
    k, n = w.shape
    return w.reshape(k // P, P, n).transpose(1, 0, 2).reshape(P, -1)


def _cols(v):
    return v.reshape(-1, P).T


def _swap(a):
    return np.concatenate([a[..., FF:], a[..., :FF]], axis=-1)


def _weights(i):
    chunks = []

    def m_blocks(w):
        for m in range(w.shape[1] // P):
            for k in range(0, w.shape[0], SLOT):
                chunks.append(_pack(w[k:k + SLOT, m * P:(m + 1) * P]))

    def pairs(w):
        return np.stack([w[:, :FF].reshape(D, KF, P), w[:, FF:].reshape(D, KF, P)], axis=2).reshape(D, 2 * FF)

    w = i["w_in"][0]
    m_blocks(np.concatenate([w[:, 2048:5120], w[:, 0:2048], w[:, 6176:7200], w[:, 7200:8224], w[:, 5152:6176],
                             w[:, 8224:10272]], axis=1))
    m_blocks(i["w_ssd_out"][0])
    m_blocks(i["w_sc_out"][0])
    m_blocks(i["w_o"][0])
    m_blocks(pairs(i["w_up"][0]))
    m_blocks(i["w_down"][0])
    w = i["w_in_2"][0]
    q, kc, vc, ks, vs, kw, vw = (w[:, 0:1024],) + tuple(w[:, 1024 + 256 * n:1280 + 256 * n] for n in range(6))
    ng, cq, ckv, kr, bg = w[:, 2560:2584], w[:, 2584:2968], w[:, 2968:3224], w[:, 3224:3288], w[:, 3288:5336]
    tok = np.concatenate([q, ks, kw, kc, vs, vw], axis=1)
    for c in range(9):
        for half in range(2):
            chunks.append(_pack(tok[half * 512:(half + 1) * 512, c * 256:(c + 1) * 256]))
    chunks.append(_pack(np.concatenate([kr, ng], axis=1)))
    m_blocks(np.concatenate([vc, cq, ckv, bg], axis=1))
    for h in range(NH):
        chunks.append(_pack(i["w_uq_2"][0][:, h * QK:(h + 1) * QK]))
    for c in range(4):
        chunks.append(_pack(i["w_ukv_2"][0][:, c * 512:(c + 1) * 512]))
    for name in ("cmp_k_w1_2", "cmp_v_w1_2"):
        m_blocks(i[name][0])
    m_blocks(i["w_o_2"][0])
    m_blocks(pairs(_swap(i["w_up_2"][0])))
    m_blocks(i["w_down_2"][0])
    assert len(chunks) == CHUNKS and all(c.shape[1] == n for c, n in zip(chunks, PLAN.cols))
    out = np.zeros((CHUNKS, P, SLOT), np.float32)
    for c, a in enumerate(chunks):
        out[c, :, :a.shape[1]] = a
    return out.reshape(CHUNKS * P, SLOT)


def _ada(i):
    a, b = (w.reshape(KD, P, ADA_GROUPS, ADA_COLS).transpose(0, 2, 1, 3) for w in (i["ada_w"][0], i["w_ada_2"][0]))
    return np.concatenate([a[:, :2].reshape(-1, ADA_COLS), a[:, 2:].reshape(-1, ADA_COLS), b.reshape(-1, ADA_COLS)])


def _rope(width):
    half = width // 2
    inv = (10000.0 ** (-np.arange(half, dtype=np.float32) * np.float32(2.0) / width)).astype(np.float32)
    ang = (np.arange(T, dtype=np.float32)[:, None] * inv[None, :]).astype(np.float32)
    cos, sin = np.cos(ang), np.sin(ang)
    tile = lambda a: a.reshape(2, P, width).transpose(1, 0, 2).reshape(P, -1).astype(np.float32)
    return tile(np.concatenate([cos, cos], axis=1)), tile(np.concatenate([-sin, sin], axis=1))


def _params(i):
    def rows(v):
        out = np.zeros((P, 1), np.float32)
        out[:len(v), 0] = v
        return out

    def taps(w):
        return np.concatenate([_cols(row) for row in w], axis=1)

    def wide(v):
        return np.broadcast_to(v, (P, len(v)))

    q, k = np.arange(P)[:, None], np.arange(P)[None, :]
    ends = 16 * np.arange(NCMP) + 31
    seen = (ends[None, None, :] <= (np.arange(2)[None, :, None] * P + np.arange(P)[:, None, None])).reshape(P, -1)
    cos, sin = _rope(HD)
    mcos, msin = _rope(ROPE)
    f = lambda a: a.astype(np.float32)
    v = {
        "c": _cols(i["c"][0]), "c_2": _cols(i["c_2"][0]), "ada_b": _cols(i["ada_b"][0]),
        "mix_pre_g": _cols(i["mix_pre_g"][0]), "mix_post_g": _cols(i["mix_post_g"][0]),
        "xconv_w": taps(i["ssd_conv_w"][0]), "xconv_b": _cols(i["ssd_conv_b"][0]),
        "dskip": _cols(np.repeat(i["ssd_d"][0], 64)), "ssd_norm_g": _cols(i["ssd_norm_g"][0]),
        "sconv_w": taps(i["sc_conv_w"][0]), "ffn_pre_g": _cols(i["ffn_pre_g"][0]), "ffn_post_g": _cols(i["ffn_post_g"][0]),
        "fconv_w": taps(i["ffn_conv_w"][0]), "fconv_b": _cols(i["ffn_conv_b"][0]),
        "dt_bias": rows(i["ssd_dt_bias"][0]), "a_log": rows(i["ssd_a_log"][0]), "w_dt": _pack(i["w_in"][0][:, 5120:5152]),
        "b_ada_2": _cols(i["b_ada_2"][0]), "attn_norm_2": _cols(i["attn_norm_2"][0]), "ffn_norm_2": _cols(i["ffn_norm_2"][0]),
        "fconv_w_2": taps(_swap(i["w_conv_2"][0])), "fconv_b_2": _cols(_swap(i["b_conv_2"][0])),
        "k_pe": i["cmp_k_pe_2"][0].T, "v_pe": i["cmp_v_pe_2"][0].T,
        "k_w2": _pack(i["cmp_k_w2_2"][0]), "v_w2": _pack(i["cmp_v_w2_2"][0]),
        "cq_g": _cols(i["mla_cq_norm_2"][0]), "ckv_g": _cols(i["mla_ckv_norm_2"][0]),
        "q_gain": wide(i["nsa_q_norm_2"][0]), "ks_gain": wide(i["nsa_ks_norm_2"][0]), "kw_gain": wide(i["nsa_kw_norm_2"][0]),
        "kc_gain": wide(i["nsa_kc_norm_2"][0]), "mq_gain": wide(i["mla_q_norm_2"][0]), "mk_gain": wide(i["mla_k_norm_2"][0]),
        "ident": np.eye(P, dtype=np.float32), "ones": np.ones((P, P), np.float32),
        "causal_add": f(np.where(k <= q, 0.0, -1e30)), "causal01": f(k >= q),
        "cos": cos, "sin": sin, "mcos": mcos, "msin": msin,
        "cmask_add": f(np.where(seen, 0.0, -1e30)), "cmask01": f(seen),
    }
    assert all(v[n].shape == (P, c) for n, c in PAR_SPEC), [(n, v[n].shape) for n, c in PAR_SPEC if v[n].shape != (P, c)]
    return np.ascontiguousarray(np.concatenate([v[n] for n, _ in PAR_SPEC], axis=1))


def kernel(**inputs):
    import concourse.bacc as bacc
    from concourse.bass_utils import run_bass_kernel_spmd

    inputs = {k: np.asarray(v) for k, v in inputs.items()}
    arrays = {
        "x_t": np.ascontiguousarray(inputs["x"][0].reshape(T, KD, P).transpose(2, 1, 0)),
        "params": _params(inputs), "ada_w": np.ascontiguousarray(_ada(inputs)), "wts": _weights(inputs),
    }
    nc = bacc.Bacc("TRN2", target_bir_lowering=False, num_devices=1)
    aps = [nc.dram_tensor(n, a.shape, mybir.dt.from_np(a.dtype), kind="ExternalInput").ap() for n, a in arrays.items()]
    out = nc.dram_tensor("out_t", (P, KD * T), mybir.dt.float32, kind="ExternalOutput").ap()
    build(nc, *aps, out)
    r = run_bass_kernel_spmd(nc, [arrays], core_ids=[0])
    y = r.results[0]["out_t"].reshape(P, KD, T).transpose(2, 1, 0).reshape(1, T, D)
    return np.ascontiguousarray(y)
```

```python
from contextlib import ExitStack, contextmanager

import concourse.bass as bass
import numpy as np
from concourse import mybir

P = 128
T = 256
D = 1024
KD = D // P
FF = 2816
KF = FF // P
EPS = 1e-6

NXBC = 24
NZ = 16
HEADS1 = 32
NGRP = 4
NH = 8
NCMP = 15
HD = 128
QK = 192
ROPE = 64

SLOTS = 4
SLOT = 8 * P
ADA_SLOTS = 4
ADA_COLS = 1024
ADA_GROUPS = 6 * D // ADA_COLS


class Stream:

    def __init__(self):
        self.cols, self.done_after, self.split_at, self.chunk_of, self.units, self.at = [], [], [], [], 0, {}

    def add(self, name, groups, cols, units=1, plain=False):
        self.at[name] = (len(self.cols), self.units)
        for _ in range(groups):
            self.units += units
            for n in cols:
                if not plain:
                    self.chunk_of.append(len(self.cols))
                self.split_at.append(None if plain else len(self.chunk_of) - 1)
                self.cols.append(n)
                self.done_after.append(self.units)

    def bare(self, name, units):
        self.at[name] = (len(self.cols), self.units)
        self.units += units

    def q(self, name):
        return self.split_at[self.at[name][0]]

    def splittable(self, q):
        if q < SLOTS:
            return 0
        before = self.chunk_of[q] - SLOTS
        return max(self.done_after[self.chunk_of[q - SLOTS]], self.done_after[before])


PLAN = Stream()
PLAN.add("in1", 80, [SLOT])
PLAN.add("sc_out", 8, [SLOT])
PLAN.add("ssd_out", 8, [SLOT, SLOT])
PLAN.add("o1", 8, [SLOT])
PLAN.add("up1", 44, [SLOT])
PLAN.add("down1", 8, [SLOT, SLOT, 6 * P])
PLAN.add("tok2", 9, [SLOT, SLOT], 2)
PLAN.add("mix2", 1, [88 * KD], 2)
PLAN.add("feat2", 23, [SLOT])
PLAN.add("uq", 8, [3 * QK], 1, True)
PLAN.add("ukv", 4, [SLOT], 2, True)
PLAN.bare("cmp", 2)
PLAN.bare("cmp_scores", 1)
PLAN.bare("nsa_scores", 2 * NH)
PLAN.bare("mla_scores", NH)
PLAN.add("o2", 8, [SLOT])
PLAN.add("up2", 44, [SLOT])
PLAN.add("down2", 8, [SLOT, SLOT, 6 * P])
CHUNKS, SPLITS = len(PLAN.cols), len(PLAN.chunk_of)
CMP_ROW = CHUNKS * P
assert all((c - q) % SLOTS == 0 for q, c in enumerate(PLAN.chunk_of))

SCRATCH = {}
_n = 0
for _name, _count in [("stat_mix", 1), ("mod_scale", 1), ("mod_shift", 1), ("dt", 1), ("mod_b", 1), ("dt_turn", 1), ("x_turn", 8),
                      ("scores", 4), ("gnorm", 4), ("stat_o1", 1), ("stat_ffn1", 1), ("stat_down1", 1),
                      ("mod_2a", 1), ("stat_attn", 1), ("stat_cq", 1), ("stat_ckv", 1), ("mod_2b", 1), ("nsa_turn", 7),
                      ("hid_k", 1), ("kc", 1), ("kc_turn", 1), ("hid_v", 1), ("vc", 1), ("cmp_turn", 4), ("nsa_p", 16),
                      ("mla_turn", 16), ("mla_p", 8), ("stat_ffn2", 1)]:
    SCRATCH[_name] = _n
    _n += _count

OUT_Y, OUT_NSA, OUT_MLA = 0, 16, 24

PAR_SPEC = [
    ("c", 8), ("c_2", 8), ("ada_b", 48), ("mix_pre_g", 8), ("ones", P), ("w_dt", KD * HEADS1),
    ("mix_post_g", 8),
    ("xconv_w", 4 * NXBC), ("xconv_b", NXBC), ("dskip", 16), ("ssd_norm_g", 16), ("sconv_w", 24),
    ("ffn_pre_g", 8), ("ffn_post_g", 8), ("fconv_w", 132), ("fconv_b", 44),
    ("dt_bias", 1), ("a_log", 1),
    ("b_ada_2", 48), ("attn_norm_2", 8), ("ffn_norm_2", 8), ("fconv_w_2", 132), ("fconv_b_2", 44),
    ("k_pe", 32), ("v_pe", 32), ("k_w2", 256), ("v_w2", 256), ("cq_g", 3), ("ckv_g", 2),
    ("q_gain", 128), ("ks_gain", 128), ("kw_gain", 128), ("kc_gain", 128), ("mq_gain", QK), ("mk_gain", QK),
    ("ident", P), ("causal_add", P), ("causal01", P),
    ("cos", 2 * 128), ("sin", 2 * 128), ("mcos", 2 * 64), ("msin", 2 * 64),
    ("cmask_add", 2 * NCMP), ("cmask01", 2 * NCMP),
]
PAR = {}
_n = 0
for _name, _count in PAR_SPEC:
    PAR[_name] = (_n, _count)
    _n += _count
NPAR = _n
PAR_FIRST = PAR["mix_post_g"][0]


def build(nc, x_t, par_in, ada_w, wts, out_t):
    F32, F32R, BF16 = mybir.dt.float32, mybir.dt.float32r, mybir.dt.bfloat16
    ALU, ACT, AX = mybir.AluOpType, mybir.ActivationFunctionType, mybir.AxisListType
    MUL, ADD, SUB = ALU.mult, ALU.add, ALU.subtract
    ctx = ExitStack()
    with ctx:
        def sb(name, shape, dt=F32):
            return ctx.enter_context(nc.sbuf_tensor(name, shape, dt))

        def sem(name):
            return ctx.enter_context(nc.semaphore(name))

        ring = sb("ring", [P, SLOTS, SLOT])
        with nc.sbuf_tensor("WH", [P, SLOTS, SLOT], F32R) as WH:
            pass
        WHF = sb("WHF", [P, SLOTS, SLOT])
        with nc.sbuf_tensor("WL", [P, SLOTS, SLOT], F32R) as WL:
            pass
        WLF = sb("WLF", [P, SLOTS, SLOT])
        adaring = sb("adaring", [P, ADA_SLOTS * ADA_COLS])
        par = sb("par", [P, NPAR])
        X = sb("X", [P, KD, T])
        SQ = sb("SQ", [P, 2048])
        with nc.sbuf_tensor("HR", [P, 4096], F32R) as HR:
            pass
        HX = sb("HX", [P, 4096])
        with nc.sbuf_tensor("RR", [P, 22528], F32R) as RR:
            pass
        R = sb("R", [P, 22528])
        CT = sb("CT", [P, 4, T])
        RS = sb("RS", [P, 2, T])
        mod = sb("mod", [P, 48])
        lead = sb("lead", [P, 32])
        csil = sb("csil", [P, 16])
        CD = sb("CD", [P, 4, 32])
        sm = sb("sm", [P, 96])
        GT = sb("GT", [P, 2, 24])
        eps_col = sb("eps_col", [P, 1])
        mlars = sb("mlars", [P, 32])
        cmx = sb("cmx", [P, 36])
        kct = sb("kct", [P, 30])
        identb = sb("identb", [P, P], BF16)
        maskb = sb("maskb", [P, P], BF16)
        psL = ctx.enter_context(nc.psum_tensor("psL", [P, 4, 512], F32))
        psS = ctx.enter_context(nc.psum_tensor("psS", [P, 2, 512], F32))
        psO = ctx.enter_context(nc.psum_tensor("psO", [P, 2, 512], F32))
        cum_dram = nc.dram_tensor("cum_dram", (HEADS1, T), F32, kind="Internal").ap()

        def pv(name, lo=0, n=None):
            at, cols = PAR[name]
            return par[:, at + lo:at + (cols if n is None else lo + n)]

        def region(buf, lo, **dims):
            a, b = dims["a"], dims["b"]
            return buf[:, lo:lo + a * b].rearrange("p (a b) -> p a b", b=b)

        HH, HL = region(HR, 0, a=8, b=T), region(HR, 2048, a=8, b=T)
        Z = region(R, 0, a=NZ, b=T)
        XBC = region(R, 4096, a=NXBC, b=T)
        G1 = region(R, 10240, a=16, b=T)
        SCQ = region(R, 14336, a=8, b=T)
        YSC = region(R, 16384, a=8, b=T)
        XTOK = region(R, 18432, a=2, b=2048)
        ACC0 = R[:, 0:2048]
        ACC1 = R[:, 18432:22528]
        WDT = region(RR, 14336, a=2, b=KD * HEADS1)
        CUMB = region(R, 14336, a=2, b=1024)
        SE = region(R, 8192, a=2, b=768)
        SM = region(adaring, 0, a=2, b=768)
        dts = SQ[0:32, 0:1536].rearrange("p (a b) -> p a b", b=T)
        SCM = region(SQ, 0, a=4, b=384)
        ZH, ZL = region(RR, 4096, a=16, b=T), region(RR, 18432, a=16, b=T)
        YH, YL = region(RR, 14336, a=8, b=T), region(RR, 8192, a=8, b=T)
        MIXIN = region(HX, 0, a=8, b=T)
        MH, ML = region(RR, 2048, a=8, b=T), region(RR, 16384, a=8, b=T)
        MIX = region(R, 4096, a=8, b=T)
        FAH, FAL = region(RR, 0, a=KF, b=T), region(RR, KF * T, a=KF, b=T)
        FO = region(R, 12288, a=8, b=T)
        ACC2 = R[:, 14336:17408]
        SUMS = CT[:, 3, :]
        QTOK = region(R, 0, a=2, b=1024)
        KTOK = region(R, 2048, a=2, b=768)
        VTOK = region(R, 3584, a=2, b=512)
        KR = region(R, 4608, a=2, b=64)
        VC = region(R, 4864, a=2, b=T)
        CQ = region(R, 5376, a=3, b=T)
        CKV = region(R, 6144, a=2, b=T)
        G2 = region(R, 6656, a=16, b=T)
        QT = region(R, 10752, a=8, b=T)
        KT = region(R, 12800, a=6, b=T)
        QB = region(R, 14336, a=2, b=1536)
        KB = region(R, 17408, a=2, b=1536)
        VB = region(R, 20480, a=2, b=1024)
        OM = region(HX, 0, a=8, b=T)
        CB = [region(HX, 2048, a=32, b=30), region(HX, 3072, a=32, b=30)]
        PR = region(SQ, 0, a=3, b=384)
        HIDT = SQ[0:30, 512:1024].rearrange("p (a b) -> p a b", b=256)
        HID = region(SQ, 1536, a=4, b=30)
        VCMP = SQ[0:NCMP, 1664:1920].rearrange("p (a b) -> p a b", b=P)
        KCD = SQ[0:30, 1920:2048]
        PT = region(R, 4864, a=2, b=384)
        KCT = kct[:, :]
        CS = RS[:, 0, 0:240]
        KCN = RS[0:30, 1, 0:P]
        PTC = region(R, 0, a=8, b=T)
        MQN = region(R, 0, a=8, b=T)
        MQR = region(R, 2048, a=8, b=T)
        MKR = region(R, 6656, a=8, b=T)
        MKN = region(R, 10752, a=8, b=T)
        OMH, OML = region(RR, 0, a=8, b=T), region(RR, 2048, a=8, b=T)

        par_in_sem, x_in = sem("par_in"), sem("x_in")
        w_arrived = [sem(f"w_arrived{i}") for i in range(SLOTS)]
        ada_arrived = [sem(f"ada_arrived{i}") for i in range(ADA_SLOTS)]
        ada_used = sem("ada_used")
        acc_cleared = sem("acc_cleared")
        hi_done = sem("hi_done")
        lo_done = sem("lo_done")
        lin_done = sem("lin_done")
        lin_free = [sem(f"lin_free{i}") for i in range(4)]
        s_done = sem("s_done")
        s_free = [sem(f"s_free{i}") for i in range(2)]
        o_free = [sem(f"o_free{i}") for i in range(2)]
        act_step, dve_step, pool_step = sem("act_step"), sem("dve_step"), sem("pool_step")
        consts_ready = sem("consts_ready")
        csil_ready = sem("csil_ready")
        sq_ready = sem("sq_ready")
        rs_ready = sem("rs_ready")
        h_ready = sem("h_ready")
        dtx_ready, dtw_ready, dtl_ready, dt_ready = sem("dtx"), sem("dtw"), sem("dtl"), sem("dt_ready")
        cum_stored, cum_in = sem("cum_stored"), [sem("cum_in0"), sem("cum_in1")]
        conv_begun, conv_done, xbc_ready = sem("conv_begun"), sem("conv_done"), sem("xbc_ready")
        sc_c_ready, ysc_ready, gates_ready = sem("sc_c_ready"), sem("ysc_ready"), sem("gates_ready")
        xtok_ready, cd_ready = sem("xtok_ready"), sem("cd_ready")
        diff_ready, decay_ready, m_ready, m_used = sem("diff"), sem("decay"), sem("m_ready"), sem("m_used")
        y_ready, yn_ready, mixin_ready = sem("y_ready"), sem("yn_ready"), sem("mixin_ready")
        x_ready = sem("x_ready")
        t_ready, hh_ready = sem("t_ready"), sem("hh_ready")
        wdt_hi, wdt_ready = sem("wdt_hi"), sem("wdt_ready")
        zh_ready, yh_ready, mh_ready, omh_ready = sem("zh_ready"), sem("yh_ready"), sem("mh_ready"), sem("omh_ready")
        zl_ready, yl_ready, ml_ready, oml_ready = sem("zl_ready"), sem("yl_ready"), sem("ml_ready"), sem("oml_ready")
        f_prod, f_hi = sem("f_prod"), sem("f_hi")
        f_begun, f_conv, f_silu, f_act = sem("f_begun"), sem("f_conv"), sem("f_silu"), sem("f_act")
        tok_sq, tok_ready, feat_ready, ng_ready = sem("tok_sq"), sem("tok_ready"), sem("feat_ready"), sem("ng_ready")
        cqn_ready, mla_tok, mla_sq = sem("cqn_ready"), sem("mla_tok"), sem("mla_sq")
        tsum, trs, troped = sem("tsum"), sem("trs"), sem("troped")
        turned = sem("turned")
        cb_ready, hid_ready, kcn_ready, vcmp_ready = sem("cb_ready"), sem("hid_ready"), sem("kcn_ready"), sem("vcmp_ready")
        kc_rs = sem("kc_rs")
        cs_ready, ce_ready, cp_ready, ptc_ready = sem("cs_ready"), sem("ce_ready"), sem("cp_ready"), sem("ptc_ready")
        max_ready, exp_ready, p_ready = sem("max_ready"), sem("exp_ready"), sem("p_ready")
        pt_ready, pt_used, om_ready = sem("pt_ready"), sem("pt_used"), sem("om_ready")
        out_sem = sem("out_stored")
        sums_ready = sem("sums_ready")
        part_used = sem("part_used")
        cmp_arrived = [sem(f"cmp_arrived{i}") for i in range(4)]
        cmp_used = sem("cmp_used")
        hidt_ready = sem("hidt_ready")
        pool_roped, kr_added = sem("pool_roped"), sem("kr_added")

        class Steps:

            def __init__(self, eng, s):
                self.eng, self.s, self.n, self.loop = eng, s, 0, 0

            def mark(self, ins):
                self.n += 1
                ins.then_inc(self.s, 1)
                return self.loop + self.n

            def link(self, ins):
                self.eng.wait_ge(self.s, self.mark(ins))

            @contextmanager
            def repeat(self, times, per):
                before = self.n
                with self.eng.Fori(0, times, 1) as i:
                    if per:
                        self.loop = i * per
                    yield i
                    assert self.n - before == per, (self.n - before, per)
                self.loop = 0
                self.n = before + per * times

        def sbank(name, i=0):
            return psS[:, (SCRATCH[name] + i) % 2, :]

        block = ctx.enter_context(nc.Block())

        @block.sync
        def _(sp):
            def load(c, i=0, per=SLOTS):
                before = c - SLOTS
                if before >= 0:
                    if PLAN.split_at[before] is None:
                        sp.wait_ge(lin_done, PLAN.done_after[before])
                    else:
                        sp.wait_ge(lo_done, PLAN.split_at[before] + 1 + i * per)
                n = PLAN.cols[c]
                sp.dma_start(ring[:, c % SLOTS, 0:n],
                             wts[bass.ds(c * P + i * (per * P), P), 0:n]).then_inc(w_arrived[c % SLOTS], 16)

            def load_ada(n, i=0, per=0):
                if n >= ADA_SLOTS:
                    sp.wait_ge(ada_used, n - ADA_SLOTS + 1 + 8 + i * per)
                k = n % ADA_SLOTS
                sp.dma_start(adaring[:, k * ADA_COLS:(k + 1) * ADA_COLS],
                             ada_w[bass.ds(n * P + i * (per * P), P), :]).then_inc(ada_arrived[k], 16)

            cmp_weights = [buf[:, :, :] for buf in (WHF, WLF, ring, WHF)]

            sp.dma_start(par[:, 0:PAR_FIRST], par_in[:, 0:PAR_FIRST]).then_inc(par_in_sem, 16)
            for n in range(4):
                load_ada(n)
            sp.dma_start(X[:, :, :], x_t).then_inc(x_in, 16)
            for n in range(4, 16):
                load_ada(n)
            for c in range(SLOTS):
                load(c)
            sp.dma_start(par[:, PAR_FIRST:NPAR], par_in[:, PAR_FIRST:NPAR]).then_inc(par_in_sem, 16)
            load_ada(16)
            load_ada(17)
            with sp.Fori(0, 7, 1) as i:
                for k in range(4):
                    load(4 + 2 * k, i, 8)
                    load(5 + 2 * k, i, 8)
                    load_ada(18 + k, i, 4)
            for c in (60, 61):
                load(c)
            load_ada(46)
            load_ada(47)
            for c in (62, 63):
                load(c)
            up = PLAN.at["up1"][0]
            with sp.Fori(0, (up + 4 - 64) // 4, 1) as i:
                for k in range(4):
                    load(64 + k, i)
            sp.wait_ge(m_used, HEADS1 // 2)
            for n in range(48, 52):
                load_ada(n)
            for k in range(8):
                load(up + 4 + k)
            with sp.Fori(0, 2, 1) as i:
                for q in range(8):
                    load_ada(52 + q, i, 8)
                    for k in range(2):
                        load(up + 12 + 2 * q + k, i, 16)
            for q in range(4):
                load_ada(68 + q)
                for k in range(2):
                    load(up + 44 + 2 * q + k)
            tok2 = PLAN.at["tok2"][0]
            for c in range(up + 52, tok2 + 4):
                load(c)
            for q in range(12):
                load_ada(72 + 2 * q)
                load(tok2 + 4 + 3 * q)
                load_ada(73 + 2 * q)
                for k in (1, 2):
                    load(tok2 + 4 + 3 * q + k)

            def load_cmp(n):
                rows = wts[CMP_ROW + n * SLOTS * P:CMP_ROW + (n + 1) * SLOTS * P, :]
                sp.dma_start(cmp_weights[n], rows.rearrange("(c p) n -> p c n", p=P)).then_inc(cmp_arrived[n], 16)

            c = tok2 + 40
            uq, ukv, o2 = (PLAN.at[name][0] for name in ("uq", "ukv", "o2"))
            assert ukv + 4 == o2
            while c < CHUNKS:
                if c == ukv + 2:
                    sp.wait_ge(lin_done, PLAN.at["uq"][1])
                    load_cmp(0)
                if c == o2:
                    load_cmp(1)
                    sp.wait_ge(lin_done, PLAN.at["cmp"][1])
                    load_cmp(2)
                    sp.wait_ge(cmp_used, 1)
                    load_cmp(3)
                    sp.wait_ge(cmp_used, 3)
                n = 0
                while (c + n < CHUNKS and PLAN.cols[c + n] == PLAN.cols[c]
                       and PLAN.split_at[c + n - SLOTS] is not None):
                    n += 1
                rounds = n // SLOTS
                if rounds >= 2:
                    with sp.Fori(0, rounds, 1) as i:
                        for k in range(SLOTS):
                            load(c + k, i)
                    c += rounds * SLOTS
                else:
                    load(c)
                    c += 1
            for j in range(KD):
                sp.wait_ge(x_ready, 3 * KD + j + 1)
                sp.dma_start(out_t[:, j * T:(j + 1) * T], X[:, j, :]).then_inc(out_sem, 16)
            sp.wait_ge(out_sem, 16 * KD)

        @block.gpsimd
        def _(pool):
            def low(q, i=0):
                pool.wait_ge(hi_done, q + 1 + i * SLOTS)
                n = PLAN.cols[PLAN.chunk_of[q]]
                k = q % SLOTS
                nc.gpsimd.tensor_tensor(WL[:, k, 0:n], ring[:, k, 0:n], WH[:, k, 0:n].bitcast(F32), SUB
                                        ).then_inc(lo_done, 1)

            def lows(q, last):
                while q < last:
                    n = 0
                    while q + n < last and PLAN.cols[PLAN.chunk_of[q + n]] == PLAN.cols[PLAN.chunk_of[q]]:
                        n += 1
                    rounds = n // SLOTS
                    if rounds >= 2:
                        with pool.Fori(0, rounds, 1) as i:
                            for k in range(SLOTS):
                                low(q + k, i)
                        q += rounds * SLOTS
                    else:
                        low(q)
                        q += 1

            lows(0, PLAN.q("o2"))

            G = nc.gpsimd
            st = Steps(pool, pool_step)

            def heads_of(ap, d):
                return ap.rearrange("p (h d) -> p h d", d=d)

            def rope(buf, heads, cos, sin):
                half = ROPE // 2
                tmp = heads_of(CT[:, 2:4, :].rearrange("p a b -> p (a b)")[:, 0:heads * ROPE], ROPE)
                st.mark(G.tensor_tensor(tmp[:, :, 0:half], buf[:, :, half:ROPE],
                                        sin[:, 0:half].unsqueeze(1).to_broadcast([P, heads, half]), MUL))
                st.link(G.tensor_tensor(tmp[:, :, half:ROPE], buf[:, :, 0:half],
                                        sin[:, half:ROPE].unsqueeze(1).to_broadcast([P, heads, half]), MUL))
                st.link(G.tensor_tensor(buf, buf, cos.unsqueeze(1).to_broadcast([P, heads, ROPE]), MUL))
                return G.tensor_tensor(buf, buf, tmp, ADD)

            pool.wait_ge(h_ready, 24)
            pool.wait_ge(mla_sq, 1)
            for t in range(2):
                st.link(G.tensor_scalar(mlars[:, 16 * t:16 * t + 8], mlars[:, 16 * t:16 * t + 8], float(QK) ** -0.5, None, MUL))
            for t in range(2):
                cos, sin = pv("mcos", t * ROPE, ROPE), pv("msin", t * ROPE, ROPE)
                q3 = heads_of(QB[:, t, :], QK)
                st.link(G.tensor_tensor(q3, q3, pv("mq_gain").unsqueeze(1).to_broadcast([P, 8, QK]), MUL))
                st.link(G.tensor_tensor(q3, q3, mlars[:, 16 * t:16 * t + 8].unsqueeze(2).to_broadcast([P, 8, QK]), MUL))
                st.link(rope(q3[:, :, HD:QK], 8, cos, sin))
                pool.sem_inc(pool_roped, 1)
                k3 = heads_of(KB[:, t, :], QK)
                st.link(G.tensor_tensor(k3[:, :, 0:HD], k3[:, :, 0:HD],
                                        pv("mk_gain", 0, HD).unsqueeze(1).to_broadcast([P, 8, HD]), MUL))
                kr = KR[:, t, :].unsqueeze(1)
                st.link(G.tensor_tensor(KR[:, t, :], KR[:, t, :], pv("mk_gain", HD, ROPE), MUL))
                st.link(rope(kr, 1, cos, sin))
                st.link(G.tensor_copy(k3[:, :, HD:QK], kr.to_broadcast([P, 8, ROPE])))
                st.link(G.tensor_tensor(k3, k3, mlars[:, 16 * t + 8:16 * t + 16].unsqueeze(2).to_broadcast([P, 8, QK]), MUL))
                pool.sem_inc(pool_roped, 1)

            lows(PLAN.q("o2"), SPLITS)

        @block.tensor
        def _(pe):
            def mm(out, lhsT, rhs, start, stop):
                return nc.tensor.matmul(out, lhsT, rhs, start=start, stop=stop)

            def chunk_wait(c, rounds=0):
                pe.wait_ge(w_arrived[c % SLOTS], 16 * (c // SLOTS + 1) + 16 * rounds)

            def split_wait(q, rounds=0):
                pe.wait_ge(lo_done, q + 1 + SLOTS * rounds)

            def bank_wait(u, rounds=0):
                if u >= 4:
                    pe.wait_ge(lin_free[u % 4], u // 4 + rounds)

            def scratch(name, i=0):
                n = SCRATCH[name] + i
                if n >= 2:
                    pe.wait_ge(s_free[n % 2], n // 2)
                return psS[:, n % 2, :]

            def obank(n):
                if n >= 2:
                    pe.wait_ge(o_free[n % 2], n // 2)
                return psO[:, n % 2, :]

            def triple(out, wh, wl, hi, lo, first, last):
                mm(out, wh, hi, first, False)
                mm(out, wh, lo, False, False)
                return mm(out, wl, hi, False, last)

            def unit(u, q, nchunks, hi, lo, rounds=0, sizes=(8, 8, 6), operand=None):
                bank_wait(u, rounds)
                kk = 0
                for c in range(nchunks):
                    split_wait(q + c, rounds)
                    s = (q + c) % SLOTS
                    for b in range(sizes[c]):
                        if operand:
                            operand(kk)
                        end = c == nchunks - 1 and b == sizes[c] - 1
                        last = triple(psL[:, u % 4, 0:T], WH[:, s, b * P:(b + 1) * P], WL[:, s, b * P:(b + 1) * P],
                                      hi(kk), lo(kk), kk == 0, end)
                        kk += 1
                    if nchunks == 3 and c < 2:
                        last.then_inc(part_used, 1)
                last.then_inc(lin_done, 1)

            def linear8(name, first, count, hi, lo, operand=None):
                q0, u0 = PLAN.q(name) + first, PLAN.at[name][1] + first
                done = SLOTS if u0 == 0 or operand else 0
                for c in range(done):
                    unit(u0 + c, q0 + c, 1, hi, lo, operand=operand if c == 0 else None)
                rounds = (count - done) // SLOTS
                if rounds >= 2:
                    with pe.Fori(0, rounds, 1) as i:
                        for c in range(done, done + SLOTS):
                            unit(u0 + c, q0 + c, 1, hi, lo, i)
                    done += rounds * SLOTS
                for c in range(done, count):
                    unit(u0 + c, q0 + c, 1, hi, lo)

            def stat_block(out, k, n, squares, base=None):
                if base is not None:
                    pe.wait_ge(sq_ready, base + k + 1)
                last = mm(out[:, 0:T], pv("ones"), squares(k), k == 0, k == n - 1)
                if k == n - 1:
                    last.then_inc(s_done, 1)

            def stat(name, squares, n, i=0, base=None):
                out = scratch(name, i)
                for k in range(n):
                    stat_block(out, k, n, squares, base)

            def stat_of_sums(name, use):
                out = scratch(name)
                pe.wait_ge(sums_ready, use)
                mm(out[:, 0:T], pv("ones"), SUMS, True, True).then_inc(s_done, 1)

            def from_count(s, base):
                return lambda k: pe.wait_ge(s, base + k + 1)

            def mod_columns(name, acc, lo, hi):
                out = scratch(name)
                for j in range(lo, hi):
                    last = mm(out[:, j - lo:j - lo + 1], acc[:, (j - lo) * P:(j - lo + 1) * P], pv("ones", 0, 1), True, True)
                last.then_inc(s_done, 1)

            def sq_at(k):
                return SQ[:, k * T:(k + 1) * T]

            def down(name, base):
                return lambda m: unit(PLAN.at[name][1] + m, PLAN.q(name) + 3 * m, 3, lambda k: FAH[:, k, :],
                                      lambda k: FAL[:, k, :], operand=from_count(f_act, base) if m == 0 else None)

            h_hi, h_lo = (lambda k: HH[:, k, :]), (lambda k: HL[:, k, :])

            pe.wait_ge(par_in_sem, 16)
            pe.wait_ge(sq_ready, 1)
            stat("stat_mix", sq_at, 8)
            pe.wait_ge(ada_used, 8 + 8)
            mod_columns("mod_scale", ACC0[:, ADA_COLS:], 0, 8)
            pe.wait_ge(ada_used, 8 + 16)
            mod_columns("mod_shift", ACC0, 0, 8)
            pe.wait_ge(wdt_ready, 1)
            out = scratch("dt")
            for k in range(KD):
                pe.wait_ge(h_ready, k + 1)
                wh, wl = (WDT[:, part, k * 32:(k + 1) * 32] for part in range(2))
                last = triple(out[0:32, 0:T], wh, wl, HH[:, k, :], HL[:, k, :], k == 0, k == 7)
            last.then_inc(s_done, 1)
            linear8("in1", 0, 64, h_hi, h_lo)
            pe.wait_ge(ada_used, 8 + 48)
            mod_columns("mod_b", ACC1, 16, 48)
            pe.wait_ge(par_in_sem, 32)
            pe.wait_ge(dt_ready, 1)
            out = scratch("dt_turn")
            for n, row in enumerate((5, 5, 3, 3)):
                last = nc.tensor.transpose(out[:, 32 * n:32 * n + 32], dts[:, row, (n % 2) * P:(n % 2 + 1) * P],
                                           pv("ident", 0, 32)[0:32, :])
            last.then_inc(s_done, 1)
            pe.wait_ge(xbc_ready, 8)
            for i in range(8):
                t, q = divmod(i, 4)
                out = scratch("x_turn", i)
                for b in range(4):
                    last = nc.tensor.transpose(out[:, b * P:(b + 1) * P], XBC[:, 4 * q + b, t * P:(t + 1) * P], pv("ident"))
                last.then_inc(s_done, 1)
            for g in range(NGRP):
                out = scratch("scores", g)
                mm(out[:, 0:256], XBC[:, 16 + g, 0:P], XBC[:, 20 + g, :], True, True)
                mm(out[:, 256:384], XBC[:, 16 + g, P:T], XBC[:, 20 + g, P:T], True, True).then_inc(s_done, 1)
            for p in range(HEADS1 // 2 + 1):
                if p < HEADS1 // 2:
                    unit(PLAN.at["in1"][1] + 64 + p, PLAN.q("in1") + 64 + p, 1, h_hi, h_lo)
                if p >= 1:
                    n = p - 1
                    ob = obank(OUT_Y + n)
                    if n == 0:
                        pe.wait_ge(xtok_ready, 8)
                    pe.wait_ge(m_ready, n + 1)
                    for e in range(2):
                        rows = slice(64 * e, 64 * e + 64)
                        cols = slice(P * n + 64 * e, P * n + 64 * e + 64)
                        mm(ob[rows, 0:T], XTOK[:, 0, cols], SM[:, n % 2, 384 * e:384 * e + 256], True, False)
                        last = mm(ob[rows, P:T], XTOK[:, 1, cols], SM[:, n % 2, 384 * e + 256:384 * e + 384], False, True)
                    last.then_inc(m_used, 1)
            def gnorm(g):
                pe.wait_ge(sq_ready, 2 + g)
                stat("gnorm", lambda k: SQ[:, (g % 2) * 1024 + k * T:(g % 2) * 1024 + (k + 1) * T], 4, g)

            gnorm(0)
            gnorm(1)
            pe.wait_ge(yl_ready, 1)
            for m in range(8):
                if m in (1, 2):
                    gnorm(m + 1)
                unit(PLAN.at["sc_out"][1] + m, PLAN.q("sc_out") + m, 1, lambda k: YH[:, k, :], lambda k: YL[:, k, :])
            for m in range(8):
                unit(PLAN.at["ssd_out"][1] + m, PLAN.q("ssd_out") + 2 * m, 2, lambda k: ZH[:, k, :], lambda k: ZL[:, k, :],
                     operand=lambda k: pe.wait_ge(zl_ready, k // 4 + 1) if m == 0 and k % 4 == 0 else None)
            linear8("o1", 0, 8, lambda k: MH[:, k, :], lambda k: ML[:, k, :], from_count(ml_ready, 0))
            stat_of_sums("stat_o1", 1)
            stat("stat_ffn1", sq_at, 8, base=13)
            linear8("up1", 0, 44, h_hi, h_lo, from_count(h_ready, 8))
            for m in range(8):
                down("down1", 0)(m)
            stat_of_sums("stat_down1", 2)
            pe.wait_ge(ada_used, 8 + 72)
            mod_columns("mod_2a", ACC2, 0, 24)

            stat("stat_attn", sq_at, 8, base=29)
            q0, u0 = PLAN.q("tok2"), PLAN.at["tok2"][1]
            for c in range(9):
                for t in range(2):
                    bank_wait(u0 + 2 * c + t)
                for part in range(2):
                    split_wait(q0 + 2 * c + part)
                    s = (q0 + 2 * c + part) % SLOTS
                    for t in range(2):
                        out = psL[:, (u0 + 2 * c + t) % 4, 0:256]
                        for b in range(4):
                            k = 4 * part + b
                            if c == 0 and t == 0:
                                pe.wait_ge(h_ready, 16 + k + 1)
                            hh, hl = (x[:, k, t * P:(t + 1) * P] for x in (HH, HL))
                            wh, wl = (x[:, s, b * 256:(b + 1) * 256] for x in (WH, WL))
                            mm(out, hh, wh, k == 0, False)
                            mm(out, hh, wl, False, False)
                            last = mm(out, hl, wh, False, k == 7)
                        if part == 1:
                            last.then_inc(lin_done, 1)
            q0, u0 = PLAN.q("mix2"), PLAN.at["mix2"][1]
            split_wait(q0)
            for t in range(2):
                bank_wait(u0 + t)
                out = psL[:, (u0 + t) % 4, 0:88]
                for k in range(KD):
                    hh, hl = (x[:, k, t * P:(t + 1) * P] for x in (HH, HL))
                    wh, wl = (x[:, q0 % SLOTS, k * 88:(k + 1) * 88] for x in (WH, WL))
                    mm(out, hh, wh, k == 0, False)
                    mm(out, hh, wl, False, False)
                    last = mm(out, hl, wh, False, k == 7)
                last.then_inc(lin_done, 1)
            linear8("feat2", 0, 9, h_hi, h_lo)
            pe.wait_ge(sq_ready, 38)
            stat("stat_cq", sq_at, 3)
            stat("stat_ckv", lambda k: sq_at(3 + k), 2)
            linear8("feat2", 9, 14, h_hi, h_lo)
            pe.wait_ge(ada_used, 8 + 96)
            mod_columns("mod_2b", ACC2, 0, 24)
            pe.wait_ge(cqn_ready, 5)
            c0, u0 = PLAN.at["uq"]
            for h in range(NH):
                chunk_wait(c0 + h)
                bank_wait(u0 + h)
                for t in range(2):
                    for k in range(3):
                        last = mm(psL[:, (u0 + h) % 4, t * QK:(t + 1) * QK], CQ[:, k, t * P:(t + 1) * P],
                                  ring[:, (c0 + h) % SLOTS, k * QK:(k + 1) * QK], k == 0, k == 2)
                last.then_inc(lin_done, 1)
            c0, u0 = PLAN.at["ukv"]
            for c in range(4):
                chunk_wait(c0 + c)
                for t in range(2):
                    u = u0 + 2 * c + t
                    bank_wait(u)
                    for k in range(2):
                        last = mm(psL[:, u % 4, :], CKV[:, k, t * P:(t + 1) * P],
                                  ring[:, (c0 + c) % SLOTS, k * 512:(k + 1) * 512], k == 0, k == 1)
                    last.then_inc(lin_done, 1)
            for i in range(7):
                if i == 0:
                    pe.wait_ge(troped, 4)
                out = scratch("nsa_turn", i)
                for n in range(4):
                    hh, t = divmod(n, 2)
                    src = (QTOK[:, t, (2 * i + hh) * HD:(2 * i + hh + 1) * HD] if i < 4 else
                           KTOK[:, t, (2 * (i - 4) + hh) * HD:(2 * (i - 4) + hh + 1) * HD])
                    last = nc.tensor.transpose(out[:, n * P:(n + 1) * P], src, pv("ident"))
                last.then_inc(s_done, 1)
            u0 = PLAN.at["cmp"][1]

            def compress(kv, lo, hi):
                out = psL[0:30, (u0 + kv) % 4, 0:256]
                for l in range(lo, hi):
                    n = 2 * kv + l // 16
                    if l % 16 == 0:
                        pe.wait_ge(cmp_arrived[n], 16)
                    wbuf = (WHF, WLF, ring, WHF)[n]
                    last = mm(out, CB[kv][:, l, :], wbuf[:, l % 16 // 4, l % 4 * 256:(l % 4 + 1) * 256], l == 0, l == 31)
                    if l == 31:
                        last.then_inc(lin_done, 1)
                    elif l == 15:
                        last.then_inc(cmp_used, 1)
                if hi == 32:
                    pe.wait_ge(lin_done, u0 + kv + 1)
                    pe.sem_inc(cmp_used, 1)

            def turn_hidden(name, kv):
                pe.wait_ge(hidt_ready, kv + 1)
                out = scratch(name)
                for half in range(2):
                    last = nc.tensor.transpose(out[:, 30 * half:30 * half + 30], HIDT[:, kv, half * P:(half + 1) * P],
                                               pv("ident", 0, 30)[0:30, :])
                last.then_inc(s_done, 1)

            pe.wait_ge(cb_ready, 1)
            bank_wait(u0)
            compress(0, 0, 32)
            pe.wait_ge(cb_ready, 2)
            bank_wait(u0 + 1)
            compress(1, 0, 8)
            turn_hidden("hid_k", 0)
            compress(1, 8, 16)
            pe.wait_ge(hid_ready, 1)
            out = scratch("kc")
            for half in range(2):
                last = mm(out[0:30, 0:P], HID[:, half, :], pv("k_w2", half * P, P), half == 0, half == 1)
            last.then_inc(s_done, 1)
            compress(1, 16, 32)
            pe.wait_ge(kcn_ready, 1)
            out = scratch("kc_turn")
            nc.tensor.transpose(out[:, 0:30], KCN, pv("ident", 0, 30)[0:30, :]).then_inc(s_done, 1)
            turn_hidden("hid_v", 1)
            pe.wait_ge(hid_ready, 2)
            out = scratch("vc")
            for g in range(2):
                for half in range(2):
                    last = mm(out[0:NCMP, g * P:(g + 1) * P], HID[:, 2 + half, g * NCMP:(g + 1) * NCMP],
                              pv("v_w2", half * P, P), half == 0, half == 1)
            last.then_inc(s_done, 1)
            u = PLAN.at["cmp_scores"][1]
            bank_wait(u)
            pe.wait_ge(turned, 7 + 1)
            for h in range(NH):
                for t in range(2):
                    o = (2 * h + t) * NCMP
                    last = mm(psL[:, u % 4, o:o + NCMP], QT[:, h, t * P:(t + 1) * P],
                              KCT[:, (h // 4) * NCMP:(h // 4 + 1) * NCMP], True, True)
            last.then_inc(lin_done, 1)

            def attend(name, pname, obase, count, score, value, lead_in, p0):
                u0 = PLAN.at[name][1]
                for i in range(count + 3):
                    if i < count:
                        u = u0 + i
                        bank_wait(u)
                        out = psL[:, u % 4, :]
                        score(i, out[:, 0:P], 0, P, True)
                        mm(out[:, 0:P], identb[:, :], maskb[:, :], False, True)
                        score(i, out[:, P:384], P, T, True)
                        mm(out[:, 256:384], identb[:, :], maskb[:, :], False, True).then_inc(lin_done, 1)
                    if i == 2 and lead_in:
                        turn_cmp()
                    if 2 <= i <= count + 1:
                        n = i - 2
                        out = scratch(pname, n)
                        pe.wait_ge(p_ready, p0 + n + 1)
                        pr = PR[:, (p0 + n) % 3, :]
                        for b in range(3):
                            last = nc.tensor.transpose(out[:, b * P:(b + 1) * P], pr[:, b * P:(b + 1) * P], pv("ident"))
                        last.then_inc(s_done, 1)
                    if i >= 3:
                        n = i - 3
                        per = 2 if name == "nsa_scores" else 1
                        if n % per == 0:
                            ob = obank(obase + n // per)
                            if lead_in:
                                lead_in(n // per, ob)
                        pe.wait_ge(pt_ready, p0 + n + 1)
                        v0, v1 = value(n)
                        mm(ob[:, 0:T], v0, PT[:, (p0 + n) % 2, 0:256], n % per == 0 and not lead_in, False)
                        last = mm(ob[:, P:T], v1, PT[:, (p0 + n) % 2, 256:384], False, n % per == per - 1)
                        last.then_inc(pt_used, 1)

            def turn_cmp():
                for j in range(4):
                    out = scratch("cmp_turn", j)
                    pe.wait_ge(cp_ready, 1)
                    for n in range(4):
                        o = (4 * j + n) * NCMP
                        last = nc.tensor.transpose(out[0:NCMP, n * P:(n + 1) * P], CS[:, o:o + NCMP], pv("ident"))
                    last.then_inc(s_done, 1)

            def nsa_score(i, out, q0, n_keys, start):
                h, b = divmod(i, 2)
                mm(out, QT[:, h, q0:q0 + P], KT[:, 2 * b + h // 4, 0:n_keys], start, False)

            def nsa_value(n):
                h, b = divmod(n, 2)
                o = b * 256 + (h // 4) * HD
                return VTOK[:, 0, o:o + HD], VTOK[:, 1, o:o + HD]

            def cmp_value(h, ob):
                if h == 0:
                    pe.wait_ge(ptc_ready, 4)
                    pe.wait_ge(vcmp_ready, 1)
                mm(ob[:, 0:T], VCMP[:, h // 4, :], PTC[0:NCMP, h, :], True, False)

            pe.wait_ge(consts_ready, 3)
            attend("nsa_scores", "nsa_p", OUT_NSA, 16, nsa_score, nsa_value, cmp_value, 0)

            for i in range(16):
                kind, pair = divmod(i, 4)
                src, lo, wd = ((QB, 0, HD), (QB, HD, ROPE), (KB, 0, HD), (KB, HD, ROPE))[kind]
                if i == 0:
                    pe.wait_ge(pool_roped, 4)
                out = scratch("mla_turn", i)
                for n in range(4):
                    hh, t = divmod(n, 2)
                    o = (2 * pair + hh) * QK + lo
                    last = nc.tensor.transpose(out[0:wd, n * P:(n + 1) * P], src[:, t, o:o + wd], pv("ident"))
                last.then_inc(s_done, 1)
            pe.wait_ge(turned, 8 + 16)

            def mla_score(i, out, q0, n_keys, start):
                mm(out, MQN[:, i, q0:q0 + P], MKN[:, i, 0:n_keys], start, False)
                mm(out, MQR[0:ROPE, i, q0:q0 + P], MKR[0:ROPE, i, 0:n_keys], False, False)

            def mla_value(n):
                return VB[:, 0, n * HD:(n + 1) * HD], VB[:, 1, n * HD:(n + 1) * HD]

            attend("mla_scores", "mla_p", OUT_MLA, 8, mla_score, mla_value, None, 16)
            linear8("o2", 0, 8, lambda k: OMH[:, k, :], lambda k: OML[:, k, :], from_count(oml_ready, 0))
            stat_of_sums("stat_ffn2", 3)
            linear8("up2", 0, 44, h_hi, h_lo, from_count(h_ready, 24))
            for m in range(8):
                down("down2", KF)(m)

        @block.scalar
        def _(act):
            st = Steps(act, act_step)
            A = nc.scalar.activation

            def stat_root(name, width, dst, i=0):
                act.wait_ge(s_done, SCRATCH[name] + i + 1)
                n = SCRATCH[name] + i
                A(dst, sbank(name, i)[:, 0:T], ACT.Ln, scale=1.0 / width, bias=eps_col[:, :]).then_inc(s_free[n % 2], 1)
                act.wait_ge(s_free[n % 2], n // 2 + 1)
                A(dst, dst, ACT.Exp, scale=-0.5).then_inc(rs_ready, 1)

            fed = [0]

            def high(q, i=0):
                c = PLAN.chunk_of[q]
                k, n = q % SLOTS, PLAN.cols[c]
                act.wait_ge(w_arrived[k], 16 * (c // SLOTS + 1) + 16 * i)
                A(WH[:, k, 0:n], ring[:, k, 0:n], ACT.Copy).then_inc(hi_done, 1)

            def feed(u):
                while fed[0] < SPLITS and PLAN.splittable(fed[0]) <= u + 1:
                    high(fed[0])
                    fed[0] += 1

            def units(name, first, count, evacuate):
                u0, q0 = PLAN.at[name][1] + first, PLAN.q(name) + first
                assert count % 4 == 0 and fed[0] == q0 + SLOTS, (name, fed, q0)
                with st.repeat(count // 4, 0) as i:
                    for k in range(4):
                        u = u0 + k
                        act.wait_ge(lin_done, u + 1 + i * 4)
                        if evacuate:
                            evacuate(k, u, i)
                        high(q0 + k + SLOTS, i)
                fed[0] += count

            def col(buf, j, n=1):
                return buf[:, bass.ds(j, n), :].rearrange("p a b -> p (a b)")

            def wide(view):
                return view.rearrange("p a b -> p (a b)")

            def make_hh(shift, base):
                for j in range(KD):
                    act.wait_ge(t_ready, base + j + 1)
                    A(HH[:, j, :], CT[:, j % 4, :], ACT.Identity, bias=shift[:, j:j + 1]).then_inc(hh_ready, 1)

            act.wait_ge(par_in_sem, 16)
            act.wait_ge(consts_ready, 1)
            A(csil[:, :], par[:, 0:16], ACT.Silu).then_inc(csil_ready, 1)
            A(WDT[:, 0, :], pv("w_dt"), ACT.Copy).then_inc(wdt_hi, 1)
            act.wait_ge(x_in, 16)
            A(SQ[:, :], wide(X[:, :, :]), ACT.Square).then_inc(sq_ready, 1)
            stat_root("stat_mix", D, RS[:, 0, :])
            feed(-1)
            make_hh(mod[:, 0:8], 0)
            n = SCRATCH["dt"]
            act.wait_ge(par_in_sem, 32)
            act.wait_ge(s_done, n + 1)
            A(dts[:, 0, :], psS[0:32, n % 2, 0:T], ACT.Identity, bias=pv("dt_bias")[0:32, :]).then_inc(s_free[n % 2], 1)
            act.wait_ge(s_free[n % 2], n // 2 + 1)
            st.link(A(dts[:, 1, :], dts[:, 0, :], ACT.Abs))
            st.link(A(dts[:, 1, :], dts[:, 1, :], ACT.Exp, scale=-1.0))
            A(sm[0:32, 95:96], pv("a_log")[0:32, :], ACT.Exp).then_inc(dtx_ready, 1)
            act.wait_ge(dtw_ready, 1)
            A(dts[:, 4, :], dts[:, 2, :], ACT.Ln).then_inc(dtl_ready, 1)
            c_w, c_b = PAR["xconv_w"][0], PAR["xconv_b"][0]

            def begin_xbc(k, u, i):
                m = i * 4 + k
                A(col(XBC, m), psL[:, u % 4, 0:T], ACT.Identity, scale=par[:, bass.ds(m + (c_w + 3 * NXBC), 1)],
                  bias=par[:, bass.ds(m + c_b, 1)]).then_inc(conv_begun, 1)

            units("in1", 0, 24, begin_xbc)
            act.wait_ge(dt_ready, 1)
            act.dma_start(cum_dram, dts[:, 5, :]).then_inc(cum_stored, 16)
            def z_bank(k, u, i):
                A(col(Z, i * 4 + k), psL[:, u % 4, 0:T], ACT.Silu).then_inc(lin_free[u % 4], 1)
                if k % 2 == 1:
                    m = i * 6 + 3 * (k // 2)
                    act.wait_ge(conv_done, m + 3)
                    A(col(XBC, m, 3), col(XBC, m, 3), ACT.Silu).then_inc(xbc_ready, 1)

            units("in1", 24, 16, z_bank)

            def sc_c_bank(k, u, i):
                A(col(SCQ, i * 4 + k), psL[:, u % 4, 0:T], ACT.Copy).then_inc(sc_c_ready, 1)
                act.wait_ge(sc_c_ready, i * 4 + (k + 1))
                act.sem_inc(lin_free[u % 4], 1)

            units("in1", 40, 8, sc_c_bank)
            units("in1", 48, 16, None)
            n = SCRATCH["dt_turn"]
            act.wait_ge(s_done, n + 1)
            A(CD[:, :, :].rearrange("p a b -> p (a b)"), psS[:, n % 2, 0:128], ACT.Copy).then_inc(s_free[n % 2], 1)
            def load_cum(i):
                act.dma_start(CUMB[:, i % 2, :],
                              cum_dram[4 * i:4 * i + 4, :].rearrange("h t -> (h t)").partition_broadcast(P)
                              ).then_inc(cum_in[i % 2], 16)

            act.wait_ge(cum_stored, 16)
            act.wait_ge(ysc_ready, 8)
            load_cum(0)
            load_cum(1)
            act.wait_ge(s_free[n % 2], n // 2 + 1)
            act.sem_inc(cd_ready, 1)
            for i in range(8):
                n = SCRATCH["x_turn"] + i
                t, q = divmod(i, 4)
                act.wait_ge(s_done, n + 1)
                A(XTOK[:, t, 512 * q:512 * q + 512], psS[:, n % 2, :], ACT.Copy).then_inc(s_free[n % 2], 1)
                act.wait_ge(s_free[n % 2], n // 2 + 1)
                act.sem_inc(xtok_ready, 1)
            for p in range(HEADS1 // 2):
                u = PLAN.at["in1"][1] + 64 + p
                act.wait_ge(diff_ready, p + 1)
                A(SE[:, p % 2, :], SE[:, p % 2, :], ACT.Exp).then_inc(decay_ready, 1)
                if p % 2 == 1 and p // 2 + 2 < 8:
                    load_cum(p // 2 + 2)
                act.wait_ge(lin_done, u + 1)
                A(G1[:, p, :], psL[:, u % 4, 0:T], ACT.Copy).then_inc(lin_free[u % 4], 1)
                feed(u)
            act.wait_ge(diff_ready, HEADS1 // 2)
            A(wide(YH), wide(YSC), ACT.Copy).then_inc(yh_ready, 1)
            def gate_sigmoid(half):
                A(wide(G1[:, 8 * half:8 * half + 8, :]), wide(G1[:, 8 * half:8 * half + 8, :]), ACT.Sigmoid
                  ).then_inc(gates_ready, 1)

            for n in range(4):
                act.wait_ge(lin_free[n], PLAN.at["sc_out"][1] // 4)

            def group_squares(g):
                A(SQ[:, (g % 2) * 1024:(g % 2 + 1) * 1024], wide(Z[:, 4 * g:4 * g + 4, :]),
                  ACT.Square).then_inc(sq_ready, 1)

            def group_roots(g):
                for e in range(2):
                    n = SCRATCH["gnorm"] + g + e
                    act.wait_ge(s_done, n + 1)
                    A(RS[:, e, :], psS[:, n % 2, 0:T], ACT.Ln, scale=1.0 / 512, bias=eps_col[:, :]
                      ).then_inc(s_free[n % 2], 1)
                for e in range(2):
                    n = SCRATCH["gnorm"] + g + e
                    act.wait_ge(s_free[n % 2], n // 2 + 1)
                    A(RS[:, e, :], RS[:, e, :], ACT.Exp, scale=-0.5).then_inc(rs_ready, 1)

            def group_high(g):
                act.wait_ge(yn_ready, 4 * g + 4)
                A(wide(ZH[:, 4 * g:4 * g + 4, :]), wide(Z[:, 4 * g:4 * g + 4, :]), ACT.Copy).then_inc(zh_ready, 1)

            def done(name, m):
                u = PLAN.at[name][1] + m
                act.wait_ge(lin_done, u + 1)
                feed(u)

            act.wait_ge(m_ready, HEADS1 // 2)
            for g in range(2):
                act.wait_ge(y_ready, 4 * (g + 1))
                group_squares(g)
            group_roots(0)
            for g in (2, 3):
                act.wait_ge(y_ready, 4 * (g + 1))
                act.wait_ge(s_done, SCRATCH["gnorm"] + g - 1)
                group_squares(g)
            gate_sigmoid(1)
            done("sc_out", 0)
            group_high(0)
            group_high(1)
            done("sc_out", 1)
            act.wait_ge(yn_ready, 8)
            group_roots(2)
            done("sc_out", 2)
            done("sc_out", 3)
            group_high(2)
            group_high(3)
            for m in range(4, 8):
                done("sc_out", m)
                if m == 4:
                    gate_sigmoid(0)

            def follow(name, after=None):
                for m in range(8):
                    u = PLAN.at[name][1] + m
                    act.wait_ge(lin_done, u + 1)
                    feed(u)
                    if after:
                        after(m)

            def mix_high(m):
                if m >= 1:
                    act.wait_ge(mixin_ready, m)
                    A(MH[:, m - 1, :], MIXIN[:, m - 1, :], ACT.Copy).then_inc(mh_ready, 1)

            act.wait_ge(zl_ready, 4)
            follow("ssd_out", mix_high)
            mix_high(8)

            def preload():
                st.link(A(sm[:, 94:95], eps_col[:, :], ACT.Ln))

            def feed_parts(name, m, before):
                for c in range(2):
                    act.wait_ge(part_used, before + 2 * m + c + 1)
                    q = PLAN.q(name) + 3 * m + c + SLOTS
                    if q < SPLITS:
                        assert fed[0] == q
                        high(q)
                        fed[0] += 1

            def copy_and_square(name, dst, sq_free_after):
                u0 = PLAN.at[name][1]
                act.wait_ge(s_done, sq_free_after + 1)
                for m in range(8):
                    u = u0 + m
                    if name == "down1":
                        feed_parts(name, m, 0)
                    if m == 7:
                        preload()
                    act.wait_ge(lin_done, u + 1)
                    st.mark(A(dst[:, m, :], psL[:, u % 4, 0:T], ACT.Copy))
                    A(SQ[:, m * T:(m + 1) * T], psL[:, u % 4, 0:T], ACT.Square).then_inc(lin_free[u % 4], 1)
                    act.wait_ge(lin_free[u % 4], u // 4 + 1)
                    act.wait_ge(act_step, st.n)
                    act.sem_inc(sq_ready, 1)
                    if m < 7:
                        feed(u)

            def square_x(base, sq_free_after=None):
                if sq_free_after is not None:
                    act.wait_ge(s_done, sq_free_after + 1)
                for j in range(KD):
                    if j == 7:
                        preload()
                    act.wait_ge(x_ready, base + j + 1)
                    A(SQ[:, j * T:(j + 1) * T], X[:, j, :], ACT.Square).then_inc(sq_ready, 1)

            copy_and_square("o1", MIX, SCRATCH["gnorm"] + 3)
            stat_root("stat_o1", D, RS[:, 0, :])
            feed(PLAN.at["o1"][1] + 7)
            square_x(0)
            stat_root("stat_ffn1", D, RS[:, 1, :])
            make_hh(mod[:, 24:32], 8)

            def ffn(name, wname, bname, base):
                u0, q0 = PLAN.at[name][1], PLAN.q(name)
                w0, b0 = PAR[wname][0], PAR[bname][0]
                assert fed[0] == q0 + SLOTS

                def begin(j, slot, it=0):
                    for b in range(2):
                        u = u0 + 2 * j + b
                        act.wait_ge(lin_done, u + 1 + it * 2)
                        if b == 0 and (j + base >= 2):
                            act.wait_ge(f_act, base + j - 1 + it)
                        A(CT[:, 2 * slot + b, :], psL[:, u % 4, 0:T], ACT.Identity,
                          scale=par[:, bass.ds(w0 + 2 * 44 + b * KF + j + it, 1)],
                          bias=par[:, bass.ds(b0 + b * KF + j + it, 1)]).then_inc(f_begun, 1)
                        q = q0 + 2 * j + b + SLOTS
                        c = PLAN.chunk_of[q]
                        act.wait_ge(w_arrived[q % SLOTS], 16 * (c // SLOTS + 1) + (it * 8))
                        n = PLAN.cols[c]
                        A(WH[:, q % SLOTS, 0:n], ring[:, q % SLOTS, 0:n], ACT.Copy).then_inc(hi_done, 1)

                def silu(j, slot, it=0):
                    act.wait_ge(f_conv, base + j + 1 + it)
                    A(CT[:, 2 * slot, :], CT[:, 2 * slot, :], ACT.Silu).then_inc(f_silu, 1)

                def product_high(j, slot, it=0):
                    act.wait_ge(f_prod, base + j + 1 + it)
                    A(col(FAH, j + it), CT[:, 2 * slot, :], ACT.Copy).then_inc(f_hi, 1)

                begin(0, 0)
                begin(1, 1)
                silu(0, 0)
                product_high(0, 0)
                with st.repeat(9, 0) as i:
                    begin(2, 0, i * 2)
                    silu(1, 1, i * 2)
                    product_high(1, 1, i * 2)
                    begin(3, 1, i * 2)
                    silu(2, 0, i * 2)
                    product_high(2, 0, i * 2)
                for j in (20, 21):
                    begin(j, j % 2)
                    silu(j - 1, (j - 1) % 2)
                    product_high(j - 1, (j - 1) % 2)
                silu(21, 1)
                product_high(21, 1)
                fed[0] += 44

            ffn("up1", "fconv_w", "fconv_b", 0)
            copy_and_square("down1", FO, SCRATCH["stat_ffn1"])
            stat_root("stat_down1", D, RS[:, 0, :])
            feed(PLAN.at["down1"][1] + 7)

            square_x(8)
            stat_root("stat_attn", D, RS[:, 1, :])
            make_hh(mod[:, 0:8], 16)
            u0 = PLAN.at["tok2"][1]
            for c in range(6):
                for t in range(2):
                    u = u0 + 2 * c + t
                    act.wait_ge(lin_done, u + 1)
                    for hh in range(2):
                        n = 4 * c + 2 * t + hh
                        if n >= 16:
                            act.wait_ge(tok_sq, n - 15)
                        A(SQ[:, n % 16 * P:(n % 16 + 1) * P], psL[:, u % 4, hh * P:(hh + 1) * P], ACT.Square,
                          accum_out=sm[:, t * 12 + 2 * c + hh:t * 12 + 2 * c + hh + 1]).then_inc(tok_sq, 1)
                    feed(u)
            for c in range(3):
                for t in range(2):
                    u = u0 + 2 * (6 + c) + t
                    act.wait_ge(lin_done, u + 1)
                    dst = KTOK[:, t, 512:768] if c == 0 else VTOK[:, t, (c - 1) * 256:c * 256]
                    A(dst, psL[:, u % 4, 0:256], ACT.Copy).then_inc(lin_free[u % 4], 1)
                    act.wait_ge(lin_free[u % 4], u // 4 + 1)
                    feed(u)
            act.sem_inc(tok_ready, 1)
            act.wait_ge(tok_sq, 24)
            st.link(A(sm[:, 0:24], sm[:, 0:24], ACT.Ln, scale=1.0 / HD, bias=eps_col[:, :]))
            A(sm[:, 0:24], sm[:, 0:24], ACT.Exp, scale=-0.5).then_inc(trs, 1)
            u0 = PLAN.at["mix2"][1]
            for t in range(2):
                u = u0 + t
                act.wait_ge(lin_done, u + 1)
                st.mark(A(KR[:, t, :], psL[:, u % 4, 0:64], ACT.Copy))
                st.mark(A(SQ[:, 64 * t:64 * t + 64], psL[:, u % 4, 0:64], ACT.Square, accum_out=sm[:, 24 + t:25 + t]))
                A(GT[:, t, :], psL[:, u % 4, 64:88], ACT.Sigmoid).then_inc(lin_free[u % 4], 1)
                act.wait_ge(lin_free[u % 4], u // 4 + 1)
                feed(u)
            act.wait_ge(act_step, st.n)
            act.sem_inc(ng_ready, 1)
            for m in range(7):
                u = u0 + 2 + m
                dst = VC[:, m, :] if m < 2 else CQ[:, m - 2, :] if m < 5 else CKV[:, m - 5, :]
                act.wait_ge(lin_done, u + 1)
                if m >= 2:
                    st.mark(A(SQ[:, (m - 2) * T:(m - 1) * T], psL[:, u % 4, 0:T], ACT.Square))
                A(dst, psL[:, u % 4, 0:T], ACT.Copy).then_inc(lin_free[u % 4], 1)
                act.wait_ge(lin_free[u % 4], u // 4 + 1)
                feed(u)
            act.wait_ge(act_step, st.n)
            act.sem_inc(sq_ready, 1)
            act.sem_inc(feat_ready, 1)
            for m in range(16):
                u = u0 + 9 + m
                act.wait_ge(lin_done, u + 1)
                A(G2[:, m, :], psL[:, u % 4, 0:T], ACT.Sigmoid).then_inc(lin_free[u % 4], 1)
                feed(u)
                if m == 2:
                    act.wait_ge(h_ready, 24)
                    stat_root("stat_cq", 384, RS[:, 0, :])
                if m == 3:
                    stat_root("stat_ckv", 256, RS[:, 1, :])
            for n in range(4):
                act.wait_ge(lin_free[(u - n) % 4], (u - n) // 4 + 1)
            act.sem_inc(gates_ready, 1)
            u0 = PLAN.at["uq"][1]
            act.wait_ge(s_done, SCRATCH["mod_2b"] + 1)
            for h in range(NH):
                u = u0 + h
                act.wait_ge(lin_done, u + 1)
                for t in range(2):
                    st.mark(A(SQ[:, 1536 + t * QK:1536 + (t + 1) * QK], psL[:, u % 4, t * QK:(t + 1) * QK], ACT.Square,
                              accum_out=mlars[:, 16 * t + h:16 * t + h + 1]))
                A(QB[:, :, h * QK:(h + 1) * QK], psL[:, u % 4, 0:2 * QK].rearrange("p (t d) -> p t d", d=QK),
                  ACT.Copy).then_inc(lin_free[u % 4], 1)
                act.wait_ge(lin_free[u % 4], u // 4 + 1)
                act.wait_ge(act_step, st.n)
            u0 = PLAN.at["ukv"][1]
            for n in range(8):
                c, t = n // 2, n % 2
                u = u0 + n
                act.wait_ge(lin_done, u + 1)
                src = psL[:, u % 4, :].rearrange("p (h w) -> p h w", w=256)
                for e in range(2):
                    h = 16 * t + 8 + 2 * c + e
                    st.mark(A(SQ[:, 1536 + e * HD:1536 + (e + 1) * HD], src[:, e, 0:HD], ACT.Square, accum_out=mlars[:, h:h + 1]))
                st.mark(A(KB[:, t, :].rearrange("p (h w) -> p h w", w=QK)[:, 2 * c:2 * c + 2, 0:HD], src[:, :, 0:HD], ACT.Copy))
                A(VB[:, t, :].rearrange("p (h w) -> p h w", w=HD)[:, 2 * c:2 * c + 2, :], src[:, :, HD:256],
                  ACT.Copy).then_inc(lin_free[u % 4], 1)
                act.wait_ge(lin_free[u % 4], u // 4 + 1)
                act.wait_ge(act_step, st.n)
            act.sem_inc(mla_tok, 1)
            for i in range(7):
                n = SCRATCH["nsa_turn"] + i
                act.wait_ge(s_done, n + 1)
                dst = (QT[:, 2 * i:2 * i + 2, :] if i < 4 else KT[:, 2 * (i - 4):2 * (i - 4) + 2, :])
                A(dst.rearrange("p a b -> p (a b)"), psS[:, n % 2, :], ACT.Copy).then_inc(s_free[n % 2], 1)
                act.wait_ge(s_free[n % 2], n // 2 + 1)
                act.sem_inc(turned, 1)
            act.wait_ge(tsum, 1)
            st.link(A(mlars[:, :], mlars[:, :], ACT.Ln, scale=1.0 / QK, bias=eps_col[:, :]))
            A(mlars[:, :], mlars[:, :], ACT.Exp, scale=-0.5).then_inc(mla_sq, 1)
            u0 = PLAN.at["cmp"][1]

            def silu_hidden(kv):
                u = u0 + kv
                act.wait_ge(lin_done, u + 1)
                A(HIDT[:, kv, :], psL[0:30, u % 4, 0:256], ACT.Silu).then_inc(lin_free[u % 4], 1)
                act.wait_ge(lin_free[u % 4], u // 4 + 1)
                act.sem_inc(hidt_ready, 1)

            def copy_hidden(name, kv):
                n = SCRATCH[name]
                act.wait_ge(s_done, n + 1)
                A(HID[:, 2 * kv:2 * kv + 2, :].rearrange("p a b -> p (a b)"), psS[:, n % 2, 0:60], ACT.Copy
                  ).then_inc(s_free[n % 2], 1)
                act.wait_ge(s_free[n % 2], n // 2 + 1)
                act.sem_inc(hid_ready, 1)

            silu_hidden(0)
            copy_hidden("hid_k", 0)
            n = SCRATCH["kc"]
            act.wait_ge(s_done, n + 1)
            st.link(A(KCD, psS[0:30, n % 2, 0:P], ACT.Square, accum_out=sm[0:30, 60:61]))
            st.link(A(sm[0:30, 60:61], sm[0:30, 60:61], ACT.Ln, scale=1.0 / HD, bias=eps_col[0:30, :]))
            A(sm[0:30, 60:61], sm[0:30, 60:61], ACT.Exp, scale=-0.5).then_inc(kc_rs, 1)
            silu_hidden(1)
            n = SCRATCH["kc_turn"]
            act.wait_ge(s_done, n + 1)
            A(KCT, psS[:, n % 2, 0:30], ACT.Copy).then_inc(s_free[n % 2], 1)
            act.wait_ge(s_free[n % 2], n // 2 + 1)
            act.sem_inc(turned, 1)
            copy_hidden("hid_v", 1)
            n = SCRATCH["vc"]
            act.wait_ge(s_done, n + 1)
            A(VCMP.rearrange("p a b -> p (a b)"), psS[0:NCMP, n % 2, 0:256], ACT.Copy).then_inc(s_free[n % 2], 1)
            act.wait_ge(s_free[n % 2], n // 2 + 1)
            act.sem_inc(vcmp_ready, 1)
            act.wait_ge(cs_ready, 1)
            A(CS, CS, ACT.Exp).then_inc(ce_ready, 1)
            feed(PLAN.at["cmp_scores"][1])
            for j in range(4):
                n = SCRATCH["cmp_turn"] + j
                act.wait_ge(s_done, n + 1)
                A(PTC[0:NCMP, 2 * j:2 * j + 2, :].rearrange("p a b -> p (a b)"), psS[0:NCMP, n % 2, :],
                  ACT.Copy).then_inc(s_free[n % 2], 1)
                act.wait_ge(s_free[n % 2], n // 2 + 1)
                act.sem_inc(ptc_ready, 1)

            def softmax(pname, count, p0):
                for i in range(count + 2):
                    if i < count:
                        n = p0 + i
                        u = PLAN.at["nsa_scores"][1] + n
                        act.wait_ge(max_ready, n + 1)
                        if n >= 3:
                            act.wait_ge(s_done, SCRATCH["nsa_p"] + n - 2 if n - 3 < 16 else SCRATCH["mla_p"] + n - 18)
                        st.mark(A(PR[:, n % 3, 0:P], psL[:, u % 4, 0:P], ACT.Exp, bias=sm[:, 26 + 4 * (n % 2):27 + 4 * (n % 2)],
                                  accum_out=sm[:, 28 + 4 * (n % 2):29 + 4 * (n % 2)]))
                        A(PR[:, n % 3, P:384], psL[:, u % 4, P:384], ACT.Exp, bias=sm[:, 27 + 4 * (n % 2):28 + 4 * (n % 2)],
                          accum_out=sm[:, 29 + 4 * (n % 2):30 + 4 * (n % 2)]).then_inc(lin_free[u % 4], 1)
                        act.wait_ge(lin_free[u % 4], u // 4 + 1)
                        act.wait_ge(act_step, st.n)
                        act.sem_inc(exp_ready, 1)
                    if i >= 2:
                        m = p0 + i - 2
                        n = SCRATCH[pname] + i - 2
                        act.wait_ge(s_done, n + 1)
                        if m >= 2:
                            act.wait_ge(pt_used, m - 1)
                        A(PT[:, m % 2, :], psS[:, n % 2, 0:384], ACT.Copy).then_inc(s_free[n % 2], 1)
                        act.wait_ge(s_free[n % 2], n // 2 + 1)
                        act.sem_inc(pt_ready, 1)

            softmax("nsa_p", 16, 0)
            act.wait_ge(pt_used, 16)
            act.wait_ge(om_ready, 8)
            for i in range(16):
                kind, pair = divmod(i, 4)
                dst, wd = ((MQN, HD), (MQR, ROPE), (MKN, HD), (MKR, ROPE))[kind]
                n = SCRATCH["mla_turn"] + i
                act.wait_ge(s_done, n + 1)
                A(dst[0:wd, 2 * pair:2 * pair + 2, :].rearrange("p a b -> p (a b)"), psS[0:wd, n % 2, :],
                  ACT.Copy).then_inc(s_free[n % 2], 1)
                act.wait_ge(s_free[n % 2], n // 2 + 1)
                act.sem_inc(turned, 1)
            softmax("mla_p", 8, 16)
            act.wait_ge(pt_used, 24)
            for h in range(NH):
                act.wait_ge(om_ready, 8 + h + 1)
                A(OMH[:, h, :], OM[:, h, :], ACT.Copy).then_inc(omh_ready, 1)
            def square_o2(m):
                if m >= 1:
                    act.wait_ge(x_ready, 16 + m)
                    A(SQ[:, (m - 1) * T:m * T], X[:, m - 1, :], ACT.Square).then_inc(sq_ready, 1)

            act.wait_ge(s_done, SCRATCH["mla_p"] + 8)
            follow("o2", square_o2)
            preload()
            square_o2(8)
            stat_root("stat_ffn2", D, RS[:, 0, :])
            make_hh(mod[:, 24:32], 24)
            ffn("up2", "fconv_w_2", "fconv_b_2", KF)
            for m in range(8):
                feed_parts("down2", m, 16)
                done("down2", m)

        @block.vector
        def _(dve):
            st = Steps(dve, dve_step)
            V = nc.vector

            def scratch_wait(name, i=0):
                n = SCRATCH[name] + i
                dve.wait_ge(s_done, n + 1)
                return psS[:, n % 2, :], s_free[n % 2]

            def lin(u, rounds=0):
                dve.wait_ge(lin_done, u + 1 + rounds)
                return psL[:, u % 4, 0:T]

            V.memset(eps_col[:, :], EPS).then_inc(consts_ready, 1)
            V.memset(ACC0, 0.0).then_inc(ada_used, 8)
            V.memset(ACC1, 0.0).then_inc(acc_cleared, 1)
            dve.wait_ge(par_in_sem, 16)
            dve.wait_ge(csil_ready, 1)
            dve.wait_ge(ada_used, 8)

            def ada_step(n, a, col, groups, rounds=0, total=0):
                k = n % ADA_SLOTS
                dve.wait_ge(ada_arrived[k], 16 * (n // ADA_SLOTS + 1) + rounds * (16 * total // ADA_SLOTS))
                dve.wait_ge(ada_used, 8 + n - groups + 1 + rounds * total)
                V.scalar_tensor_tensor(a, adaring[:, k * ADA_COLS:(k + 1) * ADA_COLS], col, a, MUL, ADD
                                       ).then_inc(ada_used, 1)

            def ada_group_step(n, a, k, rounds=0):
                slot = n % ADA_SLOTS
                dve.wait_ge(ada_arrived[slot], 16 * (n // ADA_SLOTS + 1) + rounds * (16 * KD // ADA_SLOTS))
                if k:
                    dve.wait_ge(ada_used, 8 + n + rounds * KD)
                w, col = adaring[:, slot * ADA_COLS:(slot + 1) * ADA_COLS], csil[:, 8 + k:9 + k]
                ins = V.scalar_tensor_tensor(a, w, col, a, MUL, ADD) if k else V.tensor_scalar(a, w, col, None, MUL)
                ins.then_inc(ada_used, 1)

            def part(acc, g):
                return acc[:, g * ADA_COLS:(g + 1) * ADA_COLS]

            for n, g in ((0, 1), (8, 0)):
                with st.repeat(2, 0) as i:
                    for kk in range(4):
                        ada_step(n + kk, part(ACC0, g), csil[:, bass.ds(i * 4 + kk, 1)], 1, i, 4)

            def make_h(shift, gains, rs, base):
                for j in range(KD + 1):
                    if j < KD:
                        if j >= 4:
                            dve.wait_ge(h_ready, base + j - 3)
                        V.scalar_tensor_tensor(CT[:, j % 4, :], X[:, j, :], gains[:, j:j + 1], rs, MUL, MUL
                                               ).then_inc(t_ready, 1)
                    if j >= 1:
                        n = j - 1
                        dve.wait_ge(hh_ready, base + n + 1)
                        V.scalar_tensor_tensor(HL[:, n, :], CT[:, n % 4, :], shift[:, n:n + 1], HH[:, n, :].bitcast(F32),
                                               ADD, SUB).then_inc(h_ready, 1)

            ps, free = scratch_wait("mod_scale")
            V.tensor_tensor(mod[:, 8:16], ps[:, 0:8], pv("ada_b", 8, 8), ADD).then_inc(free, 1)
            dve.wait_ge(free, SCRATCH["mod_scale"] // 2 + 1)
            st.link(V.scalar_tensor_tensor(lead[:, 0:8], mod[:, 8:16], 1.0, pv("mix_pre_g"), ADD, MUL))
            dve.wait_ge(x_in, 16)
            dve.wait_ge(rs_ready, 1)
            dve.wait_ge(wdt_hi, 1)
            V.tensor_tensor(WDT[:, 1, :], pv("w_dt"), WDT[:, 0, :].bitcast(F32), SUB).then_inc(wdt_ready, 1)
            ps, free = scratch_wait("mod_shift")
            V.tensor_tensor(mod[:, 0:8], ps[:, 0:8], pv("ada_b", 0, 8), ADD).then_inc(free, 1)
            dve.wait_ge(free, SCRATCH["mod_shift"] // 2 + 1)
            make_h(mod[:, 0:8], lead[:, 0:8], RS[:, 0, :], 0)
            dve.wait_ge(par_in_sem, 32)
            V.tensor_copy(identb[:, :], pv("ident")).then_inc(consts_ready, 1)
            V.tensor_copy(maskb[:, :], pv("causal_add")).then_inc(consts_ready, 1)

            dve.wait_ge(dtx_ready, 1)
            V.tensor_scalar(dts[:, 2, :], dts[:, 1, :], 1.0, None, ADD).then_inc(dtw_ready, 1)
            dve.wait_ge(dtw_ready, 1)
            st.link(V.tensor_scalar(dts[:, 3, :], dts[:, 2, :], 1.0, 1e-30, SUB, ALU.max))
            st.link(V.reciprocal(dts[:, 3, :], dts[:, 3, :]))
            st.link(V.tensor_tensor(dts[:, 3, :], dts[:, 3, :], dts[:, 1, :], MUL))
            dve.wait_ge(dtl_ready, 1)
            st.mark(V.scalar_tensor_tensor(dts[:, 5, :], dts[:, 2, :], 1.0, dts[:, 1, :], ALU.is_equal, MUL))
            st.link(V.tensor_tensor(dts[:, 3, :], dts[:, 3, :], dts[:, 4, :], MUL))
            st.link(V.tensor_tensor(dts[:, 3, :], dts[:, 3, :], dts[:, 5, :], ADD))
            st.link(V.scalar_tensor_tensor(dts[:, 3, :], dts[:, 0, :], 0.0, dts[:, 3, :], ALU.max, ADD))
            st.mark(V.memset(dts[:, 2, :], 1.0))
            st.link(V.tensor_scalar(dts[:, 4, :], dts[:, 3, :], sm[0:32, 95:96], -1.0, MUL, MUL))
            V.tensor_tensor_scan(dts[:, 5, :], dts[:, 2, :], dts[:, 4, :], 0.0, MUL, ADD).then_inc(dt_ready, 1)

            u0 = PLAN.at["in1"][1]
            c_w = PAR["xconv_w"][0]
            dve.wait_ge(acc_cleared, 1)
            with st.repeat(3, 16) as i:
                for k in range(8):
                    m = i * 8 + k
                    dve.wait_ge(conv_begun, m + 1)
                    for back in (1, 2, 3):
                        dst = XBC[:, bass.ds(m, 1), back:T].rearrange("p a b -> p (a b)")
                        ins = V.scalar_tensor_tensor(dst, psL[:, (u0 + k) % 4, 0:T - back],
                                                     par[:, bass.ds(m + (c_w + (3 - back) * NXBC), 1)], dst, MUL, ADD)
                        if back < 3:
                            st.link(ins)
                        else:
                            ins.then_inc(lin_free[(u0 + k) % 4], 1)
                    dve.wait_ge(lin_free[(u0 + k) % 4], (u0 + k) // 4 + 1 + i * 2)
                    dve.sem_inc(conv_done, 1)
                    if k % 2 == 1:
                        g = k // 2
                        ada_step(16 + g, part(ACC1, g), csil[:, bass.ds(i, 1)], 4, i, 4)
            with st.repeat(3, 0) as i:
                for g in range(4):
                    ada_step(28 + g, part(ACC1, g), csil[:, bass.ds(i + 3, 1)], 4, i, 4)
            for j in range(8):
                u = u0 + 48 + j
                dve.wait_ge(lin_done, u + 1)
                dve.wait_ge(sc_c_ready, j + 1)
                V.tensor_tensor(CT[:, j % 2, :], SCQ[:, j, :], psL[:, u % 4, 0:T], MUL).then_inc(lin_free[u % 4], 1)
                dve.wait_ge(lin_free[u % 4], u // 4 + 1)
                st.link(V.tensor_scalar(SCQ[:, j, :], CT[:, j % 2, :], pv("sconv_w", 16 + j, 1), None, MUL))
                for back in (1, 2):
                    st.link(V.scalar_tensor_tensor(SCQ[:, j, back:T], CT[:, j % 2, 0:T - back],
                                                   pv("sconv_w", 8 * (2 - back) + j, 1), SCQ[:, j, back:T], MUL, ADD))
                if j % 2 == 1:
                    ada_step(40 + j // 2, part(ACC1, j // 2), csil[:, 6:7], 4)
            for j in range(8):
                u = u0 + 56 + j
                dve.wait_ge(lin_done, u + 1)
                V.tensor_tensor(YSC[:, j, :], SCQ[:, j, :], psL[:, u % 4, 0:T], MUL).then_inc(lin_free[u % 4], 1)
                if j % 2 == 1:
                    ada_step(44 + j // 2, part(ACC1, j // 2), csil[:, 7:8], 4)
            for k in range(4):
                u = u0 + 60 + k
                dve.wait_ge(lin_free[u % 4], u // 4 + 1)
            dve.sem_inc(ysc_ready, 8)
            ps, free = scratch_wait("mod_b")
            V.tensor_tensor(mod[:, 16:48], ps[:, 0:32], pv("ada_b", 16, 32), ADD).then_inc(free, 1)
            dve.wait_ge(free, SCRATCH["mod_b"] // 2 + 1)
            st.mark(V.tensor_tensor(lead[:, 8:16], mod[:, 16:24], pv("mix_post_g"), MUL))
            st.mark(V.scalar_tensor_tensor(lead[:, 16:24], mod[:, 32:40], 1.0, pv("ffn_pre_g"), ADD, MUL))
            st.link(V.tensor_tensor(lead[:, 24:32], mod[:, 40:48], pv("ffn_post_g"), MUL))

            dve.wait_ge(cd_ready, 1)
            dve.wait_ge(cum_stored, 16)
            for g in range(NGRP):
                ps, free = scratch_wait("scores", g)
                st.mark(V.tensor_tensor(SCM[:, g, 0:P], ps[:, 0:P], pv("causal01"), MUL))
                st.mark(V.tensor_copy(SCM[:, g, P:256], ps[:, P:256]))
                V.tensor_tensor(SCM[:, g, 256:384], ps[:, 256:384], pv("causal01"), MUL).then_inc(free, 1)
                dve.wait_ge(free, (SCRATCH["scores"] + g) // 2 + 1)
            dve.wait_ge(dve_step, st.n)
            dve.wait_ge(xbc_ready, 8)
            for n in range(4):
                dve.wait_ge(lin_free[n], 40 // 4)

            def y_out(j):
                n = OUT_Y + j
                dve.wait_ge(m_used, j + 1)
                V.scalar_tensor_tensor(XBC[:, j, :], XBC[:, j, :], pv("dskip", j, 1), psO[:, n % 2, 0:T], MUL,
                                       ADD).then_inc(o_free[n % 2], 1)
                dve.wait_ge(o_free[n % 2], n // 2 + 1)
                V.tensor_tensor(Z[:, j, :], XBC[:, j, :], Z[:, j, :], MUL).then_inc(y_ready, 1)

            def yn(g):
                dve.wait_ge(rs_ready, 2 + g)
                dve.wait_ge(y_ready, 4 * g + 4)
                for j in range(4 * g, 4 * g + 4):
                    V.scalar_tensor_tensor(Z[:, j, :], Z[:, j, :], pv("ssd_norm_g", j, 1), RS[:, g % 2, :], MUL,
                                           MUL).then_inc(yn_ready, 1)

            NPAIR = HEADS1 // 2
            for p in range(NPAIR + 1):
                if p < NPAIR:
                    hg = p // 2
                    if p % 2 == 0:
                        dve.wait_ge(cum_in[hg % 2], 16 * (hg // 2 + 1))
                    if p >= 2:
                        dve.wait_ge(m_ready, p - 1)
                    for e in range(2):
                        h = 2 * p + e
                        bc = CUMB[:, hg % 2, (h % 4) * T:(h % 4 + 1) * T]
                        se = SE[:, p % 2, 384 * e:384 * e + 384]
                        st.mark(V.tensor_scalar(se[:, 0:256], bc, CD[:, 0, h:h + 1], 0.0, SUB, ALU.min))
                        last = V.tensor_scalar(se[:, 256:384], bc[:, P:T], CD[:, 1, h:h + 1], 0.0, SUB, ALU.min)
                        if e == 0:
                            st.mark(last)
                    last.then_inc(diff_ready, 1)
                if p >= 1:
                    n = p - 1
                    g = n // 4
                    dve.wait_ge(decay_ready, n + 1)
                    if n >= 2:
                        dve.wait_ge(m_used, n - 1)
                    for e in range(2):
                        h = 2 * n + e
                        se, m = (x[:, n % 2, 384 * e:384 * e + 384] for x in (SE, SM))
                        st.mark(V.scalar_tensor_tensor(m[:, 0:256], se[:, 0:256], CD[:, 2, h:h + 1], SCM[:, g, 0:256], MUL, MUL))
                        last = V.scalar_tensor_tensor(m[:, 256:384], se[:, 256:384], CD[:, 3, h:h + 1],
                                                      SCM[:, g, 256:384], MUL, MUL)
                        if e == 0:
                            st.mark(last)
                    last.then_inc(m_ready, 1)
                if p >= 2:
                    y_out(p - 2)
            y_out(NPAIR - 1)
            def flat(view):
                return view.rearrange("p a b -> p (a b)")

            dve.wait_ge(yh_ready, 1)
            V.tensor_tensor(flat(YL), flat(YSC), flat(YH).bitcast(F32), SUB).then_inc(yl_ready, 1)

            def z_low(g):
                dve.wait_ge(zh_ready, g + 1)
                V.tensor_tensor(flat(ZL[:, 4 * g:4 * g + 4, :]), flat(Z[:, 4 * g:4 * g + 4, :]),
                                flat(ZH[:, 4 * g:4 * g + 4, :]).bitcast(F32), SUB).then_inc(zl_ready, 1)

            u0 = PLAN.at["sc_out"][1]
            yn(0)
            yn(1)
            dve.wait_ge(gates_ready, 1)
            for m in range(8):
                if m in (2, 3):
                    z_low(m - 2)
                    yn(m)
                if m in (5, 6):
                    z_low(m - 3)
                u = u0 + m
                V.tensor_tensor(MIXIN[:, m, :], G1[:, 8 + m, :], lin(u), MUL).then_inc(lin_free[u % 4], 1)
            u0 = PLAN.at["ssd_out"][1]
            dve.wait_ge(gates_ready, 2)
            for n in range(4):
                dve.wait_ge(lin_free[n], u0 // 4)

            def mix_low(m):
                dve.wait_ge(mh_ready, m + 1)
                V.tensor_tensor(ML[:, m, :], MIXIN[:, m, :], MH[:, m, :].bitcast(F32), SUB).then_inc(ml_ready, 1)

            dve.wait_ge(yl_ready, 1)
            for m in range(8):
                u = u0 + m
                V.tensor_tensor(CT[:, m % 2, :], G1[:, m, :], lin(u), MUL).then_inc(lin_free[u % 4], 1)
                dve.wait_ge(lin_free[u % 4], u // 4 + 1)
                V.tensor_tensor(MIXIN[:, m, :], MIXIN[:, m, :], CT[:, m % 2, :], ADD).then_inc(mixin_ready, 1)
                if m >= 2:
                    mix_low(m - 2)
            mix_low(6)
            mix_low(7)

            def add_squares(m, base):
                if m == 0:
                    return
                dve.wait_ge(sq_ready, base + m + 1)
                a = SQ[:, 0:T] if m == 1 else SUMS
                ins = V.tensor_tensor(SUMS, a, SQ[:, m * T:(m + 1) * T], ADD)
                if m < 7:
                    st.link(ins)
                else:
                    ins.then_inc(sums_ready, 1)

            def add_normed(src, gains, rs, x_base):
                for j in range(KD + 1):
                    if j < KD:
                        if j >= 2:
                            dve.wait_ge(x_ready, x_base + j - 1)
                        mark = st.mark(V.scalar_tensor_tensor(CT[:, j % 2, :], src[:, j, :], gains[:, j:j + 1], rs, MUL, MUL))
                    if j >= 1:
                        dve.wait_ge(dve_step, mark - 1 if j < KD else mark)
                        V.tensor_tensor(X[:, j - 1, :], X[:, j - 1, :], CT[:, (j - 1) % 2, :], ADD).then_inc(x_ready, 1)

            for m in range(8):
                add_squares(m, 5)
            dve.wait_ge(mixin_ready, 8)
            dve.wait_ge(rs_ready, 6)
            add_normed(MIX, lead[:, 8:16], RS[:, 0, :], 0)
            dve.wait_ge(x_ready, 8)
            dve.wait_ge(rs_ready, 7)
            make_h(mod[:, 24:32], lead[:, 16:24], RS[:, 1, :], 8)

            def ffn(name, wname, base, between):
                u0 = PLAN.at[name][1]
                w0 = PAR[wname][0]

                def conv(j, slot, it=0, uses=0):
                    us = [u0 + 2 * j, u0 + 2 * j + 1]
                    for back in (1, 2):
                        for b in range(2):
                            if back == 1:
                                dve.wait_ge(f_begun, 2 * base + 2 * j + b + 1 + it * 2)
                            dst = CT[:, 2 * slot + b, back:T]
                            ins = V.scalar_tensor_tensor(
                                dst, psL[:, us[b] % 4, 0:T - back],
                                par[:, bass.ds(w0 + (2 - back) * 44 + b * KF + j + it, 1)], dst, MUL, ADD)
                            if back == 1:
                                st.mark(ins)
                            else:
                                ins.then_inc(lin_free[us[b] % 4], 1)
                        if back == 1:
                            dve.wait_ge(dve_step, st.loop + st.n)
                    for b in range(2):
                        dve.wait_ge(lin_free[us[b] % 4], us[b] // 4 + 1 + uses)
                    dve.sem_inc(f_conv, 1)

                def product(j, slot, it=0):
                    dve.wait_ge(f_silu, base + j + 1 + it)
                    V.tensor_tensor(CT[:, 2 * slot, :], CT[:, 2 * slot, :], CT[:, 2 * slot + 1, :], MUL
                                    ).then_inc(f_prod, 1)
                    dve.wait_ge(f_hi, base + j + 1 + it)
                    V.tensor_tensor(FAL[:, bass.ds(j + it, 1), :].rearrange("p a b -> p (a b)"), CT[:, 2 * slot, :],
                                    FAH[:, bass.ds(j + it, 1), :].rearrange("p a b -> p (a b)").bitcast(F32), SUB
                                    ).then_inc(f_act, 1)

                conv(0, 0)
                conv(1, 1)
                product(0, 0)
                with st.repeat(2, 16) as i:
                    for q in range(8):
                        conv(2 + q, q % 2, i * 8, i * 4)
                        product(1 + q, (1 + q) % 2, i * 8)
                        if between:
                            between(q, i)
                for j in range(18, KF):
                    conv(j, j % 2)
                    product(j - 1, (j - 1) % 2)
                    if between:
                        between(j - 2, None)
                product(21, 1)

            def ada_between(q, i):
                if i is None:
                    ada_group_step(48 + q, part(ACC2, 2), q - 16)
                else:
                    ada_group_step(48 + q, ACC2[:, bass.ds(i * ADA_COLS, ADA_COLS)], q, i)

            ffn("up1", "fconv_w", 0, ada_between)
            for q in range(20, 24):
                ada_group_step(48 + q, part(ACC2, 2), q - 16)
            for m in range(8):
                add_squares(m, 21)
            dve.wait_ge(rs_ready, 8)
            dve.wait_ge(f_act, KF)
            add_normed(FO, lead[:, 24:32], RS[:, 0, :], 8)

            ps, free = scratch_wait("mod_2a")
            V.tensor_tensor(mod[:, 0:24], ps[:, 0:24], pv("b_ada_2", 0, 24), ADD).then_inc(free, 1)
            dve.wait_ge(free, SCRATCH["mod_2a"] // 2 + 1)
            st.link(V.scalar_tensor_tensor(lead[:, 0:8], mod[:, 8:16], 1.0, pv("attn_norm_2"), ADD, MUL))
            dve.wait_ge(x_ready, 16)
            dve.wait_ge(rs_ready, 9)
            make_h(mod[:, 0:8], lead[:, 0:8], RS[:, 1, :], 16)
            u0 = PLAN.at["tok2"][1]
            for c in range(6):
                for t in range(2):
                    u = u0 + 2 * c + t
                    dve.wait_ge(tok_sq, 4 * c + 2 * t + 2)
                    gain = pv("q_gain" if c < 4 else "ks_gain" if c == 4 else "kw_gain")
                    dst = QTOK[:, t, c * 256:(c + 1) * 256] if c < 4 else KTOK[:, t, (c - 4) * 256:(c - 3) * 256]
                    V.tensor_tensor(dst.rearrange("p (h d) -> p h d", d=HD),
                                    psL[:, u % 4, 0:256].rearrange("p (h d) -> p h d", d=HD),
                                    gain.unsqueeze(1).to_broadcast([P, 2, HD]), MUL).then_inc(lin_free[u % 4], 1)
                    dve.wait_ge(lin_free[u % 4], u // 4 + 1)
                    n = 2 * c + t
                    for q in range(2 * n // 3, 2 * (n + 1) // 3):
                        ada_group_step(72 + q, part(ACC2, q // 8), q % 8)
            for q in range(8, 24):
                ada_group_step(72 + q, part(ACC2, q // 8), q % 8)
            dve.wait_ge(tok_ready, 1)
            dve.wait_ge(trs, 1)
            for t in range(2):
                st.mark(V.tensor_scalar(sm[:, t * 12:t * 12 + 8], sm[:, t * 12:t * 12 + 8], float(HD) ** -0.5, None, MUL))
            dve.wait_ge(dve_step, st.n)

            def rope(buf, heads, width, cos, sin):
                half = width // 2
                tmp = SQ[:, 0:heads * width].rearrange("p (h d) -> p h d", d=width)
                st.mark(V.tensor_tensor(tmp[:, :, 0:half], buf[:, :, half:width],
                                        sin[:, 0:half].unsqueeze(1).to_broadcast([P, heads, half]), MUL))
                st.link(V.tensor_tensor(tmp[:, :, half:width], buf[:, :, 0:half],
                                        sin[:, half:width].unsqueeze(1).to_broadcast([P, heads, half]), MUL))
                st.link(V.tensor_tensor(buf, buf, cos.unsqueeze(1).to_broadcast([P, heads, width]), MUL))
                return V.tensor_tensor(buf, buf, tmp, ADD)

            def heads_of(ap, d):
                return ap.rearrange("p (h d) -> p h d", d=d)

            dve.wait_ge(s_done, SCRATCH["stat_ckv"] + 1)
            dve.wait_ge(feat_ready, 1)
            dve.wait_ge(rs_ready, 11)
            for j in range(3):
                V.scalar_tensor_tensor(CQ[:, j, :], CQ[:, j, :], pv("cq_g", j, 1), RS[:, 0, :], MUL, MUL).then_inc(cqn_ready, 1)
            for j in range(2):
                V.scalar_tensor_tensor(CKV[:, j, :], CKV[:, j, :], pv("ckv_g", j, 1), RS[:, 1, :], MUL, MUL).then_inc(cqn_ready, 1)

            for t in range(2):
                if t == 1:
                    ps, free = scratch_wait("mod_2b")
                    V.tensor_tensor(mod[:, 24:48], ps[:, 0:24], pv("b_ada_2", 24, 24), ADD).then_inc(free, 1)
                    dve.wait_ge(free, SCRATCH["mod_2b"] // 2 + 1)
                    st.link(V.scalar_tensor_tensor(lead[:, 8:16], mod[:, 32:40], 1.0, pv("ffn_norm_2"), ADD, MUL))
                cos, sin = pv("cos", t * HD, HD), pv("sin", t * HD, HD)
                q3 = heads_of(QTOK[:, t, :], HD)
                st.link(V.tensor_tensor(q3, q3, sm[:, t * 12:t * 12 + 8].unsqueeze(2).to_broadcast([P, 8, HD]), MUL))
                rope(q3, 8, HD, cos, sin).then_inc(troped, 1)
                dve.wait_ge(troped, 2 * t + 1)
                k3 = heads_of(KTOK[:, t, :], HD)
                st.link(V.tensor_tensor(k3[:, 0:4, :], k3[:, 0:4, :],
                                        sm[:, t * 12 + 8:t * 12 + 12].unsqueeze(2).to_broadcast([P, 4, HD]), MUL))
                rope(k3, 6, HD, cos, sin).then_inc(troped, 1)
                dve.wait_ge(troped, 2 * t + 2)

            dve.wait_ge(mla_tok, 1)
            dve.wait_ge(ng_ready, 1)
            for t in range(2):
                V.tensor_scalar(mlars[:, 16 * t + 8:16 * t + 16], mlars[:, 16 * t + 8:16 * t + 16],
                                sm[:, 24 + t:25 + t], None, ADD).then_inc(kr_added, 1)
            dve.wait_ge(kr_added, 2)
            dve.sem_inc(tsum, 1)

            for kv in range(2):
                if kv == 0:
                    dve.wait_ge(turned, 7)
                for g in range(2):
                    src = KT[:, 4 + g, :] if kv == 0 else VC[:, g, :]
                    pe_cols = "k_pe" if kv == 0 else "v_pe"
                    for part in range(2):
                        dst = CB[kv][:, 16 * part:16 * part + 16, g * NCMP:(g + 1) * NCMP]
                        win = src[:, 16 * part:16 * part + 240].rearrange("p (n l) -> p l n", l=16)
                        ins = V.tensor_tensor(dst, win, pv(pe_cols, 16 * part, 16).unsqueeze(2).to_broadcast([P, 16, NCMP]), ADD)
                        st.mark(ins)
                dve.wait_ge(dve_step, st.n)
                dve.sem_inc(cb_ready, 1)

            ps, free = scratch_wait("kc")
            dve.wait_ge(kc_rs, 1)
            V.scalar_tensor_tensor(KCN, ps[0:30, 0:P], sm[0:30, 60:61], pv("kc_gain")[0:30, :], MUL, MUL).then_inc(free, 1)
            dve.wait_ge(free, SCRATCH["kc"] // 2 + 1)
            dve.sem_inc(kcn_ready, 1)
            u = PLAN.at["cmp_scores"][1]
            dve.wait_ge(lin_done, u + 1)
            cs4 = CS.rearrange("p (h t n) -> p h t n", t=2, n=NCMP)
            cs3 = CS.rearrange("p (m n) -> p m n", n=NCMP)
            V.tensor_tensor(cs4, psL[:, u % 4, 0:240].rearrange("p (h t n) -> p h t n", t=2, n=NCMP),
                            pv("cmask_add").rearrange("p (t n) -> p t n", n=NCMP).unsqueeze(1).to_broadcast([P, 8, 2, NCMP]),
                            ADD).then_inc(lin_free[u % 4], 1)
            dve.wait_ge(lin_free[u % 4], u // 4 + 1)
            st.link(V.tensor_reduce(cmx[:, 0:16], cs3, AX.X, ALU.max))
            st.link(V.tensor_tensor(cs3, cs3, cmx[:, 0:16].unsqueeze(2).to_broadcast([P, 16, NCMP]), SUB))
            dve.sem_inc(cs_ready, 1)
            dve.wait_ge(ce_ready, 1)
            st.link(V.tensor_reduce(cmx[:, 0:16], cs3, AX.X, ADD))
            st.link(V.reciprocal(cmx[:, 16:32], cmx[:, 0:16]))
            gate0 = GT[:, :, :].rearrange("p t (h b) -> p h t b", b=3)[:, :, :, 0]
            st.link(V.tensor_tensor(cmx[:, 0:16].rearrange("p (h t) -> p h t", t=2),
                                    cmx[:, 16:32].rearrange("p (h t) -> p h t", t=2), gate0, MUL))
            st.link(V.tensor_tensor(cs3, cs3, cmx[:, 0:16].unsqueeze(2).to_broadcast([P, 16, NCMP]), MUL))
            st.link(V.tensor_tensor(cs4, cs4,
                                    pv("cmask01").rearrange("p (t n) -> p t n", n=NCMP).unsqueeze(1).to_broadcast([P, 8, 2, NCMP]),
                                    MUL))
            dve.sem_inc(cp_ready, 1)

            def softmax(count, p0, gated, outs):
                for i in range(count + 1):
                    if i < count:
                        n = p0 + i
                        u = PLAN.at["nsa_scores"][1] + n
                        dve.wait_ge(lin_done, u + 1)
                        b = 26 + 4 * (n % 2)
                        st.mark(V.tensor_reduce(sm[:, b:b + 1], psL[:, u % 4, 0:P], AX.X, ALU.max, negate=True))
                        st.link(V.tensor_reduce(sm[:, b + 1:b + 2], psL[:, u % 4, P:384], AX.X, ALU.max, negate=True))
                        dve.sem_inc(max_ready, 1)
                    if i >= 1:
                        n = p0 + i - 1
                        b = 28 + 4 * (n % 2)
                        rc = cmx[:, 32 + 2 * (n % 2):34 + 2 * (n % 2)]
                        dve.wait_ge(exp_ready, n + 1)
                        st.link(V.reciprocal(rc, sm[:, b:b + 2]))
                        if gated:
                            h, br = divmod(n, 2)
                            st.link(V.tensor_tensor(rc, rc, GT[:, :, 3 * h + 1 + br], MUL))
                        st.mark(V.tensor_scalar(PR[:, n % 3, 0:P], PR[:, n % 3, 0:P], rc[:, 0:1], None, MUL))
                        st.link(V.tensor_scalar(PR[:, n % 3, P:384], PR[:, n % 3, P:384], rc[:, 1:2], None, MUL))
                        dve.sem_inc(p_ready, 1)
                    outs(i)

            def nsa_outs(i):
                for h in ([(i - 4) // 2] if i >= 4 and i % 2 == 0 and i < 16 else [6, 7] if i == 16 else []):
                    n = OUT_NSA + h
                    dve.wait_ge(pt_used, 2 * h + 2)
                    V.tensor_tensor(OM[:, h, :], G2[:, h, :], psO[:, n % 2, 0:T], MUL).then_inc(o_free[n % 2], 1)

            def mla_outs(i):
                hs = [i - 3] if i < 8 else [5, 6, 7]
                for h in hs:
                    if h < 0:
                        continue
                    n = OUT_MLA + h
                    dve.wait_ge(pt_used, 16 + h + 1)
                    V.tensor_tensor(CT[:, h % 2, :], G2[:, 8 + h, :], psO[:, n % 2, 0:T], MUL).then_inc(o_free[n % 2], 1)
                    dve.wait_ge(o_free[n % 2], n // 2 + 1)
                    V.tensor_tensor(OM[:, h, :], OM[:, h, :], CT[:, h % 2, :], ADD).then_inc(om_ready, 1)

            dve.wait_ge(gates_ready, 2)
            softmax(16, 0, True, nsa_outs)
            for n in (OUT_NSA + 6, OUT_NSA + 7):
                dve.wait_ge(o_free[n % 2], n // 2 + 1)
            dve.sem_inc(om_ready, 8)
            softmax(8, 16, False, mla_outs)
            for h in range(NH):
                dve.wait_ge(omh_ready, h + 1)
                V.tensor_tensor(OML[:, h, :], OM[:, h, :], OMH[:, h, :].bitcast(F32), SUB).then_inc(oml_ready, 1)

            def add_gated(name, gates, sq_base=None):
                u0 = PLAN.at[name][1]
                for m in range(8):
                    u = u0 + m
                    V.scalar_tensor_tensor(X[:, m, :], lin(u), gates[:, m:m + 1], X[:, m, :], MUL, ADD
                                           ).then_inc(lin_free[u % 4], 1)
                    dve.wait_ge(lin_free[u % 4], u // 4 + 1)
                    dve.sem_inc(x_ready, 1)
                    if sq_base is not None and m >= 1:
                        add_squares(m - 1, sq_base)
                if sq_base is not None:
                    add_squares(7, sq_base)

            add_gated("o2", mod[:, 16:24], 38)
            dve.wait_ge(rs_ready, 12)
            make_h(mod[:, 24:32], lead[:, 8:16], RS[:, 0, :], 24)
            ffn("up2", "fconv_w_2", KF, None)
            add_gated("down2", mod[:, 40:48])


def _pack(w):
    k, n = w.shape
    return w.reshape(k // P, P, n).transpose(1, 0, 2).reshape(P, -1)


def _cols(v):
    return v.reshape(-1, P).T


def _swap(a):
    return np.concatenate([a[..., FF:], a[..., :FF]], axis=-1)


def _weights(i):
    chunks = []

    def m_blocks(w):
        for m in range(w.shape[1] // P):
            for k in range(0, w.shape[0], SLOT):
                chunks.append(_pack(w[k:k + SLOT, m * P:(m + 1) * P]))

    def pairs(w):
        return np.stack([w[:, :FF].reshape(D, KF, P), w[:, FF:].reshape(D, KF, P)], axis=2).reshape(D, 2 * FF)

    w = i["w_in"][0]
    m_blocks(np.concatenate([w[:, 2048:5120], w[:, 0:2048], w[:, 6176:7200], w[:, 7200:8224], w[:, 5152:6176],
                             w[:, 8224:10272]], axis=1))
    m_blocks(i["w_sc_out"][0])
    m_blocks(i["w_ssd_out"][0])
    m_blocks(i["w_o"][0])
    m_blocks(pairs(i["w_up"][0]))
    m_blocks(i["w_down"][0])
    w = i["w_in_2"][0]
    q, kc, vc, ks, vs, kw, vw = (w[:, 0:1024],) + tuple(w[:, 1024 + 256 * n:1280 + 256 * n] for n in range(6))
    ng, cq, ckv, kr, bg = w[:, 2560:2584], w[:, 2584:2968], w[:, 2968:3224], w[:, 3224:3288], w[:, 3288:5336]
    tok = np.concatenate([q, ks, kw, kc, vs, vw], axis=1)
    for c in range(9):
        for half in range(2):
            chunks.append(_pack(tok[half * 512:(half + 1) * 512, c * 256:(c + 1) * 256]))
    chunks.append(_pack(np.concatenate([kr, ng], axis=1)))
    m_blocks(np.concatenate([vc, cq, ckv, bg], axis=1))
    for h in range(NH):
        chunks.append(_pack(i["w_uq_2"][0][:, h * QK:(h + 1) * QK]))
    for c in range(4):
        chunks.append(_pack(i["w_ukv_2"][0][:, c * 512:(c + 1) * 512]))
    m_blocks(i["w_o_2"][0])
    m_blocks(pairs(_swap(i["w_up_2"][0])))
    m_blocks(i["w_down_2"][0])
    assert len(chunks) == CHUNKS and all(c.shape[1] == n for c, n in zip(chunks, PLAN.cols))
    for name in ("cmp_k_w1_2", "cmp_v_w1_2"):
        chunks += [_pack(i[name][0][k:k + 512]) for k in range(0, 32 * P, 512)]
    out = np.zeros((len(chunks), P, SLOT), np.float32)
    for c, a in enumerate(chunks):
        out[c, :, :a.shape[1]] = a
    return out.reshape(-1, SLOT)


def _ada(i):
    a, b = (w.reshape(KD, P, ADA_GROUPS, ADA_COLS).transpose(0, 2, 1, 3) for w in (i["ada_w"][0], i["w_ada_2"][0]))
    return np.concatenate([a[:, [1, 0]].transpose(1, 0, 2, 3).reshape(-1, ADA_COLS), a[:, 2:].reshape(-1, ADA_COLS),
                           b.transpose(1, 0, 2, 3).reshape(-1, ADA_COLS)])


def _rope(width):
    half = width // 2
    inv = (10000.0 ** (-np.arange(half, dtype=np.float32) * np.float32(2.0) / width)).astype(np.float32)
    ang = (np.arange(T, dtype=np.float32)[:, None] * inv[None, :]).astype(np.float32)
    cos, sin = np.cos(ang), np.sin(ang)
    tile = lambda a: a.reshape(2, P, width).transpose(1, 0, 2).reshape(P, -1).astype(np.float32)
    return tile(np.concatenate([cos, cos], axis=1)), tile(np.concatenate([-sin, sin], axis=1))


def _params(i):
    def rows(v):
        out = np.zeros((P, 1), np.float32)
        out[:len(v), 0] = v
        return out

    def taps(w):
        return np.concatenate([_cols(row) for row in w], axis=1)

    def wide(v):
        return np.broadcast_to(v, (P, len(v)))

    q, k = np.arange(P)[:, None], np.arange(P)[None, :]
    ends = 16 * np.arange(NCMP) + 31
    seen = (ends[None, None, :] <= (np.arange(2)[None, :, None] * P + np.arange(P)[:, None, None])).reshape(P, -1)
    cos, sin = _rope(HD)
    mcos, msin = _rope(ROPE)
    f = lambda a: a.astype(np.float32)
    v = {
        "c": _cols(i["c"][0]), "c_2": _cols(i["c_2"][0]), "ada_b": _cols(i["ada_b"][0]),
        "mix_pre_g": _cols(i["mix_pre_g"][0]), "mix_post_g": _cols(i["mix_post_g"][0]),
        "xconv_w": taps(i["ssd_conv_w"][0]), "xconv_b": _cols(i["ssd_conv_b"][0]),
        "dskip": _cols(np.repeat(i["ssd_d"][0], 64)), "ssd_norm_g": _cols(i["ssd_norm_g"][0]),
        "sconv_w": taps(i["sc_conv_w"][0]), "ffn_pre_g": _cols(i["ffn_pre_g"][0]), "ffn_post_g": _cols(i["ffn_post_g"][0]),
        "fconv_w": taps(i["ffn_conv_w"][0]), "fconv_b": _cols(i["ffn_conv_b"][0]),
        "dt_bias": rows(i["ssd_dt_bias"][0]), "a_log": rows(i["ssd_a_log"][0]), "w_dt": _pack(i["w_in"][0][:, 5120:5152]),
        "b_ada_2": _cols(i["b_ada_2"][0]), "attn_norm_2": _cols(i["attn_norm_2"][0]), "ffn_norm_2": _cols(i["ffn_norm_2"][0]),
        "fconv_w_2": taps(_swap(i["w_conv_2"][0])), "fconv_b_2": _cols(_swap(i["b_conv_2"][0])),
        "k_pe": i["cmp_k_pe_2"][0].T, "v_pe": i["cmp_v_pe_2"][0].T,
        "k_w2": _pack(i["cmp_k_w2_2"][0]), "v_w2": _pack(i["cmp_v_w2_2"][0]),
        "cq_g": _cols(i["mla_cq_norm_2"][0]), "ckv_g": _cols(i["mla_ckv_norm_2"][0]),
        "q_gain": wide(i["nsa_q_norm_2"][0]), "ks_gain": wide(i["nsa_ks_norm_2"][0]), "kw_gain": wide(i["nsa_kw_norm_2"][0]),
        "kc_gain": wide(i["nsa_kc_norm_2"][0]), "mq_gain": wide(i["mla_q_norm_2"][0]), "mk_gain": wide(i["mla_k_norm_2"][0]),
        "ident": np.eye(P, dtype=np.float32), "ones": np.ones((P, P), np.float32),
        "causal_add": f(np.where(k <= q, 0.0, -1e30)), "causal01": f(k >= q),
        "cos": cos, "sin": sin, "mcos": mcos, "msin": msin,
        "cmask_add": f(np.where(seen, 0.0, -1e30)), "cmask01": f(seen),
    }
    assert all(v[n].shape == (P, c) for n, c in PAR_SPEC), [(n, v[n].shape) for n, c in PAR_SPEC if v[n].shape != (P, c)]
    return np.ascontiguousarray(np.concatenate([v[n] for n, _ in PAR_SPEC], axis=1))


def kernel(**inputs):
    import concourse.bacc as bacc
    from concourse.bass_utils import run_bass_kernel_spmd

    inputs = {k: np.asarray(v) for k, v in inputs.items()}
    arrays = {
        "x_t": np.ascontiguousarray(inputs["x"][0].reshape(T, KD, P).transpose(2, 1, 0)),
        "params": _params(inputs), "ada_w": np.ascontiguousarray(_ada(inputs)), "wts": _weights(inputs),
    }
    nc = bacc.Bacc("TRN2", target_bir_lowering=False, num_devices=1)
    aps = [nc.dram_tensor(n, a.shape, mybir.dt.from_np(a.dtype), kind="ExternalInput").ap() for n, a in arrays.items()]
    out = nc.dram_tensor("out_t", (P, KD * T), mybir.dt.float32, kind="ExternalOutput").ap()
    build(nc, *aps, out)
    r = run_bass_kernel_spmd(nc, [arrays], core_ids=[0])
    y = r.results[0]["out_t"].reshape(P, KD, T).transpose(2, 1, 0).reshape(1, T, D)
    return np.ascontiguousarray(y)
```
